# Optimizing a Trainium2 kernel written in Bass

```python
import math
import jax, jax.numpy as jnp
from jax import lax
import numpy as np

D_MODEL = 2048
BATCH = 1
SEQ = 256
DEPTH = 2

N_MIXERS = 2
SSD_EXPAND = 2
D_INNER = SSD_EXPAND * D_MODEL
HEAD_DIM = 64
N_HEADS = D_INNER // HEAD_DIM
N_GROUPS = 8
HEADS_PER_GROUP = N_HEADS // N_GROUPS
D_STATE = 128
CONV_WIDTH = 5
CHUNK = 128
D_BC = N_GROUPS * D_STATE
D_XBC = D_INNER + 2 * D_BC
D_IN_PROJ = D_INNER + D_XBC + 2 * N_HEADS
DT_MIN = 1e-3
DT_MAX = 1e-1
A_INIT_MIN = 1.0
A_INIT_MAX = 16.0
POOL_WINDOWS = (2, 4, 8, 16)
N_POOL_GROUPS = len(POOL_WINDOWS)
POOL_GROUP_DIM = D_MODEL // N_POOL_GROUPS
D_FF = 4 * D_MODEL
DEEPNORM_ALPHA = (2.0 * DEPTH) ** 0.25
DEEPNORM_BETA = (8.0 * DEPTH) ** -0.25
LN_EPS = 1e-5
RMS_EPS = 1e-5
N_SSD_LAYERS = (DEPTH + 1) // 2
N_POOL_LAYERS = DEPTH // 2

kernel_name = "bidir_ssd_pool_hybrid_deepnorm"

def layer_norm(x, g, b):
    xf = x.astype(jnp.float32)
    mu = jnp.mean(xf, axis=-1, keepdims=True)
    var = jnp.mean(jnp.square(xf - mu), axis=-1, keepdims=True)
    y = (xf - mu) * lax.rsqrt(var + LN_EPS) * g.astype(jnp.float32) + b.astype(jnp.float32)
    return y.astype(x.dtype)

def centred_depthwise_conv(x, w, bias):
    c = x.shape[-1]
    pad = CONV_WIDTH // 2
    y = lax.conv_general_dilated(
        x, w, window_strides=(1,), padding=[(pad, pad)],
        dimension_numbers=("NWC", "WIO", "NWC"), feature_group_count=c)
    return y + bias

def ssd_chunked(x, dt, A, Bm, Cm):
    b, T, g, r, p = x.shape
    n = Bm.shape[-1]
    c = T // CHUNK
    f32 = jnp.float32
    xdt = (x.astype(f32) * dt[..., None]).reshape(b, c, CHUNK, g, r, p)
    a_cs = jnp.cumsum((dt * A).reshape(b, c, CHUNK, g, r), axis=2)
    Bc = Bm.astype(f32).reshape(b, c, CHUNK, g, n)
    Cc = Cm.astype(f32).reshape(b, c, CHUNK, g, n)
    mask = jnp.tril(jnp.ones((CHUNK, CHUNK), dtype=bool))[None, None, :, :, None, None]
    seg = a_cs[:, :, :, None] - a_cs[:, :, None, :]
    decay = jnp.exp(jnp.where(mask, seg, -jnp.inf))
    scores = jnp.einsum("bclgn,bcsgn->bclsg", Cc, Bc)
    y_diag = jnp.einsum("bclsg,bclsgr,bcsgrp->bclgrp", scores, decay, xdt)
    decay_to_end = jnp.exp(a_cs[:, :, -1:] - a_cs)
    states = jnp.einsum("bclgn,bclgr,bclgrp->bcgrpn", Bc, decay_to_end, xdt)
    chunk_decay = jnp.exp(a_cs[:, :, -1])

    def step(h, inp):
        s_c, d_c = inp
        return h * d_c[..., None, None] + s_c, h

    h0 = jnp.zeros((b, g, r, p, n), f32)
    _, prev = lax.scan(step, h0, (jnp.moveaxis(states, 1, 0), jnp.moveaxis(chunk_decay, 1, 0)))
    prev = jnp.moveaxis(prev, 0, 1)
    y_off = jnp.einsum("bclgn,bcgrpn,bclgr->bclgrp", Cc, prev, jnp.exp(a_cs))
    return (y_diag + y_off).reshape(b, T, g, r, p)

def ssd_mixer(u, in_proj, conv_w, conv_b, dt_bias, a_log, d_skip, norm_w, out_proj):
    b, T, _ = u.shape
    f32 = jnp.float32
    zxbcdt = u @ in_proj
    z = zxbcdt[..., :D_INNER]
    xbc = zxbcdt[..., D_INNER:D_INNER + D_XBC]
    dt_raw = zxbcdt[..., D_INNER + D_XBC:]
    xbc = jax.nn.silu(centred_depthwise_conv(xbc, conv_w, conv_b))
    xs = xbc[..., :D_INNER].reshape(b, T, N_GROUPS, HEADS_PER_GROUP, HEAD_DIM)
    Bm = xbc[..., D_INNER:D_INNER + D_BC].reshape(b, T, N_GROUPS, D_STATE)
    Cm = xbc[..., D_INNER + D_BC:].reshape(b, T, N_GROUPS, D_STATE)
    dt = jax.nn.softplus(dt_raw.astype(f32).reshape(b, T, 2, N_GROUPS, HEADS_PER_GROUP)
                         + dt_bias.astype(f32).reshape(2, N_GROUPS, HEADS_PER_GROUP))
    A = -jnp.exp(a_log.astype(f32)).reshape(2, N_GROUPS, HEADS_PER_GROUP)
    flip = lambda t: jnp.flip(t, axis=1)
    y_fwd = ssd_chunked(xs, dt[:, :, 0], A[0], Bm, Cm)
    y_bwd = flip(ssd_chunked(flip(xs), flip(dt[:, :, 1]), A[1], flip(Bm), flip(Cm)))
    y = y_fwd + y_bwd + xs.astype(f32) * d_skip.astype(f32).reshape(N_GROUPS, HEADS_PER_GROUP)[..., None]
    gy = (y.reshape(b, T, D_INNER) * jax.nn.silu(z.astype(f32))).reshape(b, T, N_GROUPS, D_INNER // N_GROUPS)
    gy = gy * lax.rsqrt(jnp.mean(jnp.square(gy), axis=-1, keepdims=True) + RMS_EPS)
    gy = gy.reshape(b, T, D_INNER) * norm_w.astype(f32)
    return gy.astype(u.dtype) @ out_proj

def pool_mixer(u, w, bias, scale):
    b, T, _ = u.shape
    uf = u.astype(jnp.float32)
    cs = jnp.concatenate([jnp.zeros((b, 1, D_MODEL), jnp.float32), jnp.cumsum(uf, axis=1)], axis=1)
    t = jnp.arange(T)
    groups = []
    for gi, win in enumerate(POOL_WINDOWS):
        lo_c, hi_c = gi * POOL_GROUP_DIM, (gi + 1) * POOL_GROUP_DIM
        start = t - win // 2
        lo = jnp.clip(start, 0, T)
        hi = jnp.clip(start + win, 0, T)
        csg = cs[..., lo_c:hi_c]
        wsum = jnp.take(csg, hi, axis=1) - jnp.take(csg, lo, axis=1)
        cnt = (hi - lo).astype(jnp.float32)[None, :, None]
        groups.append(wsum / cnt - uf[..., lo_c:hi_c])
    m = jnp.stack(groups, axis=2).astype(u.dtype)
    y = jnp.einsum("btgc,gcd->btgd", m, w) + bias
    return y.reshape(b, T, D_MODEL) * scale

def sq_relu_mlp(u, w1, w2):
    return jnp.square(jax.nn.relu(u @ w1)) @ w2

def setup_inputs(seed: int = 0) -> dict:
    key = jax.random.key(seed)
    ks = jax.random.split(key, 20)
    f32 = jnp.float32
    nrm = lambda k, shape: jax.random.normal(k, shape, f32)
    x = nrm(ks[0], (BATCH, SEQ, D_MODEL))
    ssd_in_proj = nrm(ks[1], (N_SSD_LAYERS, D_MODEL, D_IN_PROJ)) * D_MODEL ** -0.5
    ssd_conv_w = nrm(ks[2], (N_SSD_LAYERS, CONV_WIDTH, 1, D_XBC)) * CONV_WIDTH ** -0.5
    ssd_conv_b = 0.01 * nrm(ks[3], (N_SSD_LAYERS, D_XBC))
    u_dt = jax.random.uniform(ks[4], (N_SSD_LAYERS, 2, N_HEADS), f32)
    dt0 = jnp.exp(u_dt * (math.log(DT_MAX) - math.log(DT_MIN)) + math.log(DT_MIN))
    dt0 = jnp.maximum(dt0, 1e-4)
    ssd_dt_bias = dt0 + jnp.log(-jnp.expm1(-dt0))
    ssd_A_log = jnp.log(jax.random.uniform(ks[5], (N_SSD_LAYERS, 2, N_HEADS), f32, A_INIT_MIN, A_INIT_MAX))
    ssd_D = 1.0 + 0.1 * nrm(ks[6], (N_SSD_LAYERS, N_HEADS))
    ssd_norm_w = 1.0 + 0.1 * nrm(ks[7], (N_SSD_LAYERS, D_INNER))
    ssd_out_proj = nrm(ks[8], (N_SSD_LAYERS, D_INNER, D_MODEL)) * (D_INNER ** -0.5 * DEEPNORM_BETA)
    pool_w = nrm(ks[9], (N_POOL_LAYERS, N_POOL_GROUPS, POOL_GROUP_DIM, POOL_GROUP_DIM)) * (POOL_GROUP_DIM ** -0.5 * DEEPNORM_BETA)
    pool_b = 0.01 * nrm(ks[10], (N_POOL_LAYERS, N_POOL_GROUPS, POOL_GROUP_DIM))
    pool_scale = 1.0 + 0.1 * nrm(ks[11], (N_POOL_LAYERS, D_MODEL))
    mlp_w1 = nrm(ks[12], (DEPTH, D_MODEL, D_FF)) * D_MODEL ** -0.5
    mlp_w2 = nrm(ks[13], (DEPTH, D_FF, D_MODEL)) * (D_FF ** -0.5 * DEEPNORM_BETA)
    ln_mix_g = 1.0 + 0.1 * nrm(ks[14], (DEPTH, D_MODEL))
    ln_mix_b = 0.01 * nrm(ks[15], (DEPTH, D_MODEL))
    ln_ffn_g = 1.0 + 0.1 * nrm(ks[16], (DEPTH, D_MODEL))
    ln_ffn_b = 0.01 * nrm(ks[17], (DEPTH, D_MODEL))
    return {"x": x, "ssd_in_proj": ssd_in_proj, "ssd_conv_w": ssd_conv_w, "ssd_conv_b": ssd_conv_b,
            "ssd_dt_bias": ssd_dt_bias, "ssd_A_log": ssd_A_log, "ssd_D": ssd_D, "ssd_norm_w": ssd_norm_w,
            "ssd_out_proj": ssd_out_proj, "pool_w": pool_w, "pool_b": pool_b, "pool_scale": pool_scale,
            "mlp_w1": mlp_w1, "mlp_w2": mlp_w2, "ln_mix_g": ln_mix_g, "ln_mix_b": ln_mix_b,
            "ln_ffn_g": ln_ffn_g, "ln_ffn_b": ln_ffn_b}

def reference(x, ssd_in_proj, ssd_conv_w, ssd_conv_b, ssd_dt_bias, ssd_A_log, ssd_D, ssd_norm_w,
              ssd_out_proj, pool_w, pool_b, pool_scale, mlp_w1, mlp_w2, ln_mix_g, ln_mix_b,
              ln_ffn_g, ln_ffn_b):
    for i in range(DEPTH):
        j = i // N_MIXERS
        if i % N_MIXERS == 0:
            mix = ssd_mixer(x, ssd_in_proj[j], ssd_conv_w[j], ssd_conv_b[j], ssd_dt_bias[j],
                            ssd_A_log[j], ssd_D[j], ssd_norm_w[j], ssd_out_proj[j])
        else:
            mix = pool_mixer(x, pool_w[j], pool_b[j], pool_scale[j])
        x = layer_norm(DEEPNORM_ALPHA * x + mix, ln_mix_g[i], ln_mix_b[i])
        x = layer_norm(DEEPNORM_ALPHA * x + sq_relu_mlp(x, mlp_w1[i], mlp_w2[i]), ln_ffn_g[i], ln_ffn_b[i])
    return x


_drawn_inputs = setup_inputs


def setup_inputs(seed=0):
    import zlib

    import numpy as np

    out = dict(_drawn_inputs(seed))
    spreads = {}
    factors = {'ssd_conv_b': 8.0, 'ssd_D': 2.688, 'pool_b': 8.0, 'ln_mix_b': 3.93, 'ln_ffn_b': 4.138}
    for name, (base, spread) in spreads.items():
        noise = np.random.default_rng([zlib.crc32(name.encode()), seed]).standard_normal(out[name].shape)
        drawn = base * np.exp(spread * noise) if base else spread * noise
        out[name] = __import__('jax').numpy.asarray(drawn.astype(out[name].dtype))
    for name, factor in factors.items():
        out[name] = (out[name] * factor).astype(out[name].dtype)
    return out
```

```python
from contextlib import ExitStack

import concourse.bass as bass
from concourse import mybir

F32 = mybir.dt.float32
F32R = mybir.dt.float32r
ALU = mybir.AluOpType
ACT = mybir.ActivationFunctionType

P = 128
DM = 2048
T = 256
TT = T // P
DEPTH = 2
DI = 2 * DM
HD = 64
NH = DI // HD
NG = 8
HPG = NH // NG
TAPS = 5
PAD = TAPS // 2
DFF = 4 * DM
NB = 512
KT = DM // P
CT = NB // P
XS0, B0, DT0 = DI, 2 * DI, 2 * DI + 2 * NG * P
CH_B = DI // P
CK = 8
CHUNKS = DFF // (CK * P)
WINDOWS = (2, 4, 8, 16)
ALPHA = (2.0 * DEPTH) ** 0.25
EPS = 1e-5
TINY = 1e-30
RING = 8
RAW = 4
SUBK = 2


class Pos:

    def __init__(self, base, step=0, loop=None):
        self.base, self.step, self.loop = base, step, loop

    def __add__(self, k):
        return Pos(self.base + k, self.step, self.loop)

    def times(self, k):
        return Pos(self.base * k, self.step * k, self.loop)

    def half(self):
        assert self.step % 2 == 0
        return Pos(self.base // 2, self.step // 2, self.loop)

    def slot(self, n):
        assert self.step % n == 0
        return self.base % n

    @property
    def n(self):
        return self.base if self.loop is None else self.loop * self.step + self.base


def wait(eng, sem, pos):
    if pos.loop is None and pos.base <= 0:
        return
    eng.wait_ge(sem, pos.n)


Q_DT, S_DT = 0, 0
Q_BC, S_BC = 1, 8
Q_P0, S_P0 = Q_BC + 4, S_BC + 32
Q_P1, S_P1 = Q_P0 + 2, S_P0 + 16
Q_SSD, S_SSD = Q_P1 + 2, S_P1 + 16
Q_D3, S_D3 = Q_SSD + 3 * 8, S_SSD + 3 * 48
Q_M0, S_M0 = Q_D3 + 8, S_D3 + 16
Q_POOL, S_POOL = Q_M0 + 6 * CHUNKS, S_M0 + 32 * CHUNKS
Q_M1, S_M1 = Q_POOL + 4, S_POOL + 8
S_END = S_M1 + 32 * CHUNKS


def build(nc, a, out):
    with ExitStack() as ctx:
        def sb(name, shape, dt=F32):
            return ctx.enter_context(nc.sbuf_tensor(name, shape, dt))

        def pb(name, shape):
            return ctx.enter_context(nc.psum_tensor(name, shape, F32))

        def sem(name):
            return ctx.enter_context(nc.semaphore(name))

        x = sb("x", [P, TT, DM])
        xT = [sb("xTh", [P, KT, T], F32R), sb("xTl", [P, KT, T], F32R)]
        hT = [sb("hTh", [P, CK, T], F32R), sb("hTl", [P, CK, T], F32R)]
        raw = sb("raw", [P, RAW, SUBK, NB])
        whi = sb("whi", [P, RING, SUBK, NB], F32R)
        wlo = sb("wlo", [P, RING, SUBK, NB], F32R)
        ident = sb("ident", [P, P])
        eps = sb("eps", [P, 1])

        area_a = sb("area_a", [P, 2 * NG * T])
        bcT = area_a[:].rearrange("p (m g t) -> p m g t", m=2, g=NG)
        gb = area_a[:].rearrange("p (m n) -> p m n", m=2)
        area_b = sb("area_b", [P, 4 * TT * NB])
        quarter = [area_b[:, i * TT * NB:(i + 1) * TT * NB] for i in range(4)]
        pj = quarter[0].rearrange("p (t n) -> p t n", t=TT)
        st = pj
        xs = quarter[1].rearrange("p (t n) -> p t n", t=TT)
        zs = quarter[2].rearrange("p (t n) -> p t n", t=TT)
        gy = quarter[3].rearrange("p (t n) -> p t n", t=TT)
        cv = quarter[3].rearrange("p (j n) -> p j n", j=CT)
        psc = area_b[:].rearrange("p (m n) -> p m n", m=2)
        area_c = sb("area_c", [P, 3 * 4 * P])
        e1, mf, mb = (area_c[:, i * 4 * P:(i + 1) * 4 * P].rearrange("p (h l) -> p h l", h=4) for i in range(3))
        hr = area_c[:, 0:TT * NB].rearrange("p (t n) -> p t n", t=TT)
        ptmp = area_c[:, 2 * NB:3 * NB]
        dtw = area_c[:].rearrange("p (k t) -> p k t", k=6)
        area_d = sb("area_d", [P, 2 * 2 * 4 * P])
        fbc = [area_d[:, i * 8 * P:(i + 1) * 8 * P].rearrange("p (d h l) -> p d h l", d=2, h=4) for i in range(2)]
        cvin = area_d[:, 0:CT * (T + 2 * PAD)].rearrange("p (j n) -> p j n", j=CT)
        bands = area_d[:].rearrange("p (w s t) -> p w s t", w=4, s=TT)
        xw = sb("xw", [P, 3, NB])
        cur = sb("cur", [P, 2, T])
        btok = sb("btok", [P, TT, P])
        gt = sb("gt", [P, TT, 2, P])
        cols = sb("cols", [P, 6, P])
        dtv = cols[:, 0:2, :].rearrange("p k t -> p (k t)")
        masks = sb("masks", [P, 2, P])
        convw = sb("convw", [P, (DI + 2 * NG * P) // P, TAPS])
        convb = sb("convb", [P, (DI + 2 * NG * P) // P])
        normw = sb("normw", [P, DI // P])
        dskip = sb("dskip", [P, NH])
        dtp = sb("dtp", [P, 4])
        ss = sb("ss", [P, TT, 3])
        bst = sb("bst", [P, TT, 4, 6])
        mv = sb("mv", [P, TT, 4])

        acc = [[pb(f"acc{i}{t}", [P, NB]) for t in range(TT)] for i in range(2)]
        tb = [pb(f"tb{i}", [P, NB]) for i in range(2)]
        sbk = [pb(f"sbk{i}", [P, NB]) for i in range(2)]
        fscr = nc.dram_tensor("f_scratch", (P, T), F32).ap()

        raw_in = [sem(f"raw_in{r}") for r in range(RAW)]
        hi_ready, lo_ready, w_used = sem("hi_ready"), sem("lo_ready"), sem("w_used")
        acc_full = [sem(f"acc_full{i}") for i in range(2)]
        acc_free = [[sem(f"acc_free{i}{t}") for t in range(TT)] for i in range(2)]
        x_in, const_in, eps_set = sem("x_in"), sem("const_in"), sem("eps_set")
        tr_done, tr_hi, tr_lo = sem("tr_done"), sem("tr_hi"), sem("tr_lo")
        x_scaled, squared = sem("x_scaled"), sem("squared")
        h_tr = [sem(f"h_tr{t}") for t in range(TT)]
        h_hi = [sem(f"h_hi{t}") for t in range(TT)]
        h_lo = [sem(f"h_lo{t}") for t in range(TT)]
        ln_vec, ln_root, x_norm, gb_in = sem("ln_vec"), sem("ln_root"), sem("x_norm"), sem("gb_in")
        stored = sem("stored")
        dk_tr, dtv_done, dt_vec, dt_act = (sem(n) for n in ("dk_tr", "dtv_done", "dt_vec", "dt_act"))
        f_ready, f_saved, col_tr, col_done = (sem(n) for n in ("f_ready", "f_saved", "col_tr", "col_done"))
        cv_tr, cvin_full, pad_set, tap_done, cv_silu = (
            sem(n) for n in ("cv_tr", "cvin_full", "pad_set", "tap_done", "cv_silu"))
        cur_half = sem("cur_half")
        back_tr, xs_out, cur_done, sc_done, gt_done, btok_done = (
            sem(n) for n in ("back_tr", "xs_out", "cur_done", "sc_done", "gt_done", "btok_done"))
        fbc_in = [sem(f"fbc_in{i}") for i in range(2)]
        e_sub, e_min, e_exp, m_done, yd_done = (sem(n) for n in ("e_sub", "e_min", "e_exp", "m_done", "yd_done"))
        xw_done, gy_skip, st_done, st_out, off_done = (
            sem(n) for n in ("xw_done", "gy_skip", "st_done", "st_out", "off_done"))
        gy_yd, gy_off, gated, sumsq, rooted, inv_root, gy_done = (
            sem(n) for n in ("gy_yd", "gy_off", "gated", "sumsq", "rooted", "inv_root", "gy_done"))
        gy_tr, gy_hi, gy_lo = sem("gy_tr"), sem("gy_hi"), sem("gy_lo")
        bands_in, psc_in, bias_scaled, pool_added, x_times = (
            sem(n) for n in ("bands_in", "psc_in", "bias_scaled", "pool_added", "x_times"))

        block = ctx.enter_context(nc.Block())

        in_w = a["in_proj"].rearrange("(k p) n -> p k n", p=P)
        out_w = a["out_proj"].rearrange("(k p) n -> p k n", p=P)
        w1 = [a["w1"][i].rearrange("(k p) n -> p k n", p=P) for i in range(DEPTH)]
        w2 = [a["w2"][i].rearrange("(k p) n -> p k n", p=P) for i in range(DEPTH)]
        pool_w = a["pool_w"].rearrange("g (k p) n -> g p k n", p=P)
        x_rows = a["x"].rearrange("(t p) n -> p t n", p=P)
        out_rows = out.rearrange("(t p) n -> p t n", p=P)
        f_rows = fscr.rearrange("(d h) t -> d h t", d=2)

        @block.sync
        def _(sp):
            sp.dma_start(x[:], x_rows).then_inc(x_in, 16)

            def load(s, src, width=NB):
                wait(sp, lo_ready, s + (1 - RAW))
                r = s.slot(RAW)
                sp.dma_start(raw[:, r, :, 0:width], src).then_inc(raw_in[r], 16)

            def load_in(s, col, width=NB):
                for i in range(KT // SUBK):
                    load(s + i, in_w[:, SUBK * i:SUBK * (i + 1), bass.ds(col, width)], width)

            def load_down(s, w, row, n, subs=CK // SUBK):
                for i in range(subs):
                    load(s + i, w[:, bass.ds(row + SUBK * i, SUBK), n * NB:(n + 1) * NB])

            def load_mlp(s0, layer):
                with sp.Fori(0, CHUNKS) as c:
                    s = Pos(s0, 32, c)
                    for j in range(2):
                        for i in range(KT // SUBK):
                            load(s + (8 * j + i), w1[layer][:, SUBK * i:SUBK * (i + 1), bass.ds(c * (CK * P) + j * NB, NB)])
                    for n in range(4):
                        load_down(s + (16 + 4 * n), w2[layer], c * CK, n)

            load_in(Pos(S_DT), DT0, P)
            with sp.Fori(0, 2) as j:
                for i in range(2):
                    load_in(Pos(S_BC + 8 * i, 16, j), j * (2 * NB) + (B0 + i * NB))
            for g in range(2):
                load_in(Pos(S_P0 + 16 * g), XS0 + g * NB)
                load_in(Pos(S_P0 + 16 * g + 8), g * NB)
            with sp.Fori(0, 3) as c:
                s = Pos(S_SSD, 48, c)
                load_in(s, c * (2 * NB) + (XS0 + 2 * NB))
                load_in(s + 8, c * (2 * NB) + 2 * NB)
                for n in range(4):
                    load_down(s + (16 + 4 * n), out_w, c * CK, n)
                load_in(s + 32, c * (2 * NB) + (XS0 + 3 * NB))
                load_in(s + 40, c * (2 * NB) + 3 * NB)
            for half in range(2):
                for n in range(4):
                    load_down(Pos(S_D3 + 8 * half + 2 * n), out_w, 3 * CK + 4 * half, n, 2)
            load_mlp(S_M0, 0)
            for g in range(4):
                for i in range(2):
                    load(Pos(S_POOL + 2 * g + i), pool_w[g][:, SUBK * i:SUBK * (i + 1), :])
            load_mlp(S_M1, 1)
            for t in range(TT):
                sp.wait_ge(x_norm, 3 * 8 + 4 * (t + 1))
                sp.dma_start(out_rows[:, t, :], x[:, t, :]).then_inc(stored, 16)
            sp.wait_ge(stored, 16 * TT)

        @block.tensor
        def _(pe):
            def rows(t):
                return slice(t * P, (t + 1) * P)

            def products(lhs, kts, t, q, s, first, last, width=NB):
                pair = q.slot(2)
                if first:
                    wait(pe, acc_free[pair][t], q.half())
                dst = acc[pair][t][:, 0:width]
                for i, kt in enumerate(kts):
                    slot = (s + i // SUBK).slot(RING)
                    if t == 0 and i % SUBK == 0:
                        wait(pe, lo_ready, s + (i // SUBK + 1))
                    hi, lo = whi[:, slot, i % SUBK, 0:width], wlo[:, slot, i % SUBK, 0:width]
                    end = last and i == len(kts) - 1
                    pe.matmul(dst, lhs[0][:, kt, rows(t)], hi, start=first and i == 0, stop=False)
                    pe.matmul(dst, lhs[1][:, kt, rows(t)], hi, start=False, stop=False)
                    mm = pe.matmul(dst, lhs[0][:, kt, rows(t)], lo, start=False, stop=end)
                    if t == 1 and i % SUBK == SUBK - 1:
                        mm.then_inc(w_used, 1)
                    elif end:
                        mm.then_inc(acc_full[pair], 1)

            def none(k):
                pass

            def wide(q, s, after=none, width=NB):
                for b in range(2):
                    for t in range(TT):
                        products(xT, range(8 * b, 8 * b + 8), t, q, s + 4 * b, b == 0, b == 1, width)
                        after(2 * b + t)

            def down(q, s, after=none, kts=range(CK), n=0):
                for t in range(TT):
                    products(hT, kts, t, q, s, True, True)
                    after(2 * n + t)

            def turn_x(first_quarter, ready):
                for t in range(TT):
                    for i in range(4):
                        u = first_quarter + 4 * t + i
                        if ready is not None:
                            pe.wait_ge(ready, u - 7)
                        wait(pe, tr_lo, Pos(u - 1))
                        for k in range(CT):
                            mm = pe.transpose(tb[u % 2][:, k * P:(k + 1) * P],
                                              x[:, t, (CT * i + k) * P:(CT * i + k + 1) * P], ident[:])
                        mm.then_inc(tr_done, 1)

            def turn_h(u, t):
                pe.wait_ge(squared, (u.times(2) + (t + 1)).n)
                for k in range(CT):
                    mm = pe.transpose(tb[t][:, k * P:(k + 1) * P], hr[:, t, k * P:(k + 1) * P], ident[:])
                mm.then_inc(h_tr[t], 1)

            def turn_pj(q):
                for t in range(TT):
                    pe.wait_ge(acc_free[q.slot(2)][t], (q.half() + 1).n)
                for t in range(TT):
                    for j in range(CT):
                        mm = pe.transpose(tb[t][:, j * P:(j + 1) * P], pj[:, t, j * P:(j + 1) * P], ident[:])
                mm.then_inc(cv_tr, 1)

            def score(g):
                pe.wait_ge(cur_done, (g + 1).n)
                wait(pe, gy_lo, g.times(4))
                for t in range(TT):
                    pe.matmul(sbk[0][:, rows(t)], cur[:, 0, rows(t)], cur[:, 1, rows(t)], start=True, stop=True)
                for t in range(TT):
                    mm = pe.transpose(sbk[1][:, rows(t)], cur[:, 0, rows(t)], ident[:])
                mm.then_inc(sc_done, 1)

            def turn_back(g):
                pe.wait_ge(cv_silu, (g + (4 + 1)).n)
                pe.wait_ge(cvin_full, (g.times(2) + 2 * (4 + 1)).n)
                for t in range(TT):
                    for j in range(CT):
                        mm = pe.transpose(tb[t][:, j * P:(j + 1) * P], cv[:, j, rows(t)], ident[:])
                mm.then_inc(back_tr, 1)

            def diag(g, u):
                t, hh = u // 2, u % 2
                pe.wait_ge(m_done, (g.times(8) + 2 * (u + 1)).n)
                pe.wait_ge(xw_done, (g.times(6) + 3 * (t + 1)).n)
                if u == 0:
                    pe.wait_ge(gt_done, (g.times(4) + 4).n)
                if u == 2:
                    pe.wait_ge(gy_yd, (g.times(2) + 1).n)
                for h in range(4):
                    head = 4 * hh + h
                    dst = sbk[0][:, head * HD:(head + 1) * HD]
                    cs = slice(head * HD, (head + 1) * HD)
                    pe.matmul(dst, mf[:, h, :], xw[:, 0, cs], start=True, stop=False)
                    mm = pe.matmul(dst, mb[:, h, :], xw[:, 1, cs], start=False, stop=True)
                mm.then_inc(yd_done, 1)

            def state(g, t):
                if t == 0:
                    pe.wait_ge(btok_done, (g + 1).n)
                else:
                    pe.wait_ge(gy_off, (g.times(16) + 8).n)
                    pe.wait_ge(xw_done, (g.times(6) + 6).n)
                pe.matmul(sbk[1][:], btok[:, t, :], xw[:, 2, :], start=True, stop=True).then_inc(st_done, 1)

            def carried(g, t):
                pe.wait_ge(st_out, (g.times(2) + (t + 1)).n)
                pe.matmul(sbk[1][:], cur[:, 1, rows(1 - t)], st[:, t, :], start=True, stop=True).then_inc(off_done, 1)

            def turn_gy(g):
                pe.wait_ge(gy_done, (g.times(2) + 2).n)
                pe.wait_ge(gy_off, (g.times(16) + 16).n)
                for b in range(2):
                    for k in range(2):
                        for t in range(TT):
                            ch = 2 * b + k
                            mm = pe.transpose(sbk[b][:, (2 * k + t) * P:(2 * k + t + 1) * P],
                                              gy[:, t, ch * P:(ch + 1) * P], ident[:])
                mm.then_inc(gy_tr, 1)

            def chain(g, k, q=None):
                if k == 0:
                    turn_pj(q)
                elif k == 1:
                    score(g)
                elif k == 2:
                    turn_back(g)
                elif k == 3:
                    diag(g, 0)
                    state(g, 0)
                elif k == 4:
                    diag(g, 1)
                    carried(g, 0)
                elif k == 5:
                    diag(g, 2)
                    state(g, 1)
                elif k == 6:
                    diag(g, 3)
                    carried(g, 1)

            def with_z(g, before, q):
                def after(k):
                    if k == 0 and before is not None:
                        turn_gy(before)
                    chain(g, k, q)
                return after

            pe.wait_ge(const_in, 16 * 8)
            pe.wait_ge(x_in, 16)
            turn_x(0, None)
            pe.wait_ge(tr_lo, 8)
            wide(Pos(Q_DT), Pos(S_DT), width=P)
            for t in range(TT):
                pe.wait_ge(acc_free[Q_DT % 2][t], 1)
                mm = pe.transpose(tb[0][:, rows(t)], pj[:, t, 0:P], ident[:])
            mm.then_inc(dk_tr, 1)
            pe.wait_ge(dtv_done, 1)
            with pe.Fori(0, 2) as j:
                for i in range(2):
                    wide(Pos(Q_BC + i, 2, j), Pos(S_BC + 8 * i, 16, j))
                    turn_pj(Pos(Q_BC + i, 2, j))
            def turn_cols(k):
                if k == 2:
                    pe.wait_ge(dt_vec, 13)
                    for t in range(TT):
                        pe.transpose(tb[0][:, rows(t)], dtw[:, 3, rows(t)], ident[:])
                    for t in range(TT):
                        pe.transpose(tb[0][:, (2 + t) * P:(3 + t) * P], dtw[:, 2, rows(t)], ident[:])
                    pe.transpose(tb[1][:, 0:P], dtw[:, 4, 0:P], ident[:])
                    pe.transpose(tb[1][:, P:2 * P], dtw[:, 4, P:2 * P], ident[:]).then_inc(col_tr, 1)
            wide(Pos(Q_P0), Pos(S_P0), turn_cols)
            pe.wait_ge(col_done, 2)
            wide(Pos(Q_P0 + 1), Pos(S_P0 + 8), with_z(Pos(0), None, Pos(Q_P0)))
            wide(Pos(Q_P1), Pos(S_P1), lambda k: chain(Pos(0), 4 + k))
            wide(Pos(Q_P1 + 1), Pos(S_P1 + 8), with_z(Pos(1), Pos(0), Pos(Q_P1)))
            with pe.Fori(0, 3) as c:
                q, s = Pos(Q_SSD, 8, c), Pos(S_SSD, 48, c)
                ge, go = Pos(2, 2, c), Pos(3, 2, c)
                gl = Pos(1, 2, c)
                wide(q, s, lambda k: chain(gl, 4 + k))
                wide(q + 1, s + 8, with_z(ge, gl, q))
                pe.wait_ge(gy_lo, ge.times(4).n)
                for n in range(4):
                    down(q + (2 + n), s + (16 + 4 * n), lambda k: chain(ge, 4 + k), n=n)
                wide(q + 6, s + 32)
                wide(q + 7, s + 40, with_z(go, ge, q + 6))
            g7 = Pos(7)
            pe.wait_ge(gy_lo, 4 * 7)
            for half in range(2):
                if half == 1:
                    turn_gy(g7)
                    pe.wait_ge(gy_lo, 4 * 8)
                for n in range(4):
                    q, s = Pos(Q_D3 + 4 * half + n), Pos(S_D3 + 8 * half + 2 * n)
                    down(q, s, (lambda k: chain(g7, 4 + k // 2) if k % 2 else None) if half == 0 else none,
                         range(4 * half, 4 * half + 4), n)

            def mlp(q0, s0, layer):
                with pe.Fori(0, CHUNKS) as c:
                    q, s = Pos(q0, 6, c), Pos(s0, 32, c)
                    u = Pos(2 * CHUNKS * layer, 2, c)
                    wide(q, s)
                    wide(q + 1, s + 8, lambda k: turn_h(u, k) if k < TT else None)
                    for t in range(TT):
                        pe.wait_ge(h_lo[t], (u + 1).n)
                        products(hT, range(0, 4), t, q + 2, s + 16, True, False)
                        turn_h(u + 1, t)
                    for t in range(TT):
                        pe.wait_ge(h_lo[t], (u + 2).n)
                        products(hT, range(4, 8), t, q + 2, s + 18, False, True)
                    for n in range(1, 4):
                        down(q + (2 + n), s + (16 + 4 * n))

            turn_x(8, x_norm)
            pe.wait_ge(tr_lo, 16)
            mlp(Q_M0, S_M0, 0)
            pe.wait_ge(bands_in, 16)
            pe.wait_ge(h_lo[0], 2 * CHUNKS)
            pe.wait_ge(h_lo[1], 2 * CHUNKS)
            pe.wait_ge(x_norm, 16)
            for u in range(8):
                wait(pe, tr_lo, Pos(16 + u - 1))
                for k in range(2):
                    ch = 2 * u + k
                    for t in range(TT):
                        mm = pe.matmul(tb[u % 2][:, k * T:(k + 1) * T], x[:, t, ch * P:(ch + 1) * P],
                                       bands[:, ch // CT, t, :], start=t == 0, stop=t == 1)
                mm.then_inc(tr_done, 1)
            for g in range(4):
                pe.wait_ge(tr_lo, 16 + 2 * g + 2)
                for t in range(TT):
                    products(xT, range(4 * g, 4 * g + 4), t, Pos(Q_POOL + g), Pos(S_POOL + 2 * g), True, True)
            for t in range(TT):
                for i in range(4):
                    u = 4 * t + i
                    pe.wait_ge(x_norm, 16 + u + 1)
                    wait(pe, tr_lo, Pos(24 + u - 1))
                    for k in range(CT):
                        mm = pe.transpose(tb[u % 2][:, k * P:(k + 1) * P],
                                          x[:, t, (CT * i + k) * P:(CT * i + k + 1) * P], ident[:])
                    mm.then_inc(tr_done, 1)
            pe.wait_ge(tr_lo, 32)
            mlp(Q_M1, S_M1, 1)

        @block.scalar
        def _(act):
            def split_hi(s):
                width = P if s.loop is None and s.base < S_BC else NB
                r = s.slot(RAW)
                act.wait_ge(raw_in[r], Pos(16 * (s.base // RAW + 1), 16 * s.step // RAW, s.loop).n)
                wait(act, w_used, s + (1 - RING))
                act.copy(whi[:, s.slot(RING), :, 0:width], raw[:, r, :, 0:width]).then_inc(hi_ready, 1)

            def none(k):
                pass

            def blocks(s, n, subs, after=none, ends=False):
                for b in range(n):
                    for i in range(subs):
                        if not ends or (s + (subs * b + 4 + i)).base < S_END:
                            split_hi(s + (subs * b + 4 + i))
                    for t in range(TT):
                        after(2 * b + t)

            def full(q, t, s_end):
                if t == 0:
                    act.wait_ge(acc_full[q.slot(2)], (q.half() + 1).n)
                else:
                    act.wait_ge(w_used, s_end.n)

            def out_of_psum(q, t, s_end, dst, func, width=NB):
                full(q, t, s_end)
                act.activation(dst, acc[q.slot(2)][t][:, 0:width], func).then_inc(acc_free[q.slot(2)][t], 1)

            def hi_x(first_quarter):
                for t in range(TT):
                    for i in range(4):
                        u = first_quarter + 4 * t + i
                        act.wait_ge(tr_done, u + 1)
                        act.copy(xT[0][:, CT * i:CT * (i + 1), t * P:(t + 1) * P],
                                 tb[u % 2][:].rearrange("p (k n) -> p k n", k=CT)).then_inc(tr_hi, 1)

            def pj_evac(q, s_end, t):
                out_of_psum(q, t, s_end, pj[:, t, :], ACT.Copy)

            def cvin_fill(k):
                act.wait_ge(cv_tr, (k + 1).n)
                for t in range(TT):
                    act.copy(cvin[:, :, PAD + t * P:PAD + (t + 1) * P],
                             tb[t][:].rearrange("p (j n) -> p j n", j=CT)).then_inc(cvin_full, 1)

            def silu_cv(k, dst):
                act.wait_ge(tap_done, (k + 1).times(TAPS * CT).n)
                act.activation(dst, cv[:], ACT.Silu).then_inc(cv_silu, 1)

            def decay(g, u):
                act.wait_ge(e_min, (g.times(4) + (u + 1)).n)
                act.activation(e1[:], e1[:], ACT.Exp).then_inc(e_exp, 1)

            def state_out(g, t):
                act.wait_ge(st_done, (g.times(2) + (t + 1)).n)
                act.copy(st[:, t, :], sbk[1][:]).then_inc(st_out, 1)

            def gy_high(g):
                act.wait_ge(gy_tr, (g + 1).n)
                for k in range(CT):
                    w = normw[:, bass.ds(g.times(CT).n + k, 1)]
                    act.activation(hT[0][:, CT * g.slot(2) + k, :], sbk[k // 2][:, (k % 2) * T:(k % 2 + 1) * T],
                                   ACT.Copy, scale=w).then_inc(gy_hi, 1)

            def chain(g, k, zq=None, z_end=None):
                if k == 0:
                    wait(act, e_sub, g.times(8))
                    cvin_fill(g + 4)
                elif k == 1:
                    silu_cv(g + 4, cv[:])
                    act.wait_ge(sc_done, (g + 1).n)
                    act.copy(btok[:].rearrange("p t n -> p (t n)"), sbk[1][:, 0:T]).then_inc(btok_done, 1)
                elif k == 2:
                    act.wait_ge(back_tr, (g + 1).n)
                    wait(act, xw_done, g.times(6))
                    wait(act, gy_skip, g.times(2))
                    for t in range(TT):
                        act.copy(xs[:, t, :], tb[t][:]).then_inc(xs_out, 1)
                    decay(g, 0)
                elif k == 3:
                    wait(act, gated, g.times(2))
                    wait(act, sumsq, g.times(2))
                    for t in range(TT):
                        out_of_psum(zq, t, z_end, zs[:, t, :], ACT.Silu)
                    state_out(g, 0)
                    decay(g, 1)
                elif k == 4:
                    decay(g, 2)
                elif k == 5:
                    state_out(g, 1)
                    decay(g, 3)
                elif k == 7:
                    act.wait_ge(gated, (g.times(2) + 2).n)
                    for t in range(TT):
                        act.activation(zs[:, t, :], gy[:, t, :], ACT.Square,
                                       accum_out=ss[:, t, 0:1]).then_inc(sumsq, 1)
                    for t in range(TT):
                        act.wait_ge(sumsq, (g.times(2) + (t + 1)).n)
                        act.activation(ss[:, t, 1:2], ss[:, t, 0:1], ACT.Sqrt, bias=eps[:],
                                       scale=1.0 / NB).then_inc(rooted, 1)

            def xs_group(q, s, g, prior=None):
                def after(k):
                    if k >= 2:
                        if k == 2:
                            wait(act, off_done, g.times(2) + -1)
                        else:
                            wait(act, off_done, g.times(2))
                        pj_evac(q, s + 8, k - 2)
                    if prior is not None:
                        chain(prior, 4 + k)
                blocks(s, 2, 4, after)

            def z_group(q, s, g, before):
                def after(k):
                    if k == 0 and before is not None:
                        gy_high(before)
                    chain(g, k, q, s + 8)
                blocks(s, 2, 4, after)

            def dt_steps(k):
                if k == 0:
                    act.wait_ge(dt_vec, 1)
                    act.activation(dtw[:, 0, :], dtw[:, 0, :], ACT.Exp, scale=-1.0).then_inc(dt_act, 1)
                    act.activation(dtp[:, 2:3], dtp[:, 1:2], ACT.Exp).then_inc(dt_act, 1)
                    act.wait_ge(dt_vec, 4)
                    act.activation(dtw[:, 3, :], dtw[:, 1, :], ACT.Ln).then_inc(dt_act, 1)
                    act.wait_ge(f_ready, 4)
                    f, h = dtw[:, 3, :], P // 2
                    act.activation(dtw[0:h, 4, 0:P], f[0:h, 0:P], ACT.Exp, scale=-1.0,
                                   bias=f[0:h, P - 1:P]).then_inc(dt_act, 1)
                    act.activation(dtw[h:P, 4, 0:P], f[h:P, P:T], ACT.Exp, scale=-1.0,
                                   bias=f[h:P, P:P + 1]).then_inc(dt_act, 1)
                    act.activation(dtw[0:h, 4, P:T], f[0:h, P:T], ACT.Exp).then_inc(dt_act, 1)
                    act.activation(dtw[h:P, 4, P:T], f[h:P, 0:P], ACT.Exp).then_inc(dt_act, 1)
                elif k == 2:
                    act.wait_ge(col_tr, 1)
                    act.copy(cols[:, 0:4, :], tb[0][:].rearrange("p (k n) -> p k n", k=4)).then_inc(col_done, 1)
                    act.copy(cols[:, 4:6, :], tb[1][:, 0:T].rearrange("p (k n) -> p k n", k=2)).then_inc(col_done, 1)

            act.wait_ge(const_in, 16 * 8)
            act.wait_ge(eps_set, 1)
            for i in range(4):
                split_hi(Pos(S_DT + i))
            hi_x(0)
            def dt_out(k):
                if k >= 2:
                    out_of_psum(Pos(Q_DT), k - 2, Pos(S_BC), pj[:, k - 2, 0:P], ACT.Copy, P)
            blocks(Pos(S_DT), 2, 4, dt_out)
            act.wait_ge(dk_tr, 1)
            with act.Fori(0, 2) as j:
                for i in range(2):
                    k, s = Pos(i, 2, j), Pos(S_BC + 8 * i, 16, j)
                    def bc_out(n):
                        if n >= 2:
                            out_of_psum(Pos(Q_BC + i, 2, j), n - 2, s + 8, pj[:, n - 2, :], ACT.Copy)
                        if n == 3:
                            cvin_fill(k)
                            silu_cv(k, area_a[:, bass.ds(j * (NG * T) + i * (CT * T), CT * T)].rearrange(
                                "p (g t) -> p g t", g=CT))
                    blocks(s, 2, 4, bc_out)

            def first_xs(k):
                dt_steps(k)
                if k >= 2:
                    pj_evac(Pos(Q_P0), Pos(S_P0 + 8), k - 2)
            blocks(Pos(S_P0), 2, 4, first_xs)
            z_group(Pos(Q_P0 + 1), Pos(S_P0 + 8), Pos(0), None)
            xs_group(Pos(Q_P1), Pos(S_P1), Pos(1), Pos(0))
            z_group(Pos(Q_P1 + 1), Pos(S_P1 + 8), Pos(1), Pos(0))
            with act.Fori(0, 3) as c:
                q, s = Pos(Q_SSD, 8, c), Pos(S_SSD, 48, c)
                gl, ge, go = Pos(1, 2, c), Pos(2, 2, c), Pos(3, 2, c)
                xs_group(q, s, ge, gl)
                z_group(q + 1, s + 8, ge, gl)
                blocks(s + 16, 4, 4, lambda k: chain(ge, 4 + k))
                xs_group(q + 6, s + 32, go)
                z_group(q + 7, s + 40, go, ge)
            blocks(Pos(S_D3), 4, 2, lambda k: chain(Pos(7), 4 + k // 2) if k % 2 else None)
            gy_high(Pos(7))
            blocks(Pos(S_D3 + 8), 4, 2)

            def root(i, t):
                act.wait_ge(ln_vec, 14 * (2 * i + t) + 5)
                act.activation(mv[:, t, 2:3], mv[:, t, 1:2], ACT.Sqrt, bias=eps[:]).then_inc(ln_root, 1)

            def hidden(q, s_end, u, t):
                out_of_psum(q, t, s_end, hr[:, t, :], ACT.Relu)
                act.wait_ge(acc_free[q.slot(2)][t], (q.half() + 1).n)
                act.activation(hr[:, t, :], hr[:, t, :], ACT.Square).then_inc(squared, 1)

            def hi_h(u, t):
                act.wait_ge(h_tr[t], (u + 1).n)
                kt = CT * u.slot(2)
                act.copy(hT[0][:, kt:kt + CT, t * P:(t + 1) * P],
                         tb[t][:].rearrange("p (k n) -> p k n", k=CT)).then_inc(h_hi[t], 1)

            def mlp_chunk(q, s, u, ends=False):
                blocks(s, 2, 4, lambda k: hidden(q, s + 8, u, k - 2) if k >= 2 else None)
                def second(k):
                    if k < 2:
                        hi_h(u, k)
                    else:
                        hidden(q + 1, s + 16, u + 1, k - 2)
                blocks(s + 8, 2, 4, second)
                blocks(s + 16, 1, 4, lambda t: hi_h(u + 1, t))
                blocks(s + 20, 3, 4, none, ends)

            def mlp(q0, s0, layer):
                last = CHUNKS - 1
                with act.Fori(0, last) as c:
                    mlp_chunk(Pos(q0, 6, c), Pos(s0, 32, c), Pos(2 * CHUNKS * layer, 2, c))
                mlp_chunk(Pos(q0 + 6 * last), Pos(s0 + 32 * last), Pos(2 * CHUNKS * layer + 2 * last), True)

            root(0, 0)
            root(0, 1)
            hi_x(8)
            act.wait_ge(yd_done, 4 * NG)
            mlp(Q_M0, S_M0, 0)
            root(1, 0)
            root(1, 1)
            for u in range(8):
                act.wait_ge(tr_done, 16 + u + 1)
                act.copy(xT[0][:, 2 * u:2 * u + 2, :],
                         tb[u % 2][:].rearrange("p (k n) -> p k n", k=2)).then_inc(tr_hi, 1)
            blocks(Pos(S_POOL), 4, 2)
            root(2, 0)
            root(2, 1)
            hi_x(24)
            mlp(Q_M1, S_M1, 1)
            root(3, 0)
            root(3, 1)

        @block.vector
        def _(dve):
            def split_lo(s):
                width = P if s.loop is None and s.base < S_BC else NB
                r, slot = s.slot(RAW), s.slot(RING)
                dve.wait_ge(hi_ready, (s + 1).n)
                dve.tensor_tensor(wlo[:, slot, :, 0:width], raw[:, r, :, 0:width],
                                  whi[:, slot, :, 0:width].bitcast(F32), ALU.subtract).then_inc(lo_ready, 1)

            def none(k):
                pass

            def blocks(s, n, subs, after=none, ends=False):
                for b in range(n):
                    for i in range(subs):
                        if not ends or (s + (subs * b + 4 + i)).base < S_END:
                            split_lo(s + (subs * b + 4 + i))
                    for t in range(TT):
                        after(2 * b + t)

            def full(q, t, s_end):
                if t == 0:
                    dve.wait_ge(acc_full[q.slot(2)], (q.half() + 1).n)
                else:
                    dve.wait_ge(w_used, s_end.n)

            def lo_of(dst, src, hi, done):
                dve.tensor_tensor(dst, src, hi.bitcast(F32), ALU.subtract).then_inc(done, 1)

            def lo_x(first_quarter):
                for t in range(TT):
                    for i in range(4):
                        u = first_quarter + 4 * t + i
                        dve.wait_ge(tr_hi, u + 1)
                        part = (slice(None), slice(CT * i, CT * (i + 1)), slice(t * P, (t + 1) * P))
                        lo_of(xT[1][part], tb[u % 2][:].rearrange("p (k n) -> p k n", k=CT), xT[0][part], tr_lo)

            def add_x(q, s_end, t, n):
                full(q, t, s_end)
                cs = slice(n * NB, (n + 1) * NB)
                dve.tensor_tensor(x[:, t, cs], x[:, t, cs], acc[q.slot(2)][t][:], ALU.add).then_inc(
                    acc_free[q.slot(2)][t], 1)

            def down(q, s, n, after=none, subs=4):
                def both(t):
                    add_x(q, s + subs, t, n)
                    after(2 * n + t)
                blocks(s, 1, subs, both)

            def set_pads():
                dve.memset(cvin[:, :, 0:PAD], 0.0).then_inc(pad_set, 1)
                dve.memset(cvin[:, :, PAD + T:PAD + T + PAD], 0.0).then_inc(pad_set, 1)

            def convolve(k, ch):
                dve.wait_ge(cvin_full, (k.times(2) + 2).n)
                n = k.times(TAPS * CT)
                for tap in range(TAPS):
                    for j in range(CT):
                        w = convw[:, bass.ds(ch.n + j, 1), tap]
                        src = cvin[:, j, tap:tap + T]
                        if tap == 0:
                            dve.tensor_scalar(cv[:, j, :], src, w, convb[:, bass.ds(ch.n + j, 1)],
                                              ALU.mult, ALU.add).then_inc(tap_done, 1)
                        else:
                            dve.wait_ge(tap_done, (n + (CT * (tap - 1) + j + 1)).n)
                            dve.scalar_tensor_tensor(cv[:, j, :], src, w, cv[:, j, :],
                                                     ALU.mult, ALU.add).then_inc(tap_done, 1)

            def gy_low(g):
                for k in range(CT):
                    dve.wait_ge(gy_hi, (g.times(CT) + 2 * (k // 2 + 1)).n)
                    kt = CT * g.slot(2) + k
                    w = normw[:, bass.ds(g.times(CT).n + k, 1)]
                    dve.scalar_tensor_tensor(hT[1][:, kt, :], sbk[k // 2][:, (k % 2) * T:(k % 2 + 1) * T], w,
                                             hT[0][:, kt, :].bitcast(F32), ALU.mult, ALU.subtract).then_inc(gy_lo, 1)

            def heads(buf, g, first):
                return buf[:, bass.ds(g.times(HPG).n + first, 4)]

            def unit(g, u):
                t, hh = u // 2, u % 2
                dve.wait_ge(fbc_in[u % 2], (g.times(64) + 32 * (u // 2 + 1)).n)
                wait(dve, m_done, g.times(8) + 2 * u)
                wait(dve, yd_done, g.times(4) + u)
                for d, dst in ((0, e1), (1, mb)):
                    col = heads(cols[:, t, :], g, d * NH + 4 * hh)
                    dve.tensor_tensor(dst[:], fbc[u % 2][:, d], col.unsqueeze(2).to_broadcast([P, 4, P]),
                                      ALU.subtract).then_inc(e_sub, 1)
                dve.wait_ge(e_sub, (g.times(8) + 2 * (u + 1)).n)
                dve.tensor_tensor(e1[:], e1[:], mb[:], ALU.min).then_inc(e_min, 1)
                dve.wait_ge(gt_done, (g.times(4) + 4).n)
                dve.wait_ge(e_exp, (g.times(4) + (u + 1)).n)
                for d, dst in ((0, mf), (1, mb)):
                    dve.tensor_tensor(dst[:], e1[:], gt[:, t, d, :].unsqueeze(1).to_broadcast([P, 4, P]),
                                      ALU.mult).then_inc(m_done, 1)

            def add_carried(g, t):
                o = 1 - t
                dve.wait_ge(off_done, (g.times(2) + (t + 1)).n)
                for h in range(HPG):
                    cs = slice(h * HD, (h + 1) * HD)
                    ef = cols[:, 5, bass.ds(g.times(HPG).n + t * NH + h, 1)]
                    dve.scalar_tensor_tensor(gy[:, o, cs], sbk[1][:, cs], ef, gy[:, o, cs],
                                             ALU.mult, ALU.add).then_inc(gy_off, 1)

            def chain(g, k, zq=None):
                if k == 0:
                    wait(dve, gy_tr, g)
                    wait(dve, e_sub, g.times(8))
                    set_pads()
                    dve.wait_ge(pad_set, (g.times(2) + 4).n)
                    convolve(g + 4, g.times(CT))
                elif k == 1:
                    dve.wait_ge(sc_done, (g + 1).n)
                    for t in range(TT):
                        for d in range(2):
                            dve.tensor_tensor(gt[:, t, d, :], sbk[0][:, t * P:(t + 1) * P], masks[:, d, :],
                                              ALU.mult).then_inc(gt_done, 1)
                elif k == 2:
                    unit(g, 0)
                elif k == 3:
                    unit(g, 1)
                elif k == 4:
                    dve.wait_ge(yd_done, (g.times(4) + 2).n)
                    dve.wait_ge(gy_skip, (g.times(2) + 2).n)
                    dve.tensor_tensor(gy[:, 0, :], gy[:, 0, :], sbk[0][:], ALU.add).then_inc(gy_yd, 1)
                    add_carried(g, 0)
                    unit(g, 2)
                elif k == 5:
                    unit(g, 3)
                elif k == 6:
                    dve.wait_ge(yd_done, (g.times(4) + 4).n)
                    dve.wait_ge(gy_off, (g.times(16) + 8).n)
                    dve.tensor_tensor(gy[:, 1, :], gy[:, 1, :], sbk[0][:], ALU.add).then_inc(gy_yd, 1)
                    dve.wait_ge(gy_yd, (g.times(2) + 1).n)
                    add_carried(g, 1)
                    dve.wait_ge(gy_off, (g.times(16) + 16).n)
                    dve.wait_ge(gy_yd, (g.times(2) + 2).n)
                    for t in range(TT):
                        dve.wait_ge(acc_free[zq.slot(2)][t], (zq.half() + 1).n)
                        dve.tensor_tensor(gy[:, t, :], gy[:, t, :], zs[:, t, :], ALU.mult).then_inc(gated, 1)
                elif k == 7:
                    for t in range(TT):
                        dve.wait_ge(rooted, (g.times(2) + (t + 1)).n)
                        dve.reciprocal(ss[:, t, 2:3], ss[:, t, 1:2]).then_inc(inv_root, 1)
                    for t in range(TT):
                        dve.wait_ge(inv_root, (g.times(2) + (t + 1)).n)
                        dve.tensor_scalar(gy[:, t, :], gy[:, t, :], ss[:, t, 2:3], None, ALU.mult).then_inc(gy_done, 1)

            def z_group(s, g, before):
                def after(k):
                    if k == 0 and before is not None:
                        gy_low(before)
                    chain(g, k)
                blocks(s, 2, 4, after)

            def dt_steps(k):
                if k != 0:
                    return
                h = P // 2
                dve.scalar_tensor_tensor(dtw[:, 0, :], dtv, -1.0, dtv, ALU.mult, ALU.max).then_inc(dt_vec, 1)
                dve.memset(dtw[:, 5, :], 1.0).then_inc(dt_vec, 1)
                dve.tensor_scalar(dtw[:, 2, :], dtv, 0.0, None, ALU.max).then_inc(dt_vec, 1)
                dve.wait_ge(dt_act, 1)
                dve.tensor_scalar(dtw[:, 1, :], dtw[:, 0, :], 1.0, None, ALU.add).then_inc(dt_vec, 1)
                dve.wait_ge(dt_vec, 4)
                dve.tensor_scalar(dtw[:, 4, :], dtw[:, 1, :], -1.0, TINY, ALU.add, ALU.add).then_inc(dt_vec, 1)
                dve.wait_ge(dt_vec, 5)
                dve.reciprocal(dtw[:, 4, :], dtw[:, 4, :]).then_inc(dt_vec, 1)
                dve.wait_ge(dt_vec, 6)
                dve.wait_ge(dt_act, 3)
                dve.scalar_tensor_tensor(dtw[:, 3, :], dtw[:, 3, :], TINY, dtw[:, 4, :], ALU.add, ALU.mult).then_inc(dt_vec, 1)
                dve.wait_ge(dt_vec, 7)
                dve.tensor_tensor(dtw[:, 3, :], dtw[:, 3, :], dtw[:, 0, :], ALU.mult).then_inc(dt_vec, 1)
                dve.wait_ge(dt_vec, 8)
                dve.tensor_tensor(dtw[:, 2, :], dtw[:, 2, :], dtw[:, 3, :], ALU.add).then_inc(dt_vec, 1)
                dve.tensor_scalar(dtp[:, 3:4], dtp[:, 2:3], -1.0, None, ALU.mult).then_inc(dt_vec, 1)
                dve.wait_ge(dt_vec, 10)
                dve.tensor_scalar(dtw[:, 0, :], dtw[:, 2, :], dtp[:, 3:4], None, ALU.mult).then_inc(dt_vec, 1)
                dve.wait_ge(dt_vec, 11)
                for t in range(TT):
                    for fwd in (True, False):
                        part = slice(0, h) if fwd else slice(h, P)
                        ts = slice(t * P, (t + 1) * P)
                        one, a_, f = dtw[part, 5, ts], dtw[part, 0, ts], dtw[part, 3, ts]
                        if not fwd:
                            a_, f = a_[:, ::-1], f[:, ::-1]
                        dve.tensor_tensor_scan(f, one, a_, 0.0, ALU.mult, ALU.add).then_inc(f_ready, 1)
                dve.wait_ge(dt_act, 7)
                dve.tensor_tensor(dtw[0:h, 4, 0:P], dtw[0:h, 4, 0:P], dtw[0:h, 2, 0:P], ALU.mult).then_inc(dt_vec, 1)
                dve.tensor_tensor(dtw[h:P, 4, 0:P], dtw[h:P, 4, 0:P], dtw[h:P, 2, P:T], ALU.mult).then_inc(dt_vec, 1)

            def layer_norm(i, t, q):
                n = 14 * (2 * i + t)
                for p in q:
                    dve.wait_ge(acc_free[p.slot(2)][t], (p.half() + 1).n)
                for j in range(4):
                    dve.bn_stats(bst[:, t, j, :], x[:, t, j * NB:(j + 1) * NB]).then_inc(ln_vec, 1)
                dve.wait_ge(ln_vec, n + 4)
                dve.bn_aggr(mv[:, t, 0:2], bst[:, t].rearrange("p j n -> p (j n)")).then_inc(ln_vec, 1)
                dve.wait_ge(ln_root, 2 * i + t + 1)
                dve.reciprocal(mv[:, t, 3:4], mv[:, t, 2:3]).then_inc(ln_vec, 1)
                dve.wait_ge(ln_vec, n + 6)
                for j in range(4):
                    part = x[:, t, j * NB:(j + 1) * NB]
                    dve.tensor_scalar(part, part, mv[:, t, 0:1], mv[:, t, 3:4], ALU.subtract, ALU.mult).then_inc(ln_vec, 1)
                dve.wait_ge(gb_in, 32 * (i + 1))
                for j in range(4):
                    cs = slice(j * NB, (j + 1) * NB)
                    dve.wait_ge(ln_vec, n + 6 + j + 1)
                    dve.tensor_tensor(x[:, t, cs], x[:, t, cs], gb[:, 0, cs], ALU.mult).then_inc(ln_vec, 1)
                    dve.wait_ge(ln_vec, n + 6 + 4 + j + 1)
                    dve.tensor_tensor(x[:, t, cs], x[:, t, cs], gb[:, 1, cs], ALU.add).then_inc(x_norm, 1)

            def lo_h(u, t):
                dve.wait_ge(h_hi[t], (u + 1).n)
                kt = CT * u.slot(2)
                part = (slice(None), slice(kt, kt + CT), slice(t * P, (t + 1) * P))
                lo_of(hT[1][part], tb[t][:].rearrange("p (k n) -> p k n", k=CT), hT[0][part], h_lo[t])

            def mlp_chunk(q, s, u, ends=False):
                blocks(s, 2, 4)
                blocks(s + 8, 2, 4, lambda k: lo_h(u, k) if k < 2 else None)
                for i in range(4):
                    split_lo(s + (20 + i))
                for t in range(TT):
                    lo_h(u + 1, t)
                for t in range(TT):
                    add_x(q + 2, s + 20, t, 0)
                for n in range(1, 4):
                    def both(t):
                        add_x(q + (2 + n), s + (20 + 4 * n), t, n)
                    blocks(s + (16 + 4 * n), 1, 4, both, ends)

            def mlp(q0, s0, layer):
                last = CHUNKS - 1
                with dve.Fori(0, last) as c:
                    mlp_chunk(Pos(q0, 6, c), Pos(s0, 32, c), Pos(2 * CHUNKS * layer, 2, c))
                mlp_chunk(Pos(q0 + 6 * last), Pos(s0 + 32 * last), Pos(2 * CHUNKS * layer + 2 * last), True)

            dve.memset(eps[:], EPS).then_inc(eps_set, 1)
            dve.wait_ge(const_in, 16 * 8)
            for i in range(4):
                split_lo(Pos(S_DT + i))
            lo_x(0)
            blocks(Pos(S_DT), 2, 4)
            dve.wait_ge(dk_tr, 1)
            dve.tensor_scalar(dtv, tb[0][:, 0:T], dtp[:, 0:1], None, ALU.add).then_inc(dtv_done, 1)
            set_pads()
            dve.wait_ge(pad_set, 2)
            with dve.Fori(0, 2) as j:
                for i in range(2):
                    blocks(Pos(S_BC + 8 * i, 16, j), 2, 4,
                           lambda n: convolve(Pos(i, 2, j), Pos(CH_B + CT * i, 2 * CT, j)) if n == 3 else None)
            dve.wait_ge(dtv_done, 1)
            blocks(Pos(S_P0), 2, 4, dt_steps)
            dve.wait_ge(col_done, 2)
            z_group(Pos(S_P0 + 8), Pos(0), None)
            blocks(Pos(S_P1), 2, 4, lambda k: chain(Pos(0), 4 + k, Pos(Q_P0 + 1)))
            z_group(Pos(S_P1 + 8), Pos(1), Pos(0))
            dve.wait_ge(x_scaled, 1)
            with dve.Fori(0, 3) as c:
                q, s = Pos(Q_SSD, 8, c), Pos(S_SSD, 48, c)
                gl, ge, go = Pos(1, 2, c), Pos(2, 2, c), Pos(3, 2, c)
                blocks(s, 2, 4, lambda k: chain(gl, 4 + k, q + -1))
                z_group(s + 8, ge, gl)
                for n in range(4):
                    down(q + (2 + n), s + (16 + 4 * n), n, lambda k: chain(ge, 4 + k, q + 1))
                blocks(s + 32, 2, 4)
                z_group(s + 40, go, ge)
            for n in range(4):
                down(Pos(Q_D3 + n), Pos(S_D3 + 2 * n), n,
                     lambda k: chain(Pos(7), 4 + k // 2, Pos(Q_D3 - 1)) if k % 2 else None, 2)
            gy_low(Pos(7))
            for n in range(4):
                down(Pos(Q_D3 + 4 + n), Pos(S_D3 + 8 + 2 * n), n, none, 2)

            for t in range(TT):
                layer_norm(0, t, (Pos(Q_M0 - 2), Pos(Q_M0 - 1)))
            lo_x(8)
            dve.wait_ge(x_scaled, 2)
            mlp(Q_M0, S_M0, 0)
            for t in range(TT):
                layer_norm(1, t, (Pos(Q_POOL - 2), Pos(Q_POOL - 1)))
            for u in range(8):
                dve.wait_ge(tr_hi, 16 + u + 1)
                lo_of(xT[1][:, 2 * u:2 * u + 2, :], tb[u % 2][:].rearrange("p (k n) -> p k n", k=2),
                      xT[0][:, 2 * u:2 * u + 2, :], tr_lo)
            dve.wait_ge(x_scaled, 3)
            dve.wait_ge(psc_in, 32)
            for g in range(4):
                q, s = Pos(Q_POOL + g), Pos(S_POOL + 2 * g)
                cs = slice(g * NB, (g + 1) * NB)
                def pooled(t):
                    full(q, t, s + 2)
                    wait(dve, pool_added, Pos(2 * g + t))
                    dve.tensor_tensor(ptmp, acc[q.slot(2)][t][:], psc[:, 0, cs], ALU.mult).then_inc(
                        acc_free[q.slot(2)][t], 1)
                    dve.wait_ge(acc_free[q.slot(2)][t], (q.half() + 1).n)
                    dve.tensor_tensor(x[:, t, cs], x[:, t, cs], ptmp, ALU.add).then_inc(pool_added, 1)
                blocks(s, 1, 2, pooled)
            dve.wait_ge(pool_added, 8)
            for t in range(TT):
                layer_norm(2, t, ())
            lo_x(24)
            dve.wait_ge(x_scaled, 4)
            mlp(Q_M1, S_M1, 1)
            for t in range(TT):
                layer_norm(3, t, (Pos(Q_M1 + 6 * CHUNKS - 2), Pos(Q_M1 + 6 * CHUNKS - 1)))

        @block.gpsimd
        def _(pool):
            for dst, name in ((ident, "ident"), (masks, "masks"), (convw, "conv_w"), (convb, "conv_b"),
                              (normw, "norm_w")):
                pool.dma_start(dst[:], a[name]).then_inc(const_in, 16)
            pool.dma_start(dtp[:, 0:1], a["dt_bias"]).then_inc(const_in, 16)
            pool.dma_start(dtp[:, 1:2], a["a_log"]).then_inc(const_in, 16)
            pool.dma_start(dskip[:], a["d_skip"].partition_broadcast(P)).then_inc(const_in, 16)

            def scale_x(i):
                pool.wait_ge(tr_done, 8 * i)
                pool.tensor_scalar(x[:], x[:], ALPHA, None, ALU.mult).then_inc(x_scaled, 1)

            def load_gb(i):
                for m, name in enumerate(("ln_g", "ln_b")):
                    pool.dma_start(gb[:, m, :], a[name][i].partition_broadcast(P)).then_inc(gb_in, 16)

            def load_f(g, u):
                t, hh = u // 2, u % 2
                for d in range(2):
                    src = f_rows[d, bass.ds(g.times(HPG).n + 4 * hh, 4), t * P:(t + 1) * P]
                    pool.dma_start(fbc[u % 2][:, d], src.partition_broadcast(P)).then_inc(fbc_in[u % 2], 16)

            def weigh(g, t):
                pool.wait_ge(xs_out, (g.times(2) + 2).n)
                src = xs[:, t, :].rearrange("p (h c) -> p h c", h=HPG)
                for i, row in ((0, cols[:, 2 + t, :]), (1, cols[:, 2 + t, :]), (2, cols[:, 4, :])):
                    first = NH if i == 1 or (i == 2 and t == 1) else 0
                    w = row[:, bass.ds(g.times(HPG).n + first, HPG)].unsqueeze(2).to_broadcast([P, HPG, HD])
                    pool.tensor_tensor(xw[:, i, :].rearrange("p (h c) -> p h c", h=HPG), src, w,
                                       ALU.mult).then_inc(xw_done, 1)

            def skip(g):
                for t in range(TT):
                    w = dskip[:, bass.ds(g.times(HPG).n, HPG)].unsqueeze(2).to_broadcast([P, HPG, HD])
                    pool.tensor_tensor(gy[:, t, :].rearrange("p (h c) -> p h c", h=HPG),
                                       xs[:, t, :].rearrange("p (h c) -> p h c", h=HPG), w, ALU.mult).then_inc(gy_skip, 1)

            def head_group(g):
                wait(pool, off_done, g.times(2))
                for m in range(2):
                    src = area_a[:, bass.ds(g.times(T).n + m * (NG * T), T)]
                    if m == 1:
                        pool.tensor_copy(cur[:, m, :], src).then_inc(cur_done, 1)
                    else:
                        pool.tensor_copy(cur[:, m, :], src).then_inc(cur_half, 1)
                pool.wait_ge(tap_done, (g + 5).times(TAPS * CT).n)
                load_f(g, 0)
                load_f(g, 1)
                wait(pool, yd_done, g.times(4))
                weigh(g, 0)
                skip(g)
                pool.wait_ge(e_sub, (g.times(8) + 2).n)
                load_f(g, 2)
                pool.wait_ge(e_sub, (g.times(8) + 4).n)
                load_f(g, 3)
                pool.wait_ge(yd_done, (g.times(4) + 2).n)
                pool.wait_ge(st_done, (g.times(2) + 1).n)
                weigh(g, 1)

            scale_x(1)
            pool.wait_ge(f_ready, 4)
            pool.dma_start(fscr, dtw[:, 3, :]).then_inc(f_saved, 16)
            pool.wait_ge(f_saved, 16)
            pool.wait_ge(cv_silu, 4)
            pool.wait_ge(col_done, 2)
            head_group(Pos(0))
            with pool.Fori(0, NG - 1) as c:
                head_group(Pos(1, 1, c))
            pool.wait_ge(cur_done, NG)
            load_gb(0)
            pool.wait_ge(e_sub, 8 * NG)
            pool.dma_start(bands[:], a["bands"]).then_inc(bands_in, 16)
            pool.wait_ge(gy_tr, NG)
            for m, name in enumerate(("pool_scale", "pool_b")):
                pool.dma_start(psc[:, m, :], a[name].partition_broadcast(P)).then_inc(psc_in, 16)
            pool.wait_ge(psc_in, 32)
            pool.tensor_tensor(psc[:, 1, :], psc[:, 1, :], psc[:, 0, :], ALU.mult).then_inc(bias_scaled, 1)
            scale_x(2)
            pool.wait_ge(x_norm, 8)
            load_gb(1)
            pool.wait_ge(x_norm, 16)
            load_gb(2)
            pool.wait_ge(tr_done, 24)
            pool.tensor_scalar(x[:], x[:], ALPHA, None, ALU.mult).then_inc(x_times, 1)
            pool.wait_ge(x_times, 1)
            pool.wait_ge(bias_scaled, 1)
            for t in range(TT):
                pool.tensor_tensor(x[:, t, :], x[:, t, :], psc[:, 1, :], ALU.add).then_inc(
                    x_scaled if t == 1 else x_times, 1)
            pool.wait_ge(x_norm, 24)
            load_gb(3)
            scale_x(4)


def kernel(**inputs):
    import numpy as np
    import concourse.bacc as bacc
    from concourse.bass_utils import run_bass_kernel_spmd

    s, l = np.arange(P)[:, None], np.arange(P)[None, :]
    masks = np.stack([s <= l, s >= l], axis=1).astype(np.float32)
    bands = np.zeros((T, len(WINDOWS), T), np.float32)
    for i, w in enumerate(WINDOWS):
        for t in range(T):
            lo, hi = max(t - w // 2, 0), min(t - w // 2 + w, T)
            bands[lo:hi, i, t] = np.float32(1.0) / np.float32(hi - lo)
            bands[t, i, t] -= 1.0
    bands = bands.reshape(TT, P, len(WINDOWS), T).transpose(1, 2, 0, 3)

    def by_channel(v):
        return np.asarray(v).reshape(-1, P).T

    d = {k: np.asarray(v) for k, v in inputs.items()}
    arrays = {
        "x": d["x"][0], "in_proj": d["ssd_in_proj"][0], "out_proj": d["ssd_out_proj"][0],
        "pool_w": d["pool_w"][0], "w1": d["mlp_w1"], "w2": d["mlp_w2"],
        "conv_w": d["ssd_conv_w"][0, :, 0, :].reshape(TAPS, -1, P).transpose(2, 1, 0),
        "conv_b": by_channel(d["ssd_conv_b"][0]), "norm_w": by_channel(d["ssd_norm_w"][0]),
        "dt_bias": d["ssd_dt_bias"][0].reshape(P, 1), "a_log": d["ssd_A_log"][0].reshape(P, 1),
        "d_skip": d["ssd_D"][0], "pool_scale": d["pool_scale"][0], "pool_b": d["pool_b"][0].reshape(DM),
        "ln_g": np.stack([d["ln_mix_g"][0], d["ln_ffn_g"][0], d["ln_mix_g"][1], d["ln_ffn_g"][1]]),
        "ln_b": np.stack([d["ln_mix_b"][0], d["ln_ffn_b"][0], d["ln_mix_b"][1], d["ln_ffn_b"][1]]),
        "ident": np.eye(P, dtype=np.float32), "masks": masks, "bands": bands,
    }
    arrays = {k: np.ascontiguousarray(v) for k, v in arrays.items()}
    nc = bacc.Bacc("TRN2", target_bir_lowering=False, num_devices=1)
    aps = {k: nc.dram_tensor(f"in_{k}", v.shape, mybir.dt.from_np(v.dtype), kind="ExternalInput").ap()
           for k, v in arrays.items()}
    out = nc.dram_tensor("out", (T, DM), F32, kind="ExternalOutput").ap()
    build(nc, aps, out)
    r = run_bass_kernel_spmd(nc, [{f"in_{k}": v for k, v in arrays.items()}], core_ids=[0])
    return r.results[0]["out"].reshape(1, T, DM)
```

```python
from contextlib import ExitStack

import concourse.bass as bass
from concourse import mybir

F32 = mybir.dt.float32
F32R = mybir.dt.float32r
ALU = mybir.AluOpType
ACT = mybir.ActivationFunctionType

P = 128
DM = 2048
T = 256
TT = T // P
DEPTH = 2
DI = 2 * DM
HD = 64
NH = DI // HD
NG = 8
HPG = NH // NG
TAPS = 5
PAD = TAPS // 2
DFF = 4 * DM
NB = 512
KT = DM // P
CT = NB // P
XS0, B0, DT0 = DI, 2 * DI, 2 * DI + 2 * NG * P
CH_B = DI // P
CK = 8
CHUNKS = DFF // (CK * P)
WINDOWS = (2, 4, 8, 16)
ALPHA = (2.0 * DEPTH) ** 0.25
EPS = 1e-5
TINY = 1e-30
RING = 8
RAW = 4
SUBK = 2


class Pos:

    def __init__(self, base, step=0, loop=None):
        self.base, self.step, self.loop = base, step, loop

    def __add__(self, k):
        return Pos(self.base + k, self.step, self.loop)

    def times(self, k):
        return Pos(self.base * k, self.step * k, self.loop)

    def half(self):
        assert self.step % 2 == 0
        return Pos(self.base // 2, self.step // 2, self.loop)

    def slot(self, n):
        assert self.step % n == 0
        return self.base % n

    @property
    def n(self):
        return self.base if self.loop is None else self.loop * self.step + self.base


def wait(eng, sem, pos):
    if pos.loop is None and pos.base <= 0:
        return
    eng.wait_ge(sem, pos.n)


Q_DT, S_DT = 2, 0
Q_BC, S_BC = Q_DT + 1, 8
Q_P0, S_P0 = Q_BC + 4, S_BC + 32
Q_P1, S_P1 = Q_P0 + 2, S_P0 + 16
Q_SSD, S_SSD = Q_P1 + 2, S_P1 + 16
Q_D3, S_D3 = Q_SSD + 3 * 8, S_SSD + 3 * 48
Q_M0, S_M0 = Q_D3 + 8, S_D3 + 16
Q_POOL, S_POOL = Q_M0 + 6 * CHUNKS, S_M0 + 32 * CHUNKS
Q_M1, S_M1 = Q_POOL + 4, S_POOL + 8
S_END = S_M1 + 32 * CHUNKS


def build(nc, a, out):
    with ExitStack() as ctx:
        def sb(name, shape, dt=F32):
            return ctx.enter_context(nc.sbuf_tensor(name, shape, dt))

        def pb(name, shape):
            return ctx.enter_context(nc.psum_tensor(name, shape, F32))

        def sem(name):
            return ctx.enter_context(nc.semaphore(name))

        x = sb("x", [P, TT, DM])
        xT = [sb("xTh", [P, KT, T], F32R), sb("xTl", [P, KT, T], F32R)]
        hT = [sb("hTh", [P, CK, T], F32R), sb("hTl", [P, CK, T], F32R)]
        raw = sb("raw", [P, RAW, SUBK, NB])
        whi = sb("whi", [P, RING, SUBK, NB], F32R)
        wlo = sb("wlo", [P, RING, SUBK, NB], F32R)
        ident = sb("ident", [P, P])
        eps = sb("eps", [P, 1])

        area_a = sb("area_a", [P, 2 * NG * T])
        bcT = area_a[:].rearrange("p (m g t) -> p m g t", m=2, g=NG)
        gb = area_a[:].rearrange("p (m n) -> p m n", m=2)
        area_b = sb("area_b", [P, 4 * TT * NB])
        quarter = [area_b[:, i * TT * NB:(i + 1) * TT * NB] for i in range(4)]
        pj = quarter[0].rearrange("p (t n) -> p t n", t=TT)
        st = pj
        xs = quarter[1].rearrange("p (t n) -> p t n", t=TT)
        zs = quarter[2].rearrange("p (t n) -> p t n", t=TT)
        gy = quarter[3].rearrange("p (t n) -> p t n", t=TT)
        cv = quarter[3].rearrange("p (j n) -> p j n", j=CT)
        psc = area_b[:].rearrange("p (m n) -> p m n", m=2)
        area_c = sb("area_c", [P, 3 * 4 * P])
        e1, e2, mx = (area_c[:, i * 4 * P:(i + 1) * 4 * P].rearrange("p (h l) -> p h l", h=4) for i in range(3))
        hr = area_c[:, 0:TT * NB].rearrange("p (t n) -> p t n", t=TT)
        ptmp = area_c[:, 2 * NB:3 * NB]
        dtw = area_c[:].rearrange("p (k t) -> p k t", k=6)
        area_d = sb("area_d", [P, 2 * 2 * 4 * P])
        fbc = [area_d[:, i * 8 * P:(i + 1) * 8 * P].rearrange("p (d h l) -> p d h l", d=2, h=4) for i in range(2)]
        cvin = area_d[:, 0:CT * (T + 2 * PAD)].rearrange("p (j n) -> p j n", j=CT)
        bands = area_d[:].rearrange("p (w s t) -> p w s t", w=4, s=TT)
        xw = sb("xw", [P, NB])
        gd = sb("gd", [P, 2, 4, P])
        cur = sb("cur", [P, 2, T])
        btok = sb("btok", [P, TT, P])
        gt = sb("gt", [P, TT, 2, P])
        cols = sb("cols", [P, 6, P])
        dtv = cols[:, 0:2, :].rearrange("p k t -> p (k t)")
        masks = sb("masks", [P, 2, P])
        convw = sb("convw", [P, (DI + 2 * NG * P) // P, TAPS])
        convb = sb("convb", [P, (DI + 2 * NG * P) // P])
        normw = sb("normw", [P, DI // P])
        dskip = sb("dskip", [P, NH])
        dtp = sb("dtp", [P, 4])
        ss = sb("ss", [P, TT, 3])
        bst = sb("bst", [P, TT, 4, 6])
        mv = sb("mv", [P, TT, 4])

        acc = [[pb(f"acc{i}{t}", [P, NB]) for t in range(TT)] for i in range(2)]
        tb = [pb(f"tb{i}", [P, NB]) for i in range(2)]
        sbk = [pb(f"sbk{i}", [P, NB]) for i in range(2)]
        fscr = nc.dram_tensor("f_scratch", (P, T), F32).ap()

        raw_in = [sem(f"raw_in{r}") for r in range(RAW)]
        hi_ready, lo_ready, w_used = sem("hi_ready"), sem("lo_ready"), sem("w_used")
        acc_full = [sem(f"acc_full{i}") for i in range(2)]
        acc_free = [[sem(f"acc_free{i}{t}") for t in range(TT)] for i in range(2)]
        x_in = [sem("x_in_t0_left"), sem("x_in_t0_right"), sem("x_in_t1")]
        ident_in, const_in, eps_set = sem("ident_in"), sem("const_in"), sem("eps_set")
        tr_done, tr_hi, tr_lo = sem("tr_done"), sem("tr_hi"), sem("tr_lo")
        x_scaled, squared = sem("x_scaled"), sem("squared")
        h_tr = [sem(f"h_tr{t}") for t in range(TT)]
        h_hi = [sem(f"h_hi{t}") for t in range(TT)]
        h_lo = [sem(f"h_lo{t}") for t in range(TT)]
        ln_vec = [sem(f"ln_vec{t}") for t in range(TT)]
        ln_root = [sem(f"ln_root{t}") for t in range(TT)]
        x_norm = [sem(f"x_norm{t}") for t in range(TT)]
        gb_in = sem("gb_in")
        stored = sem("stored")
        dk_tr, dtv_done, dt_vec, dt_act = (sem(n) for n in ("dk_tr", "dtv_done", "dt_vec", "dt_act"))
        f_ready, f_saved, col_tr, col_done = (sem(n) for n in ("f_ready", "f_saved", "col_tr", "col_done"))
        cv_tr, cvin_full, pad_set, tap_done, cv_silu = (
            sem(n) for n in ("cv_tr", "cvin_full", "pad_set", "tap_done", "cv_silu"))
        cur_half = sem("cur_half")
        back_tr, xs_out, cur_done, sc_done, gt_done, btok_done = (
            sem(n) for n in ("back_tr", "xs_out", "cur_done", "sc_done", "gt_done", "btok_done"))
        fbc_in = [sem(f"fbc_in{i}") for i in range(2)]
        e_sub, e_min, e_exp, m_done, yd_done = (sem(n) for n in ("e_sub", "e_min", "e_exp", "m_done", "yd_done"))
        xw_done, gy_skip, st_done, st_out, off_done = (
            sem(n) for n in ("xw_done", "gy_skip", "st_done", "st_out", "off_done"))
        gy_yd, gy_off, gated, sumsq, rooted, inv_root, gy_done = (
            sem(n) for n in ("gy_yd", "gy_off", "gated", "sumsq", "rooted", "inv_root", "gy_done"))
        gy_tr, gy_hi, gy_lo = sem("gy_tr"), sem("gy_hi"), sem("gy_lo")
        bands_in, psc_in, bias_scaled, pool_added, pool_bias = (
            sem(n) for n in ("bands_in", "psc_in", "bias_scaled", "pool_added", "pool_bias"))
        gd_part, gd_done = sem("gd_part"), sem("gd_done")

        block = ctx.enter_context(nc.Block())

        in_w = a["in_proj"].rearrange("(k p) n -> p k n", p=P)
        out_w = a["out_proj"].rearrange("(k p) n -> p k n", p=P)
        w1 = [a["w1"][i].rearrange("(k p) n -> p k n", p=P) for i in range(DEPTH)]
        w2 = [a["w2"][i].rearrange("(k p) n -> p k n", p=P) for i in range(DEPTH)]
        pool_w = a["pool_w"].rearrange("g (k p) n -> g p k n", p=P)
        x_rows = a["x"].rearrange("(t p) n -> p t n", p=P)
        out_rows = out.rearrange("(t p) n -> p t n", p=P)
        f_rows = fscr.rearrange("(d h) t -> d h t", d=2)

        @block.sync
        def _(sp):
            sp.dma_start(ident[:], a["ident"]).then_inc(ident_in, 16)
            for h in range(2):
                cs = slice(h * DM // 2, (h + 1) * DM // 2)
                sp.dma_start(x[:, 0, cs], x_rows[:, 0, cs]).then_inc(x_in[h], 16)

            def load(s, src, width=NB):
                wait(sp, lo_ready, s + (1 - RAW))
                r = s.slot(RAW)
                sp.dma_start(raw[:, r, :, 0:width], src).then_inc(raw_in[r], 16)

            def load_in(s, col, width=NB):
                for i in range(KT // SUBK):
                    load(s + i, in_w[:, SUBK * i:SUBK * (i + 1), bass.ds(col, width)], width)

            def load_down(s, w, row, n, subs=CK // SUBK):
                for i in range(subs):
                    load(s + i, w[:, bass.ds(row + SUBK * i, SUBK), n * NB:(n + 1) * NB])

            def load_mlp(s0, layer):
                with sp.Fori(0, CHUNKS) as c:
                    s = Pos(s0, 32, c)
                    for j in range(2):
                        for i in range(KT // SUBK):
                            load(s + (8 * j + i), w1[layer][:, SUBK * i:SUBK * (i + 1), bass.ds(c * (CK * P) + j * NB, NB)])
                    for n in range(4):
                        load_down(s + (16 + 4 * n), w2[layer], c * CK, n)

            for i in range(RAW):
                load(Pos(S_DT + i), in_w[:, SUBK * i:SUBK * (i + 1), DT0:DT0 + P], P)
            sp.dma_start(x[:, 1, :], x_rows[:, 1, :]).then_inc(x_in[2], 16)
            for i in range(RAW, KT // SUBK):
                load(Pos(S_DT + i), in_w[:, SUBK * i:SUBK * (i + 1), DT0:DT0 + P], P)
            with sp.Fori(0, 2) as j:
                for i in range(2):
                    load_in(Pos(S_BC + 8 * i, 16, j), j * (2 * NB) + (B0 + i * NB))
            for g in range(2):
                load_in(Pos(S_P0 + 16 * g), XS0 + g * NB)
                load_in(Pos(S_P0 + 16 * g + 8), g * NB)
            with sp.Fori(0, 3) as c:
                s = Pos(S_SSD, 48, c)
                load_in(s, c * (2 * NB) + (XS0 + 2 * NB))
                load_in(s + 8, c * (2 * NB) + 2 * NB)
                for n in range(4):
                    load_down(s + (16 + 4 * n), out_w, c * CK, n)
                load_in(s + 32, c * (2 * NB) + (XS0 + 3 * NB))
                load_in(s + 40, c * (2 * NB) + 3 * NB)
            for half in range(2):
                for n in range(4):
                    load_down(Pos(S_D3 + 8 * half + 2 * n), out_w, 3 * CK + 4 * half, n, 2)
            load_mlp(S_M0, 0)
            for g in range(4):
                for i in range(2):
                    load(Pos(S_POOL + 2 * g + i), pool_w[g][:, SUBK * i:SUBK * (i + 1), :])
            load_mlp(S_M1, 1)
            for t in range(TT):
                for i in range(4):
                    sp.wait_ge(x_norm[t], 3 * 4 + i + 1)
                    cs = slice(i * NB, (i + 1) * NB)
                    sp.dma_start(out_rows[:, t, cs], x[:, t, cs]).then_inc(stored, 16)
            sp.wait_ge(stored, 16 * TT * 4)

        @block.tensor
        def _(pe):
            def rows(t):
                return slice(t * P, (t + 1) * P)

            def products(lhs, kts, t, q, s, first, last, width=NB):
                pair = q.slot(2)
                if first:
                    pe.wait_ge(acc_free[pair][t], q.half().n)
                dst = acc[pair][t][:, 0:width]
                for i, kt in enumerate(kts):
                    slot = (s + i // SUBK).slot(RING)
                    if t == 0 and i % SUBK == 0:
                        wait(pe, lo_ready, s + (i // SUBK + 1))
                    hi, lo = whi[:, slot, i % SUBK, 0:width], wlo[:, slot, i % SUBK, 0:width]
                    end = last and i == len(kts) - 1
                    pe.matmul(dst, lhs[1][:, kt, rows(t)], hi, start=first and i == 0, stop=False)
                    pe.matmul(dst, lhs[0][:, kt, rows(t)], hi, start=False, stop=False)
                    mm = pe.matmul(dst, lhs[0][:, kt, rows(t)], lo, start=False, stop=end)
                    if t == 1 and i % SUBK == SUBK - 1:
                        mm.then_inc(w_used, 1)
                    elif end:
                        mm.then_inc(acc_full[pair], 1)

            def none(k):
                pass

            def wide(q, s, after=none, width=NB):
                for b in range(2):
                    for t in range(TT):
                        products(xT, range(8 * b, 8 * b + 8), t, q, s + 4 * b, b == 0, b == 1, width)
                        after(2 * b + t)

            def down(q, s, after=none, kts=range(CK), n=0):
                for t in range(TT):
                    products(hT, kts, t, q, s, True, True)
                    after(2 * n + t)

            def turn_x(first, t, ready):
                for i in range(4):
                    u = first + 4 * t + i
                    ready(i)
                    wait(pe, tr_lo, Pos(u - 1))
                    for k in range(CT):
                        mm = pe.transpose(tb[u % 2][:, k * P:(k + 1) * P],
                                          x[:, t, (CT * i + k) * P:(CT * i + k + 1) * P], ident[:])
                    mm.then_inc(tr_done, 1)

            def wide_turning(q, s, first, ready, width=NB):
                turn_x(first, 0, lambda i: ready(0, i))
                pe.wait_ge(tr_lo, first + 4)
                def after(k):
                    if k == 0:
                        turn_x(first, 1, lambda i: ready(1, i))
                        pe.wait_ge(tr_lo, first + 8)
                wide(q, s, after, width)

            def turn_h(u, t):
                pe.wait_ge(squared, (u.times(2) + (t + 1)).n)
                for k in range(CT):
                    mm = pe.transpose(tb[t][:, k * P:(k + 1) * P], hr[:, t, k * P:(k + 1) * P], ident[:])
                mm.then_inc(h_tr[t], 1)

            def turn_pj(q):
                for t in range(TT):
                    pe.wait_ge(acc_free[q.slot(2)][t], (q.half() + 1).n)
                for t in range(TT):
                    for j in range(CT):
                        mm = pe.transpose(tb[t][:, j * P:(j + 1) * P], pj[:, t, j * P:(j + 1) * P], ident[:])
                mm.then_inc(cv_tr, 1)

            def score(g):
                pe.wait_ge(cur_done, (g + 1).n)
                wait(pe, gy_lo, g.times(4))
                for t in range(TT):
                    pe.matmul(sbk[0][:, rows(t)], cur[:, 0, rows(t)], cur[:, 1, rows(t)], start=True, stop=True)
                for t in range(TT):
                    mm = pe.transpose(sbk[1][:, rows(t)], cur[:, 0, rows(t)], ident[:])
                mm.then_inc(sc_done, 1)

            def turn_back(g):
                pe.wait_ge(cv_silu, (g + (4 + 1)).n)
                pe.wait_ge(cvin_full, (g.times(2) + 2 * (4 + 1)).n)
                for t in range(TT):
                    for j in range(CT):
                        mm = pe.transpose(tb[t][:, j * P:(j + 1) * P], cv[:, j, rows(t)], ident[:])
                mm.then_inc(back_tr, 1)

            def diag(g, u):
                t, hh = u // 2, u % 2
                pe.wait_ge(m_done, (g.times(4) + (u + 1)).n)
                pe.wait_ge(xs_out, (g.times(2) + (t + 1)).n)
                if u == 0:
                    pe.wait_ge(gt_done, (g.times(4) + 4).n)
                if u == 2:
                    pe.wait_ge(gy_yd, (g.times(2) + 1).n)
                for h in range(4):
                    cs = slice((4 * hh + h) * HD, (4 * hh + h + 1) * HD)
                    mm = pe.matmul(sbk[0][:, cs], mx[:, h, :], xs[:, t, cs], start=True, stop=True)
                mm.then_inc(yd_done, 1)

            def state(g, t):
                if t == 0:
                    pe.wait_ge(btok_done, (g + 1).n)
                else:
                    pe.wait_ge(gy_off, (g.times(16) + 8).n)
                pe.wait_ge(xw_done, (g.times(2) + (t + 1)).n)
                pe.matmul(sbk[1][:], btok[:, t, :], xw[:], start=True, stop=True).then_inc(st_done, 1)

            def carried(g, t):
                pe.wait_ge(st_out, (g.times(2) + (t + 1)).n)
                pe.matmul(sbk[1][:], cur[:, 1, rows(1 - t)], st[:, t, :], start=True, stop=True).then_inc(off_done, 1)

            def turn_gy(g):
                pe.wait_ge(gy_done, (g.times(2) + 2).n)
                pe.wait_ge(gy_off, (g.times(16) + 16).n)
                for b in range(2):
                    for k in range(2):
                        for t in range(TT):
                            ch = 2 * b + k
                            mm = pe.transpose(sbk[b][:, (2 * k + t) * P:(2 * k + t + 1) * P],
                                              gy[:, t, ch * P:(ch + 1) * P], ident[:])
                mm.then_inc(gy_tr, 1)

            def chain(g, k, q=None):
                if k == 0:
                    turn_pj(q)
                elif k == 1:
                    score(g)
                elif k == 2:
                    turn_back(g)
                elif k == 3:
                    diag(g, 0)
                    state(g, 0)
                elif k == 4:
                    diag(g, 1)
                    carried(g, 0)
                elif k == 5:
                    diag(g, 2)
                    state(g, 1)
                elif k == 6:
                    diag(g, 3)
                    carried(g, 1)

            def with_z(g, before, q):
                def after(k):
                    if k == 0 and before is not None:
                        turn_gy(before)
                    chain(g, k, q)
                return after

            pe.wait_ge(ident_in, 16)
            wide_turning(Pos(Q_DT), Pos(S_DT), 0,
                         lambda t, i: pe.wait_ge(x_in[i // 2 if t == 0 else 2], 16), P)
            for t in range(TT):
                pe.wait_ge(acc_free[Q_DT % 2][t], Q_DT // 2 + 1)
                mm = pe.transpose(tb[0][:, rows(t)], pj[:, t, 0:P], ident[:])
            mm.then_inc(dk_tr, 1)
            pe.wait_ge(dtv_done, 1)
            with pe.Fori(0, 2) as j:
                for i in range(2):
                    wide(Pos(Q_BC + i, 2, j), Pos(S_BC + 8 * i, 16, j))
                    turn_pj(Pos(Q_BC + i, 2, j))
            def turn_cols(k):
                if k == 2:
                    pe.wait_ge(dt_vec, 13)
                    for t in range(TT):
                        pe.transpose(tb[0][:, rows(t)], dtw[:, 3, rows(t)], ident[:])
                    for t in range(TT):
                        pe.transpose(tb[0][:, (2 + t) * P:(3 + t) * P], dtw[:, 2, rows(t)], ident[:])
                    pe.transpose(tb[1][:, 0:P], dtw[:, 4, 0:P], ident[:])
                    pe.transpose(tb[1][:, P:2 * P], dtw[:, 4, P:2 * P], ident[:]).then_inc(col_tr, 1)
            wide(Pos(Q_P0), Pos(S_P0), turn_cols)
            pe.wait_ge(col_done, 2)
            wide(Pos(Q_P0 + 1), Pos(S_P0 + 8), with_z(Pos(0), None, Pos(Q_P0)))
            wide(Pos(Q_P1), Pos(S_P1), lambda k: chain(Pos(0), 4 + k))
            wide(Pos(Q_P1 + 1), Pos(S_P1 + 8), with_z(Pos(1), Pos(0), Pos(Q_P1)))
            with pe.Fori(0, 3) as c:
                q, s = Pos(Q_SSD, 8, c), Pos(S_SSD, 48, c)
                ge, go = Pos(2, 2, c), Pos(3, 2, c)
                gl = Pos(1, 2, c)
                wide(q, s, lambda k: chain(gl, 4 + k))
                wide(q + 1, s + 8, with_z(ge, gl, q))
                pe.wait_ge(gy_lo, ge.times(4).n)
                for n in range(4):
                    down(q + (2 + n), s + (16 + 4 * n), lambda k: chain(ge, 4 + k), n=n)
                wide(q + 6, s + 32)
                wide(q + 7, s + 40, with_z(go, ge, q + 6))
            g7 = Pos(7)
            pe.wait_ge(gy_lo, 4 * 7)
            for half in range(2):
                if half == 1:
                    turn_gy(g7)
                    pe.wait_ge(gy_lo, 4 * 8)
                for n in range(4):
                    q, s = Pos(Q_D3 + 4 * half + n), Pos(S_D3 + 8 * half + 2 * n)
                    down(q, s, (lambda k: chain(g7, 4 + k // 2) if k in (1, 3, 5) else None) if half == 0 else none,
                         range(4 * half, 4 * half + 4), n)

            def mlp_chunk(q, s, u, turning=None):
                if turning is None:
                    wide(q, s)
                else:
                    i, first = turning
                    wide_turning(q, s, first, lambda t, j: pe.wait_ge(x_norm[t], 4 * i + j + 1))
                wide(q + 1, s + 8, lambda k: turn_h(u, k) if k < TT else None)
                for t in range(TT):
                    pe.wait_ge(h_lo[t], (u + 1).n)
                    products(hT, range(0, 4), t, q + 2, s + 16, True, False)
                    turn_h(u + 1, t)
                for t in range(TT):
                    pe.wait_ge(h_lo[t], (u + 2).n)
                    products(hT, range(4, 8), t, q + 2, s + 18, False, True)
                for n in range(1, 4):
                    down(q + (2 + n), s + (16 + 4 * n))

            def mlp(q0, s0, layer, i, first):
                u0 = 2 * CHUNKS * layer
                mlp_chunk(Pos(q0), Pos(s0), Pos(u0), (i, first))
                with pe.Fori(0, CHUNKS - 1) as c:
                    mlp_chunk(Pos(q0 + 6, 6, c), Pos(s0 + 32, 32, c), Pos(u0 + 2, 2, c))

            mlp(Q_M0, S_M0, 0, 0, 8)

            def pool_x(g):
                for t in range(TT):
                    pe.wait_ge(x_norm[t], 4 + g + 1)
                halo = WINDOWS[-1] // 2
                for u in (2 * g, 2 * g + 1):
                    pe.wait_ge(tr_lo, 16 + u - 1)
                    for k in range(2):
                        ch = 2 * u + k
                        lhs = [x[:, t, ch * P:(ch + 1) * P] for t in range(TT)]
                        col = k * T
                        pe.matmul(tb[u % 2][:, col:col + P + halo], lhs[0], bands[:, g, 0, 0:P + halo],
                                  start=True, stop=False)
                        pe.matmul(tb[u % 2][:, col + P - halo:col + P + halo], lhs[1],
                                  bands[:, g, 1, P - halo:P + halo], start=False, stop=False)
                        mm = pe.matmul(tb[u % 2][:, col + P + halo:col + T], lhs[1], bands[:, g, 1, P + halo:T],
                                       start=False, stop=True)
                    mm.then_inc(tr_done, 1)

            def pool_products(g):
                pe.wait_ge(tr_lo, 16 + 2 * g + 2)
                for t in range(TT):
                    products(xT, range(4 * g, 4 * g + 4), t, Pos(Q_POOL + g), Pos(S_POOL + 2 * g), True, True)

            pe.wait_ge(bands_in, 16)
            for t in range(TT):
                pe.wait_ge(h_lo[t], 2 * CHUNKS)
            pool_x(0)
            for g in range(1, 4):
                pool_x(g)
                pool_products(g - 1)
            pool_products(3)
            mlp(Q_M1, S_M1, 1, 2, 24)

        @block.scalar
        def _(act):
            def split_hi(s):
                width = P if s.loop is None and s.base < S_BC else NB
                r = s.slot(RAW)
                act.wait_ge(raw_in[r], Pos(16 * (s.base // RAW + 1), 16 * s.step // RAW, s.loop).n)
                wait(act, w_used, s + (1 - RING))
                act.copy(whi[:, s.slot(RING), :, 0:width], raw[:, r, :, 0:width]).then_inc(hi_ready, 1)

            def none(k):
                pass

            def blocks(s, n, subs, after=none, ends=False, early=False):
                for b in range(n):
                    for i in range(subs):
                        if not (early and b == 0) and (not ends or (s + (subs * b + 4 + i)).base < S_END):
                            split_hi(s + (subs * b + 4 + i))
                    for t in range(TT):
                        after(2 * b + t)

            def full(q, t, s_end):
                if t == 0:
                    act.wait_ge(acc_full[q.slot(2)], q.half().n)
                else:
                    act.wait_ge(w_used, s_end.n)

            def out_of_psum(q, t, s_end, dst, func, width=NB):
                full(q, t, s_end)
                act.activation(dst, acc[q.slot(2)][t][:, 0:width], func).then_inc(acc_free[q.slot(2)][t], 1)

            def hi_x(first, t):
                for i in range(4):
                    u = first + 4 * t + i
                    act.wait_ge(tr_done, u + 1)
                    act.copy(xT[0][:, CT * i:CT * (i + 1), t * P:(t + 1) * P],
                             tb[u % 2][:].rearrange("p (k n) -> p k n", k=CT)).then_inc(tr_hi, 1)

            def pj_evac(q, s_end, t):
                out_of_psum(q, t, s_end, pj[:, t, :], ACT.Copy)

            def cvin_fill(k):
                act.wait_ge(cv_tr, (k + 1).n)
                for t in range(TT):
                    act.copy(cvin[:, :, PAD + t * P:PAD + (t + 1) * P],
                             tb[t][:].rearrange("p (j n) -> p j n", j=CT)).then_inc(cvin_full, 1)

            def silu_cv(k, dst):
                act.wait_ge(tap_done, (k + 1).times(TAPS * CT).n)
                act.activation(dst, cv[:], ACT.Silu).then_inc(cv_silu, 1)

            def decay(g, u):
                act.wait_ge(e_min, (g.times(4) + (u + 1)).n)
                act.activation(e1[:], e1[:], ACT.Exp).then_inc(e_exp, 1)

            def state_out(g, t):
                act.wait_ge(st_done, (g.times(2) + (t + 1)).n)
                act.copy(st[:, t, :], sbk[1][:]).then_inc(st_out, 1)

            def gy_high(g):
                act.wait_ge(gy_tr, (g + 1).n)
                for k in range(CT):
                    w = normw[:, bass.ds(g.times(CT).n + k, 1)]
                    act.activation(hT[0][:, CT * g.slot(2) + k, :], sbk[k // 2][:, (k % 2) * T:(k % 2 + 1) * T],
                                   ACT.Copy, scale=w).then_inc(gy_hi, 1)

            def chain(g, k, zq=None, z_end=None):
                if k == 0:
                    wait(act, e_sub, g.times(8))
                    cvin_fill(g + 4)
                elif k == 1:
                    silu_cv(g + 4, cv[:])
                    act.wait_ge(sc_done, (g + 1).n)
                    act.copy(btok[:].rearrange("p t n -> p (t n)"), sbk[1][:, 0:T]).then_inc(btok_done, 1)
                elif k == 2:
                    act.wait_ge(back_tr, (g + 1).n)
                    wait(act, yd_done, g.times(4))
                    wait(act, xw_done, g.times(2))
                    wait(act, gy_skip, g.times(2))
                    for t in range(TT):
                        act.copy(xs[:, t, :], tb[t][:]).then_inc(xs_out, 1)
                    decay(g, 0)
                elif k == 3:
                    wait(act, gated, g.times(2))
                    wait(act, sumsq, g.times(2))
                    for t in range(TT):
                        out_of_psum(zq, t, z_end, zs[:, t, :], ACT.Silu)
                    state_out(g, 0)
                    decay(g, 1)
                elif k == 4:
                    decay(g, 2)
                elif k == 5:
                    state_out(g, 1)
                    decay(g, 3)
                elif k == 7:
                    act.wait_ge(gated, (g.times(2) + 2).n)
                    for t in range(TT):
                        act.activation(zs[:, t, :], gy[:, t, :], ACT.Square,
                                       accum_out=ss[:, t, 0:1]).then_inc(sumsq, 1)
                    for t in range(TT):
                        act.wait_ge(sumsq, (g.times(2) + (t + 1)).n)
                        act.activation(ss[:, t, 1:2], ss[:, t, 0:1], ACT.Sqrt, bias=eps[:],
                                       scale=1.0 / NB).then_inc(rooted, 1)

            def xs_group(q, s, g, prior=None):
                def after(k):
                    if k >= 2:
                        if k == 2:
                            wait(act, off_done, g.times(2) + -1)
                        else:
                            wait(act, off_done, g.times(2))
                        pj_evac(q, s + 8, k - 2)
                    if prior is not None:
                        chain(prior, 4 + k)
                blocks(s, 2, 4, after)

            def z_group(q, s, g, before):
                def after(k):
                    if k == 0 and before is not None:
                        gy_high(before)
                    chain(g, k, q, s + 8)
                blocks(s, 2, 4, after)

            def dt_steps(k):
                if k == 0:
                    act.wait_ge(dt_vec, 1)
                    act.activation(dtw[:, 0, :], dtw[:, 0, :], ACT.Exp, scale=-1.0).then_inc(dt_act, 1)
                    act.activation(dtp[:, 2:3], dtp[:, 1:2], ACT.Exp).then_inc(dt_act, 1)
                    act.wait_ge(dt_vec, 4)
                    act.activation(dtw[:, 3, :], dtw[:, 1, :], ACT.Ln).then_inc(dt_act, 1)
                    act.wait_ge(f_ready, 4)
                    f, h = dtw[:, 3, :], P // 2
                    act.activation(dtw[0:h, 4, 0:P], f[0:h, 0:P], ACT.Exp, scale=-1.0,
                                   bias=f[0:h, P - 1:P]).then_inc(dt_act, 1)
                    act.activation(dtw[h:P, 4, 0:P], f[h:P, P:T], ACT.Exp, scale=-1.0,
                                   bias=f[h:P, P:P + 1]).then_inc(dt_act, 1)
                    act.activation(dtw[0:h, 4, P:T], f[0:h, P:T], ACT.Exp).then_inc(dt_act, 1)
                    act.activation(dtw[h:P, 4, P:T], f[h:P, 0:P], ACT.Exp).then_inc(dt_act, 1)
                elif k == 2:
                    act.wait_ge(col_tr, 1)
                    act.copy(cols[:, 0:4, :], tb[0][:].rearrange("p (k n) -> p k n", k=4)).then_inc(col_done, 1)
                    act.copy(cols[:, 4:6, :], tb[1][:, 0:T].rearrange("p (k n) -> p k n", k=2)).then_inc(col_done, 1)

            hi_x(0, 0)
            for i in range(4):
                split_hi(Pos(S_DT + i))
            def dt_out(k):
                if k == 0:
                    hi_x(0, 1)
                if k >= 2:
                    out_of_psum(Pos(Q_DT), k - 2, Pos(S_BC), pj[:, k - 2, 0:P], ACT.Copy, P)
            blocks(Pos(S_DT), 2, 4, dt_out)
            act.wait_ge(dk_tr, 1)
            act.wait_ge(const_in, 16 * 7)
            act.wait_ge(eps_set, 1)
            for i in range(4):
                split_hi(Pos(S_BC + 4 + i))
            with act.Fori(0, 2) as j:
                for i in range(2):
                    k, s = Pos(i, 2, j), Pos(S_BC + 8 * i, 16, j)
                    def bc_out(n):
                        if n >= 2:
                            out_of_psum(Pos(Q_BC + i, 2, j), n - 2, s + 8, pj[:, n - 2, :], ACT.Copy)
                        if n == 3:
                            cvin_fill(k)
                            for m in range(4):
                                split_hi(s + (12 + m))
                            silu_cv(k, area_a[:, bass.ds(j * (NG * T) + i * (CT * T), CT * T)].rearrange(
                                "p (g t) -> p g t", g=CT))
                    blocks(s, 2, 4, bc_out, early=True)

            def first_xs(k):
                dt_steps(k)
                if k >= 2:
                    pj_evac(Pos(Q_P0), Pos(S_P0 + 8), k - 2)
            blocks(Pos(S_P0), 2, 4, first_xs, early=True)
            z_group(Pos(Q_P0 + 1), Pos(S_P0 + 8), Pos(0), None)
            xs_group(Pos(Q_P1), Pos(S_P1), Pos(1), Pos(0))
            z_group(Pos(Q_P1 + 1), Pos(S_P1 + 8), Pos(1), Pos(0))
            with act.Fori(0, 3) as c:
                q, s = Pos(Q_SSD, 8, c), Pos(S_SSD, 48, c)
                gl, ge, go = Pos(1, 2, c), Pos(2, 2, c), Pos(3, 2, c)
                xs_group(q, s, ge, gl)
                z_group(q + 1, s + 8, ge, gl)
                blocks(s + 16, 4, 4, lambda k: chain(ge, 4 + k))
                xs_group(q + 6, s + 32, go)
                z_group(q + 7, s + 40, go, ge)
            blocks(Pos(S_D3), 4, 2, lambda k: chain(Pos(7), {1: 4, 3: 5, 5: 6, 6: 7}[k]) if k in (1, 3, 5, 6) else None)
            gy_high(Pos(7))
            blocks(Pos(S_D3 + 8), 4, 2)

            def root(i, t):
                act.wait_ge(ln_vec[t], 10 * i + 5)
                act.activation(mv[:, t, 2:3], mv[:, t, 1:2], ACT.Sqrt, bias=eps[:]).then_inc(ln_root[t], 1)

            def hidden(q, s_end, u, t):
                out_of_psum(q, t, s_end, hr[:, t, :], ACT.Relu)
                act.wait_ge(acc_free[q.slot(2)][t], (q.half() + 1).n)
                act.activation(hr[:, t, :], hr[:, t, :], ACT.Square).then_inc(squared, 1)

            def hi_h(u, t):
                act.wait_ge(h_tr[t], (u + 1).n)
                kt = CT * u.slot(2)
                act.copy(hT[0][:, kt:kt + CT, t * P:(t + 1) * P],
                         tb[t][:].rearrange("p (k n) -> p k n", k=CT)).then_inc(h_hi[t], 1)

            def mlp_chunk(q, s, u, first=None, ends=False):
                def up(k):
                    if k == 0 and first is not None:
                        hi_x(first, 1)
                    if k >= 2:
                        hidden(q, s + 8, u, k - 2)
                blocks(s, 2, 4, up)
                def second(k):
                    if k < 2:
                        hi_h(u, k)
                    else:
                        hidden(q + 1, s + 16, u + 1, k - 2)
                blocks(s + 8, 2, 4, second)
                for t in range(TT):
                    for i in range(2):
                        split_hi(s + (20 + 2 * t + i))
                    hi_h(u + 1, t)
                blocks(s + 20, 3, 4, none, ends)

            def mlp(q0, s0, layer, i, first):
                root(i, 0)
                hi_x(first, 0)
                root(i, 1)
                u0, last = 2 * CHUNKS * layer, CHUNKS - 1
                mlp_chunk(Pos(q0), Pos(s0), Pos(u0), first)
                with act.Fori(0, CHUNKS - 2) as c:
                    mlp_chunk(Pos(q0 + 6, 6, c), Pos(s0 + 32, 32, c), Pos(u0 + 2, 2, c))
                mlp_chunk(Pos(q0 + 6 * last), Pos(s0 + 32 * last), Pos(u0 + 2 * last), ends=True)

            act.wait_ge(yd_done, 4 * NG)
            mlp(Q_M0, S_M0, 0, 0, 8)
            root(1, 0)
            root(1, 1)

            def hi_pool(g):
                for u in (2 * g, 2 * g + 1):
                    act.wait_ge(tr_done, 16 + u + 1)
                    act.copy(xT[0][:, 2 * u:2 * u + 2, :],
                             tb[u % 2][:].rearrange("p (k n) -> p k n", k=2)).then_inc(tr_hi, 1)
            hi_pool(0)
            hi_pool(1)
            blocks(Pos(S_POOL), 4, 2, lambda k: hi_pool(2 + k // 2) if k in (0, 2) else None)
            mlp(Q_M1, S_M1, 1, 2, 24)
            root(3, 0)
            root(3, 1)

        @block.vector
        def _(dve):
            def split_lo(s):
                width = P if s.loop is None and s.base < S_BC else NB
                r, slot = s.slot(RAW), s.slot(RING)
                dve.wait_ge(hi_ready, (s + 1).n)
                dve.tensor_tensor(wlo[:, slot, :, 0:width], raw[:, r, :, 0:width],
                                  whi[:, slot, :, 0:width].bitcast(F32), ALU.subtract).then_inc(lo_ready, 1)

            def none(k):
                pass

            def blocks(s, n, subs, after=none, ends=False):
                for b in range(n):
                    for i in range(subs):
                        if not ends or (s + (subs * b + 4 + i)).base < S_END:
                            split_lo(s + (subs * b + 4 + i))
                    for t in range(TT):
                        after(2 * b + t)

            def full(q, t, s_end):
                if t == 0:
                    dve.wait_ge(acc_full[q.slot(2)], q.half().n)
                else:
                    dve.wait_ge(w_used, s_end.n)

            def lo_of(dst, src, hi, done):
                dve.tensor_tensor(dst, src, hi.bitcast(F32), ALU.subtract).then_inc(done, 1)

            def lo_x(first, t, i):
                u = first + 4 * t + i
                dve.wait_ge(tr_hi, u + 1)
                part = (slice(None), slice(CT * i, CT * (i + 1)), slice(t * P, (t + 1) * P))
                lo_of(xT[1][part], tb[u % 2][:].rearrange("p (k n) -> p k n", k=CT), xT[0][part], tr_lo)

            def add_x(q, s_end, t, n, first=False, norm=None):
                full(q, t, s_end)
                cs, free = slice(n * NB, (n + 1) * NB), acc_free[q.slot(2)][t]
                if first:
                    dve.scalar_tensor_tensor(x[:, t, cs], x[:, t, cs], ALPHA, acc[q.slot(2)][t][:],
                                             ALU.mult, ALU.add).then_inc(free, 1)
                else:
                    dve.tensor_tensor(x[:, t, cs], x[:, t, cs], acc[q.slot(2)][t][:], ALU.add).then_inc(free, 1)
                if norm is not None:
                    dve.wait_ge(free, (q.half() + 1).n)
                    stats(t, n)

            def stats(t, n):
                dve.bn_stats(bst[:, t, n, :], x[:, t, n * NB:(n + 1) * NB]).then_inc(ln_vec[t], 1)

            def down(q, s, n, after=none, subs=4, first=False, norm=None, ends=False):
                def both(t):
                    add_x(q, s + subs, t, n, first, norm)
                    after(2 * n + t)
                blocks(s, 1, subs, both, ends)

            def set_pads():
                dve.memset(cvin[:, :, 0:PAD], 0.0).then_inc(pad_set, 1)
                dve.memset(cvin[:, :, PAD + T:PAD + T + PAD], 0.0).then_inc(pad_set, 1)

            def convolve(k, ch):
                dve.wait_ge(cvin_full, (k.times(2) + 2).n)
                n = k.times(TAPS * CT)
                for tap in range(TAPS):
                    for j in range(CT):
                        w = convw[:, bass.ds(ch.n + j, 1), tap]
                        src = cvin[:, j, tap:tap + T]
                        if tap == 0:
                            dve.tensor_scalar(cv[:, j, :], src, w, convb[:, bass.ds(ch.n + j, 1)],
                                              ALU.mult, ALU.add).then_inc(tap_done, 1)
                        else:
                            dve.wait_ge(tap_done, (n + (CT * (tap - 1) + j + 1)).n)
                            dve.scalar_tensor_tensor(cv[:, j, :], src, w, cv[:, j, :],
                                                     ALU.mult, ALU.add).then_inc(tap_done, 1)

            def gy_low(g):
                for k in range(CT):
                    dve.wait_ge(gy_hi, (g.times(CT) + 2 * (k // 2 + 1)).n)
                    kt = CT * g.slot(2) + k
                    w = normw[:, bass.ds(g.times(CT).n + k, 1)]
                    dve.scalar_tensor_tensor(hT[1][:, kt, :], sbk[k // 2][:, (k % 2) * T:(k % 2 + 1) * T], w,
                                             hT[0][:, kt, :].bitcast(F32), ALU.mult, ALU.subtract).then_inc(gy_lo, 1)

            def heads(buf, g, first):
                return buf[:, bass.ds(g.times(HPG).n + first, 4)]

            def unit(g, u):
                t, hh = u // 2, u % 2
                dve.wait_ge(fbc_in[u % 2], (g.times(64) + 32 * (u // 2 + 1)).n)
                wait(dve, yd_done, g.times(4) + u)
                for d, dst in ((0, e1), (1, e2)):
                    col = heads(cols[:, t, :], g, d * NH + 4 * hh)
                    dve.tensor_tensor(dst[:], fbc[u % 2][:, d], col.unsqueeze(2).to_broadcast([P, 4, P]),
                                      ALU.subtract).then_inc(e_sub, 1)
                dve.wait_ge(e_sub, (g.times(8) + 2 * (u + 1)).n)
                dve.tensor_tensor(e1[:], e1[:], e2[:], ALU.min).then_inc(e_min, 1)
                dve.wait_ge(gd_done, (g.times(4) + (u + 1)).n)
                dve.wait_ge(e_exp, (g.times(4) + (u + 1)).n)
                dve.tensor_tensor(mx[:], e1[:], gd[:, 0], ALU.mult).then_inc(m_done, 1)

            def add_carried(g, t):
                o = 1 - t
                dve.wait_ge(off_done, (g.times(2) + (t + 1)).n)
                for h in range(HPG):
                    cs = slice(h * HD, (h + 1) * HD)
                    ef = cols[:, 5, bass.ds(g.times(HPG).n + t * NH + h, 1)]
                    dve.scalar_tensor_tensor(gy[:, o, cs], sbk[1][:, cs], ef, gy[:, o, cs],
                                             ALU.mult, ALU.add).then_inc(gy_off, 1)

            def chain(g, k, zq=None):
                if k == 0:
                    wait(dve, gy_tr, g)
                    wait(dve, e_sub, g.times(8))
                    set_pads()
                    dve.wait_ge(pad_set, (g.times(2) + 4).n)
                    convolve(g + 4, g.times(CT))
                elif k == 1:
                    dve.wait_ge(sc_done, (g + 1).n)
                    for t in range(TT):
                        for d in range(2):
                            dve.tensor_tensor(gt[:, t, d, :], sbk[0][:, t * P:(t + 1) * P], masks[:, d, :],
                                              ALU.mult).then_inc(gt_done, 1)
                elif k == 2:
                    unit(g, 0)
                elif k == 3:
                    unit(g, 1)
                elif k == 4:
                    dve.wait_ge(yd_done, (g.times(4) + 2).n)
                    dve.wait_ge(gy_skip, (g.times(2) + 2).n)
                    dve.tensor_tensor(gy[:, 0, :], gy[:, 0, :], sbk[0][:], ALU.add).then_inc(gy_yd, 1)
                    add_carried(g, 0)
                    unit(g, 2)
                elif k == 5:
                    unit(g, 3)
                elif k == 6:
                    dve.wait_ge(yd_done, (g.times(4) + 4).n)
                    dve.wait_ge(gy_off, (g.times(16) + 8).n)
                    dve.tensor_tensor(gy[:, 1, :], gy[:, 1, :], sbk[0][:], ALU.add).then_inc(gy_yd, 1)
                    dve.wait_ge(gy_yd, (g.times(2) + 1).n)
                    add_carried(g, 1)
                    dve.wait_ge(gy_off, (g.times(16) + 16).n)
                    dve.wait_ge(gy_yd, (g.times(2) + 2).n)
                    for t in range(TT):
                        dve.wait_ge(acc_free[zq.slot(2)][t], (zq.half() + 1).n)
                        dve.tensor_tensor(gy[:, t, :], gy[:, t, :], zs[:, t, :], ALU.mult).then_inc(gated, 1)
                elif k == 7:
                    for t in range(TT):
                        dve.wait_ge(rooted, (g.times(2) + (t + 1)).n)
                        dve.reciprocal(ss[:, t, 2:3], ss[:, t, 1:2]).then_inc(inv_root, 1)
                    for t in range(TT):
                        dve.wait_ge(inv_root, (g.times(2) + (t + 1)).n)
                        dve.tensor_scalar(gy[:, t, :], gy[:, t, :], ss[:, t, 2:3], None, ALU.mult).then_inc(gy_done, 1)

            def z_group(s, g, before):
                def after(k):
                    if k == 0 and before is not None:
                        gy_low(before)
                    chain(g, k)
                blocks(s, 2, 4, after)

            def dt_steps(k):
                if k != 0:
                    return
                h = P // 2
                dve.scalar_tensor_tensor(dtw[:, 0, :], dtv, -1.0, dtv, ALU.mult, ALU.max).then_inc(dt_vec, 1)
                dve.memset(dtw[:, 5, :], 1.0).then_inc(dt_vec, 1)
                dve.tensor_scalar(dtw[:, 2, :], dtv, 0.0, None, ALU.max).then_inc(dt_vec, 1)
                dve.wait_ge(dt_act, 1)
                dve.tensor_scalar(dtw[:, 1, :], dtw[:, 0, :], 1.0, None, ALU.add).then_inc(dt_vec, 1)
                dve.wait_ge(dt_vec, 4)
                dve.tensor_scalar(dtw[:, 4, :], dtw[:, 1, :], -1.0, TINY, ALU.add, ALU.add).then_inc(dt_vec, 1)
                dve.wait_ge(dt_vec, 5)
                dve.reciprocal(dtw[:, 4, :], dtw[:, 4, :]).then_inc(dt_vec, 1)
                dve.wait_ge(dt_vec, 6)
                dve.wait_ge(dt_act, 3)
                dve.scalar_tensor_tensor(dtw[:, 3, :], dtw[:, 3, :], TINY, dtw[:, 4, :], ALU.add, ALU.mult).then_inc(dt_vec, 1)
                dve.wait_ge(dt_vec, 7)
                dve.tensor_tensor(dtw[:, 3, :], dtw[:, 3, :], dtw[:, 0, :], ALU.mult).then_inc(dt_vec, 1)
                dve.wait_ge(dt_vec, 8)
                dve.tensor_tensor(dtw[:, 2, :], dtw[:, 2, :], dtw[:, 3, :], ALU.add).then_inc(dt_vec, 1)
                dve.tensor_scalar(dtp[:, 3:4], dtp[:, 2:3], -1.0, None, ALU.mult).then_inc(dt_vec, 1)
                dve.wait_ge(dt_vec, 10)
                dve.tensor_scalar(dtw[:, 0, :], dtw[:, 2, :], dtp[:, 3:4], None, ALU.mult).then_inc(dt_vec, 1)
                dve.wait_ge(dt_vec, 11)
                for t in range(TT):
                    for fwd in (True, False):
                        part = slice(0, h) if fwd else slice(h, P)
                        ts = slice(t * P, (t + 1) * P)
                        one, a_, f = dtw[part, 5, ts], dtw[part, 0, ts], dtw[part, 3, ts]
                        if not fwd:
                            a_, f = a_[:, ::-1], f[:, ::-1]
                        dve.tensor_tensor_scan(f, one, a_, 0.0, ALU.mult, ALU.add).then_inc(f_ready, 1)
                dve.wait_ge(dt_act, 7)
                dve.tensor_tensor(dtw[0:h, 4, 0:P], dtw[0:h, 4, 0:P], dtw[0:h, 2, 0:P], ALU.mult).then_inc(dt_vec, 1)
                dve.tensor_tensor(dtw[h:P, 4, 0:P], dtw[h:P, 4, 0:P], dtw[h:P, 2, P:T], ALU.mult).then_inc(dt_vec, 1)

            def moments(i, t):
                dve.wait_ge(ln_vec[t], 10 * i + 4)
                dve.bn_aggr(mv[:, t, 0:2], bst[:, t].rearrange("p j n -> p (j n)")).then_inc(ln_vec[t], 1)
                dve.wait_ge(gb_in, 32 * (i + 1))
                dve.wait_ge(ln_vec[t], 10 * i + 5)
                centre(t, 0)
                dve.wait_ge(ln_root[t], i + 1)
                dve.reciprocal(mv[:, t, 3:4], mv[:, t, 2:3]).then_inc(ln_vec[t], 1)

            def centre(t, j):
                cs = slice(j * NB, (j + 1) * NB)
                dve.scalar_tensor_tensor(x[:, t, cs], x[:, t, cs], mv[:, t, 0:1], gb[:, 0, cs],
                                         ALU.subtract, ALU.mult).then_inc(ln_vec[t], 1)

            def normed(i, t, j):
                if j > 0:
                    centre(t, j)
                cs = slice(j * NB, (j + 1) * NB)
                dve.wait_ge(ln_vec[t], 10 * i + 7 + j)
                dve.scalar_tensor_tensor(x[:, t, cs], x[:, t, cs], mv[:, t, 3:4], gb[:, 1, cs],
                                         ALU.mult, ALU.add).then_inc(x_norm[t], 1)

            def lo_h(u, t):
                dve.wait_ge(h_hi[t], (u + 1).n)
                kt = CT * u.slot(2)
                part = (slice(None), slice(kt, kt + CT), slice(t * P, (t + 1) * P))
                lo_of(hT[1][part], tb[t][:].rearrange("p (k n) -> p k n", k=CT), hT[0][part], h_lo[t])

            def mlp_chunk(q, s, u, first=None, norm=None):
                def up(k):
                    if k == 0 and first is not None:
                        for i in range(4):
                            lo_x(first, 1, i)
                blocks(s, 2, 4, up)
                blocks(s + 8, 2, 4, lambda k: lo_h(u, k) if k < 2 else None)
                for t in range(TT):
                    for i in range(2):
                        split_lo(s + (20 + 2 * t + i))
                    lo_h(u + 1, t)
                for t in range(TT):
                    add_x(q + 2, s + 20, t, 0, first is not None, norm)
                for n in range(1, 4):
                    down(q + (2 + n), s + (16 + 4 * n), n, first=first is not None, norm=norm, ends=norm == 3)

            def mlp(q0, s0, layer, i, first):
                moments(i, 0)
                for j in range(4):
                    normed(i, 0, j)
                    if j >= 2:
                        lo_x(first, 0, j - 2)
                moments(i, 1)
                lo_x(first, 0, 2)
                lo_x(first, 0, 3)
                for j in range(4):
                    normed(i, 1, j)
                u0, last = 2 * CHUNKS * layer, CHUNKS - 1
                mlp_chunk(Pos(q0), Pos(s0), Pos(u0), first)
                with dve.Fori(0, CHUNKS - 2) as c:
                    mlp_chunk(Pos(q0 + 6, 6, c), Pos(s0 + 32, 32, c), Pos(u0 + 2, 2, c))
                mlp_chunk(Pos(q0 + 6 * last), Pos(s0 + 32 * last), Pos(u0 + 2 * last), norm=i + 1)

            dve.memset(eps[:], EPS).then_inc(eps_set, 1)
            for pair in range(2):
                for t in range(TT):
                    dve.sem_inc(acc_free[pair][t], 1)
            for i in range(4):
                lo_x(0, 0, i)
            for i in range(4):
                split_lo(Pos(S_DT + i))
            def second_tile(k):
                if k == 0:
                    for i in range(4):
                        lo_x(0, 1, i)
            blocks(Pos(S_DT), 2, 4, second_tile)
            dve.wait_ge(const_in, 16 * 7)
            dve.wait_ge(dk_tr, 1)
            dve.tensor_scalar(dtv, tb[0][:, 0:T], dtp[:, 0:1], None, ALU.add).then_inc(dtv_done, 1)
            set_pads()
            dve.wait_ge(pad_set, 2)
            with dve.Fori(0, 2) as j:
                for i in range(2):
                    blocks(Pos(S_BC + 8 * i, 16, j), 2, 4,
                           lambda n: convolve(Pos(i, 2, j), Pos(CH_B + CT * i, 2 * CT, j)) if n == 3 else None)
            dve.wait_ge(dtv_done, 1)
            blocks(Pos(S_P0), 2, 4, dt_steps)
            dve.wait_ge(col_done, 2)
            z_group(Pos(S_P0 + 8), Pos(0), None)
            blocks(Pos(S_P1), 2, 4, lambda k: chain(Pos(0), 4 + k, Pos(Q_P0 + 1)))
            z_group(Pos(S_P1 + 8), Pos(1), Pos(0))
            dve.wait_ge(x_scaled, 1)
            with dve.Fori(0, 3) as c:
                q, s = Pos(Q_SSD, 8, c), Pos(S_SSD, 48, c)
                gl, ge, go = Pos(1, 2, c), Pos(2, 2, c), Pos(3, 2, c)
                blocks(s, 2, 4, lambda k: chain(gl, 4 + k, q + -1))
                z_group(s + 8, ge, gl)
                for n in range(4):
                    down(q + (2 + n), s + (16 + 4 * n), n, lambda k: chain(ge, 4 + k, q + 1))
                blocks(s + 32, 2, 4)
                z_group(s + 40, go, ge)
            for n in range(4):
                down(Pos(Q_D3 + n), Pos(S_D3 + 2 * n), n,
                     lambda k: chain(Pos(7), {1: 4, 3: 5, 5: 6, 6: 7}[k], Pos(Q_D3 - 1)) if k in (1, 3, 5, 6) else None,
                     2)
            gy_low(Pos(7))
            for n in range(4):
                down(Pos(Q_D3 + 4 + n), Pos(S_D3 + 8 + 2 * n), n, none, 2, norm=0)

            mlp(Q_M0, S_M0, 0, 0, 8)

            def lo_pool(g):
                for u in (2 * g, 2 * g + 1):
                    dve.wait_ge(tr_hi, 16 + u + 1)
                    lo_of(xT[1][:, 2 * u:2 * u + 2, :], tb[u % 2][:].rearrange("p (k n) -> p k n", k=2),
                          xT[0][:, 2 * u:2 * u + 2, :], tr_lo)

            def pool_residual(g):
                cs = slice(g * NB, (g + 1) * NB)
                for t in range(TT):
                    dve.scalar_tensor_tensor(x[:, t, cs], x[:, t, cs], ALPHA, psc[:, 1, cs],
                                             ALU.mult, ALU.add).then_inc(pool_bias, 1)

            dve.wait_ge(psc_in, 32)
            dve.wait_ge(bias_scaled, 1)
            moments(1, 0)
            moments(1, 1)
            for g in range(4):
                for t in range(TT):
                    normed(1, t, g)
                if g % 2 == 1:
                    lo_pool(g // 2)
                    pool_residual(g // 2)
            for g in range(4):
                q, s = Pos(Q_POOL + g), Pos(S_POOL + 2 * g)
                cs = slice(g * NB, (g + 1) * NB)
                def pooled(t):
                    if t == 0 and g < 2:
                        lo_pool(g + 2)
                        pool_residual(g + 2)
                    full(q, t, s + 2)
                    wait(dve, pool_added, Pos(2 * g + t))
                    dve.tensor_tensor(ptmp, acc[q.slot(2)][t][:], psc[:, 0, cs], ALU.mult).then_inc(
                        acc_free[q.slot(2)][t], 1)
                    dve.wait_ge(pool_bias, 2 * (g + 1))
                    dve.wait_ge(acc_free[q.slot(2)][t], (q.half() + 1).n)
                    dve.tensor_tensor(x[:, t, cs], x[:, t, cs], ptmp, ALU.add).then_inc(pool_added, 1)
                    dve.wait_ge(pool_added, 2 * g + t + 1)
                    stats(t, g)
                blocks(s, 1, 2, pooled)
            mlp(Q_M1, S_M1, 1, 2, 24)
            for t in range(TT):
                moments(3, t)
                for j in range(4):
                    normed(3, t, j)

        @block.gpsimd
        def _(pool):
            for dst, name in ((masks, "masks"), (convw, "conv_w"), (convb, "conv_b"),
                              (normw, "norm_w")):
                pool.dma_start(dst[:], a[name]).then_inc(const_in, 16)
            pool.dma_start(dtp[:, 0:1], a["dt_bias"]).then_inc(const_in, 16)
            pool.dma_start(dtp[:, 1:2], a["a_log"]).then_inc(const_in, 16)
            pool.dma_start(dskip[:], a["d_skip"].partition_broadcast(P)).then_inc(const_in, 16)

            def load_gb(i):
                for m, name in enumerate(("ln_g", "ln_b")):
                    pool.dma_start(gb[:, m, :], a[name][i].partition_broadcast(P)).then_inc(gb_in, 16)

            def load_f(g, u):
                t, hh = u // 2, u % 2
                for d in range(2):
                    src = f_rows[d, bass.ds(g.times(HPG).n + 4 * hh, 4), t * P:(t + 1) * P]
                    pool.dma_start(fbc[u % 2][:, d], src.partition_broadcast(P)).then_inc(fbc_in[u % 2], 16)

            def weigh(g, t):
                pool.wait_ge(xs_out, (g.times(2) + (t + 1)).n)
                wait(pool, st_done, g.times(2) + t)
                w = cols[:, 4, bass.ds(g.times(HPG).n + t * NH, HPG)].unsqueeze(2).to_broadcast([P, HPG, HD])
                pool.tensor_tensor(xw[:].rearrange("p (h c) -> p h c", h=HPG),
                                   xs[:, t, :].rearrange("p (h c) -> p h c", h=HPG), w, ALU.mult).then_inc(xw_done, 1)

            def weigh_scores(g, u):
                t, hh = u // 2, u % 2
                pool.wait_ge(gt_done, (g.times(4) + 4).n)
                wait(pool, m_done, g.times(4) + u)
                for d in range(2):
                    w = cols[:, 2 + t, bass.ds(g.times(HPG).n + d * NH + 4 * hh, 4)]
                    pool.tensor_tensor(gd[:, d], gt[:, t, d, :].unsqueeze(1).to_broadcast([P, 4, P]),
                                       w.unsqueeze(2).to_broadcast([P, 4, P]), ALU.mult).then_inc(gd_part, 1)
                pool.wait_ge(gd_part, (g.times(8) + 2 * (u + 1)).n)
                pool.tensor_tensor(gd[:, 0], gd[:, 0], gd[:, 1], ALU.add).then_inc(gd_done, 1)

            def skip(g):
                pool.wait_ge(xs_out, (g.times(2) + 2).n)
                for t in range(TT):
                    w = dskip[:, bass.ds(g.times(HPG).n, HPG)].unsqueeze(2).to_broadcast([P, HPG, HD])
                    pool.tensor_tensor(gy[:, t, :].rearrange("p (h c) -> p h c", h=HPG),
                                       xs[:, t, :].rearrange("p (h c) -> p h c", h=HPG), w, ALU.mult).then_inc(gy_skip, 1)

            def head_group(g):
                wait(pool, off_done, g.times(2))
                for m in range(2):
                    src = area_a[:, bass.ds(g.times(T).n + m * (NG * T), T)]
                    if m == 1:
                        pool.tensor_copy(cur[:, m, :], src).then_inc(cur_done, 1)
                    else:
                        pool.tensor_copy(cur[:, m, :], src).then_inc(cur_half, 1)
                pool.wait_ge(tap_done, (g + 5).times(TAPS * CT).n)
                load_f(g, 0)
                weigh_scores(g, 0)
                load_f(g, 1)
                weigh(g, 0)
                skip(g)
                weigh_scores(g, 1)
                pool.wait_ge(e_sub, (g.times(8) + 2).n)
                load_f(g, 2)
                weigh(g, 1)
                weigh_scores(g, 2)
                pool.wait_ge(e_sub, (g.times(8) + 4).n)
                load_f(g, 3)
                weigh_scores(g, 3)

            pool.wait_ge(tr_done, 8)
            pool.tensor_scalar(x[:], x[:], ALPHA, None, ALU.mult).then_inc(x_scaled, 1)
            pool.wait_ge(f_ready, 4)
            pool.dma_start(fscr, dtw[:, 3, :]).then_inc(f_saved, 16)
            pool.wait_ge(f_saved, 16)
            pool.wait_ge(cv_silu, 4)
            pool.wait_ge(col_done, 2)
            head_group(Pos(0))
            with pool.Fori(0, NG - 1) as c:
                head_group(Pos(1, 1, c))
            pool.wait_ge(cur_done, NG)
            load_gb(0)
            pool.wait_ge(e_sub, 8 * NG)
            pool.dma_start(bands[:], a["bands"]).then_inc(bands_in, 16)
            pool.wait_ge(gy_tr, NG)
            for m, name in enumerate(("pool_scale", "pool_b")):
                pool.dma_start(psc[:, m, :], a[name].partition_broadcast(P)).then_inc(psc_in, 16)
            pool.wait_ge(psc_in, 32)
            pool.tensor_tensor(psc[:, 1, :], psc[:, 1, :], psc[:, 0, :], ALU.mult).then_inc(bias_scaled, 1)
            for i in range(1, 4):
                for t in range(TT):
                    pool.wait_ge(x_norm[t], 4 * i)
                load_gb(i)


def kernel(**inputs):
    import numpy as np
    import concourse.bacc as bacc
    from concourse.bass_utils import run_bass_kernel_spmd

    s, l = np.arange(P)[:, None], np.arange(P)[None, :]
    masks = np.stack([s <= l, s >= l], axis=1).astype(np.float32)
    bands = np.zeros((T, len(WINDOWS), T), np.float32)
    for i, w in enumerate(WINDOWS):
        for t in range(T):
            lo, hi = max(t - w // 2, 0), min(t - w // 2 + w, T)
            bands[lo:hi, i, t] = np.float32(1.0) / np.float32(hi - lo)
            bands[t, i, t] -= 1.0
    bands = bands.reshape(TT, P, len(WINDOWS), T).transpose(1, 2, 0, 3)

    def by_channel(v):
        return np.asarray(v).reshape(-1, P).T

    d = {k: np.asarray(v) for k, v in inputs.items()}
    arrays = {
        "x": d["x"][0], "in_proj": d["ssd_in_proj"][0], "out_proj": d["ssd_out_proj"][0],
        "pool_w": d["pool_w"][0], "w1": d["mlp_w1"], "w2": d["mlp_w2"],
        "conv_w": d["ssd_conv_w"][0, :, 0, :].reshape(TAPS, -1, P).transpose(2, 1, 0),
        "conv_b": by_channel(d["ssd_conv_b"][0]), "norm_w": by_channel(d["ssd_norm_w"][0]),
        "dt_bias": d["ssd_dt_bias"][0].reshape(P, 1), "a_log": d["ssd_A_log"][0].reshape(P, 1),
        "d_skip": d["ssd_D"][0], "pool_scale": d["pool_scale"][0], "pool_b": d["pool_b"][0].reshape(DM),
        "ln_g": np.stack([d["ln_mix_g"][0], d["ln_ffn_g"][0], d["ln_mix_g"][1], d["ln_ffn_g"][1]]),
        "ln_b": np.stack([d["ln_mix_b"][0], d["ln_ffn_b"][0], d["ln_mix_b"][1], d["ln_ffn_b"][1]]),
        "ident": np.eye(P, dtype=np.float32), "masks": masks, "bands": bands,
    }
    arrays = {k: np.ascontiguousarray(v) for k, v in arrays.items()}
    nc = bacc.Bacc("TRN2", target_bir_lowering=False, num_devices=1)
    aps = {k: nc.dram_tensor(f"in_{k}", v.shape, mybir.dt.from_np(v.dtype), kind="ExternalInput").ap()
           for k, v in arrays.items()}
    out = nc.dram_tensor("out", (T, DM), F32, kind="ExternalOutput").ap()
    build(nc, aps, out)
    r = run_bass_kernel_spmd(nc, [{f"in_{k}": v for k, v in arrays.items()}], core_ids=[0])
    return r.results[0]["out"].reshape(1, T, DM)
```

```python
from contextlib import ExitStack

import concourse.bass as bass
from concourse import mybir

F32 = mybir.dt.float32
F32R = mybir.dt.float32r
ALU = mybir.AluOpType
ACT = mybir.ActivationFunctionType

P = 128
DM = 2048
T = 256
TT = T // P
DEPTH = 2
DI = 2 * DM
HD = 64
NH = DI // HD
NG = 8
HPG = NH // NG
TAPS = 5
PAD = TAPS // 2
DFF = 4 * DM
NB = 512
KT = DM // P
CT = NB // P
XS0, B0, DT0 = DI, 2 * DI, 2 * DI + 2 * NG * P
CH_B = DI // P
CK = 8
CHUNKS = DFF // (CK * P)
WINDOWS = (2, 4, 8, 16)
ALPHA = (2.0 * DEPTH) ** 0.25
EPS = 1e-5
TINY = 1e-30
RING = 8
RAW = 4
SUBK = 2


class Pos:

    def __init__(self, base, step=0, loop=None):
        self.base, self.step, self.loop = base, step, loop

    def __add__(self, k):
        return Pos(self.base + k, self.step, self.loop)

    def times(self, k):
        return Pos(self.base * k, self.step * k, self.loop)

    def half(self):
        assert self.step % 2 == 0
        return Pos(self.base // 2, self.step // 2, self.loop)

    def slot(self, n):
        assert self.step % n == 0
        return self.base % n

    @property
    def n(self):
        return self.base if self.loop is None else self.loop * self.step + self.base


def wait(eng, sem, pos):
    if pos.loop is None and pos.base <= 0:
        return
    eng.wait_ge(sem, pos.n)


Q_DT, S_DT = 2, 0
Q_BC, S_BC = Q_DT + 1, 2
Q_P0, S_P0 = Q_BC + 4, S_BC + 32
Q_P1, S_P1 = Q_P0 + 2, S_P0 + 16
Q_SSD, S_SSD = Q_P1 + 2, S_P1 + 16
Q_D3, S_D3 = Q_SSD + 3 * 8, S_SSD + 3 * 48
Q_M0, S_M0 = Q_D3 + 8, S_D3 + 16
Q_POOL, S_POOL = Q_M0 + 6 * CHUNKS, S_M0 + 32 * CHUNKS
Q_M1, S_M1 = Q_POOL + 4, S_POOL + 8
LAST_SSD = {0: 4, 2: 5, 4: 6, 5: 7}
TURN_BACK = 2
NORMED = [[0, 4, 8, 12, 16], [0, 4, 7, 11, 14]]
LN_BASE = [[0, 11, 22, 33], [0, 11, 21, 32]]


def build(nc, a, out):
    with ExitStack() as ctx:
        def sb(name, shape, dt=F32):
            return ctx.enter_context(nc.sbuf_tensor(name, shape, dt))

        def pb(name, shape):
            return ctx.enter_context(nc.psum_tensor(name, shape, F32))

        def sem(name):
            return ctx.enter_context(nc.semaphore(name))

        x = sb("x", [P, TT, DM])
        xT = [sb("xTh", [P, KT, T], F32R), sb("xTl", [P, KT, T], F32R)]
        hT = [sb("hTh", [P, CK, T], F32R), sb("hTl", [P, CK, T], F32R)]
        raw = sb("raw", [P, RAW, SUBK, NB])
        whi = sb("whi", [P, RING, SUBK, NB], F32R)
        wlo = sb("wlo", [P, RING, SUBK, NB], F32R)
        ident = sb("ident", [P, P])
        eps = sb("eps", [P, 1])
        warm = sb("warm", [P, 1])

        area_a = sb("area_a", [P, 2 * NG * T])
        bcT = area_a[:].rearrange("p (m g t) -> p m g t", m=2, g=NG)
        gb = area_a[:].rearrange("p (m n) -> p m n", m=2)
        area_b = sb("area_b", [P, 4 * TT * NB])
        quarter = [area_b[:, i * TT * NB:(i + 1) * TT * NB] for i in range(4)]
        pj = quarter[0].rearrange("p (t n) -> p t n", t=TT)
        st = pj
        xs = quarter[1].rearrange("p (t n) -> p t n", t=TT)
        zs = quarter[2].rearrange("p (t n) -> p t n", t=TT)
        gy = quarter[3].rearrange("p (t n) -> p t n", t=TT)
        cv = quarter[3].rearrange("p (j n) -> p j n", j=CT)
        psc = area_b[:].rearrange("p (m n) -> p m n", m=2)
        area_c = sb("area_c", [P, 3 * 4 * P])
        e1, e2, mx = (area_c[:, i * 4 * P:(i + 1) * 4 * P].rearrange("p (h l) -> p h l", h=4) for i in range(3))
        hr = area_c[:, 0:TT * NB].rearrange("p (t n) -> p t n", t=TT)
        ptmp = area_c[:, 2 * NB:3 * NB]
        dtw = area_c[:].rearrange("p (k t) -> p k t", k=6)
        area_d = sb("area_d", [P, 8 * P + CT * (T + 2 * PAD)])
        fbc = [area_d[:, i * 8 * P:(i + 1) * 8 * P].rearrange("p (d h l) -> p d h l", d=2, h=4) for i in range(2)]
        cvin = area_d[:, 8 * P:8 * P + CT * (T + 2 * PAD)].rearrange("p (j n) -> p j n", j=CT)
        bands = area_d[:, 0:4 * TT * T].rearrange("p (w s t) -> p w s t", w=4, s=TT)
        xw = sb("xw", [P, NB])
        gd = sb("gd", [P, 2, 4, P])
        cur = sb("cur", [P, 2, T])
        btok = sb("btok", [P, TT, P])
        gt = sb("gt", [P, TT, 2, P])
        cols = sb("cols", [P, 6, P])
        dtv = cols[:, 0:2, :].rearrange("p k t -> p (k t)")
        masks = sb("masks", [P, 2, P])
        convw = sb("convw", [P, (DI + 2 * NG * P) // P, TAPS])
        convb = sb("convb", [P, (DI + 2 * NG * P) // P])
        normw = sb("normw", [P, DI // P])
        dskip = sb("dskip", [P, NH])
        dtp = sb("dtp", [P, 4])
        ss = sb("ss", [P, TT, 3])
        bst = sb("bst", [P, TT, 4, 6])
        mv = sb("mv", [P, TT, 5])

        acc = [[pb(f"acc{i}{t}", [P, NB]) for t in range(TT)] for i in range(2)]
        tb = [pb(f"tb{i}", [P, NB]) for i in range(2)]
        sbk = [pb(f"sbk{i}", [P, NB]) for i in range(2)]
        fscr = nc.dram_tensor("f_scratch", (P, T), F32).ap()

        raw_in = [sem(f"raw_in{r}") for r in range(RAW)]
        hi_ready, lo_ready, w_used = sem("hi_ready"), sem("lo_ready"), sem("w_used")
        acc_full = [sem(f"acc_full{i}") for i in range(2)]
        acc_free = [[sem(f"acc_free{i}{t}") for t in range(TT)] for i in range(2)]
        x_in = [sem("x_in_t0_left"), sem("x_in_t0_right"), sem("x_in_t1")]
        ident_in, const_in, eps_set = sem("ident_in"), sem("const_in"), sem("eps_set")
        gt_set = sem("gt_set")
        tr_done, tr_hi, tr_lo = sem("tr_done"), sem("tr_hi"), sem("tr_lo")
        x_scaled, squared = sem("x_scaled"), sem("squared")
        h_tr = [sem(f"h_tr{t}") for t in range(TT)]
        h_hi = [sem(f"h_hi{t}") for t in range(TT)]
        h_lo = [sem(f"h_lo{t}") for t in range(TT)]
        ln_vec = [sem(f"ln_vec{t}") for t in range(TT)]
        ln_root = [sem(f"ln_root{t}") for t in range(TT)]
        ln_act = [sem(f"ln_act{t}") for t in range(TT)]
        x_norm = [sem(f"x_norm{t}") for t in range(TT)]
        q3_gain, x_norm_q3 = sem("q3_gain"), sem("x_norm_q3")
        gb_in = sem("gb_in")
        stored = sem("stored")
        dt_vec, dt_act = sem("dt_vec"), sem("dt_act")
        f_ready, f_saved, col_tr, col_done = (sem(n) for n in ("f_ready", "f_saved", "col_tr", "col_done"))
        cv_tr, cvin_full, pad_set, tap_done, cv_silu = (
            sem(n) for n in ("cv_tr", "cvin_full", "pad_set", "tap_done", "cv_silu"))
        cur_half = sem("cur_half")
        back_tr, xs_out, cur_done, sc_done, gt_done, btok_done = (
            sem(n) for n in ("back_tr", "xs_out", "cur_done", "sc_done", "gt_done", "btok_done"))
        fbc_in = [sem(f"fbc_unit{u}_in") for u in range(4)]
        e_sub, e_min, e_exp, m_done, yd_done = (sem(n) for n in ("e_sub", "e_min", "e_exp", "m_done", "yd_done"))
        xw_done, gy_skip, st_done, st_out, off_done = (
            sem(n) for n in ("xw_done", "gy_skip", "st_done", "st_out", "off_done"))
        gy_yd, gy_off, gated, sumsq, rooted, inv_root, gy_done = (
            sem(n) for n in ("gy_yd", "gy_off", "gated", "sumsq", "rooted", "inv_root", "gy_done"))
        gy_tr, gy_hi, gy_lo, z_silu = sem("gy_tr"), sem("gy_hi"), sem("gy_lo"), sem("z_silu")
        bands_in, psc_in, bias_scaled, pool_added, pool_bias = (
            sem(n) for n in ("bands_in", "psc_in", "bias_scaled", "pool_added", "pool_bias"))
        pool_alpha = sem("pool_alpha")
        gd_part, gd_done = sem("gd_part"), sem("gd_done")

        block = ctx.enter_context(nc.Block())

        in_w = a["in_proj"].rearrange("(k p) n -> p k n", p=P)
        out_w = a["out_proj"].rearrange("(k p) n -> p k n", p=P)
        w1 = [a["w1"][i].rearrange("(k p) n -> p k n", p=P) for i in range(DEPTH)]
        w2 = [a["w2"][i].rearrange("(k p) n -> p k n", p=P) for i in range(DEPTH)]
        pool_w = a["pool_w"].rearrange("g (k p) n -> g p k n", p=P)
        x_rows = a["x"].rearrange("(t p) n -> p t n", p=P)
        out_rows = out.rearrange("(t p) n -> p t n", p=P)
        f_rows = fscr.rearrange("(d h) t -> d h t", d=2)

        def load_f(eng, g, u):
            t, hh = u // 2, u % 2
            for d in range(2):
                src = f_rows[d, bass.ds(g.times(HPG).n + 4 * hh, 4), t * P:(t + 1) * P]
                eng.dma_start(fbc[u % 2][:, d], src.partition_broadcast(P)).then_inc(fbc_in[u], 16)

        def narrow(sub):
            return sub.rearrange("p k (m n) -> p (k m) n", n=P)

        @block.sync
        def _(sp):
            sp.dma_start(ident[:], a["ident"]).then_inc(ident_in, 16)
            for h in range(2):
                cs = slice(h * DM // 2, (h + 1) * DM // 2)
                sp.dma_start(x[:, 0, cs], x_rows[:, 0, cs]).then_inc(x_in[h], 16)

            def load(s, src, dst=None):
                wait(sp, lo_ready, s + (1 - RAW))
                r = s.slot(RAW)
                sp.dma_start(raw[:, r] if dst is None else dst(raw[:, r]), src).then_inc(raw_in[r], 16)

            def load_in(s, col):
                for i in range(KT // SUBK):
                    load(s + i, in_w[:, SUBK * i:SUBK * (i + 1), bass.ds(col, NB)])

            def load_down(s, w, row, n, subs=CK // SUBK):
                for i in range(subs):
                    load(s + i, w[:, bass.ds(row + SUBK * i, SUBK), n * NB:(n + 1) * NB])

            def load_mlp(s0, layer):
                with sp.Fori(0, CHUNKS) as c:
                    s = Pos(s0, 32, c)
                    for j in range(2):
                        for i in range(KT // SUBK):
                            load(s + (8 * j + i), w1[layer][:, SUBK * i:SUBK * (i + 1), bass.ds(c * (CK * P) + j * NB, NB)])
                    for n in range(4):
                        load_down(s + (16 + 4 * n), w2[layer], c * CK, n)

            sp.dma_start(x[:, 1, :], x_rows[:, 1, :]).then_inc(x_in[2], 16)
            for i in range(2):
                load(Pos(S_DT + i), in_w[:, 8 * i:8 * (i + 1), DT0:DT0 + P], narrow)
            for i in range(4):
                load_in(Pos(S_BC + 8 * i), B0 + i * NB)
            for g in range(2):
                load_in(Pos(S_P0 + 16 * g), XS0 + g * NB)
                load_in(Pos(S_P0 + 16 * g + 8), g * NB)
            with sp.Fori(0, 3) as c:
                s = Pos(S_SSD, 48, c)
                load_in(s, c * (2 * NB) + (XS0 + 2 * NB))
                load_in(s + 8, c * (2 * NB) + 2 * NB)
                for n in range(4):
                    load_down(s + (16 + 4 * n), out_w, c * CK, n)
                load_in(s + 32, c * (2 * NB) + (XS0 + 3 * NB))
                load_in(s + 40, c * (2 * NB) + 3 * NB)
            for half in range(2):
                for n in range(4):
                    load_down(Pos(S_D3 + 8 * half + 2 * n), out_w, 3 * CK + 4 * half, n, 2)
            load_mlp(S_M0, 0)
            for g in range(4):
                for i in range(2):
                    load(Pos(S_POOL + 2 * g + i), pool_w[g][:, SUBK * i:SUBK * (i + 1), :])
            load_mlp(S_M1, 1)
            for t in range(TT):
                for i in range(4):
                    if t == 1 and i == 3:
                        sp.wait_ge(x_norm_q3, 2)
                    else:
                        sp.wait_ge(x_norm[t], NORMED[t][3] + i + 1)
                    cs = slice(i * NB, (i + 1) * NB)
                    sp.dma_start(out_rows[:, t, cs], x[:, t, cs]).then_inc(stored, 16)
            sp.wait_ge(stored, 16 * TT * 4)

        @block.tensor
        def _(pe):
            def rows(t):
                return slice(t * P, (t + 1) * P)

            def products(lhs, kts, t, q, s, first, last):
                pair = q.slot(2)
                if first:
                    pe.wait_ge(acc_free[pair][t], q.half().n)
                dst = acc[pair][t][:]
                for i, kt in enumerate(kts):
                    slot = (s + i // SUBK).slot(RING)
                    if t == 0 and i % SUBK == 0:
                        wait(pe, lo_ready, s + (i // SUBK + 1))
                    hi, lo = whi[:, slot, i % SUBK, :], wlo[:, slot, i % SUBK, :]
                    end = last and i == len(kts) - 1
                    pe.matmul(dst, lhs[1][:, kt, rows(t)], hi, start=first and i == 0, stop=False)
                    pe.matmul(dst, lhs[0][:, kt, rows(t)], hi, start=False, stop=False)
                    mm = pe.matmul(dst, lhs[0][:, kt, rows(t)], lo, start=False, stop=end)
                    if t == 1 and i % SUBK == SUBK - 1:
                        mm.then_inc(w_used, 1)
                    elif end:
                        mm.then_inc(acc_full[pair], 1)

            def none(k):
                pass

            def wide(q, s, after=none, amid={}):
                for b in range(2):
                    for t in range(TT):
                        if 2 * b + t in amid:
                            n, inner = amid[2 * b + t]
                            products(xT, range(8 * b, 8 * b + n), t, q, s + 4 * b, b == 0, False)
                            inner()
                            products(xT, range(8 * b + n, 8 * b + 8), t, q, s + (4 * b + n // SUBK), False, b == 1)
                        else:
                            products(xT, range(8 * b, 8 * b + 8), t, q, s + 4 * b, b == 0, b == 1)
                        after(2 * b + t)

            def down(q, s, after=none, kts=range(CK), n=0):
                for t in range(TT):
                    products(hT, kts, t, q, s, True, True)
                    after(2 * n + t)

            def turn_x(first, t, ready, quarters=range(4)):
                for i in quarters:
                    u = first + 4 * t + i
                    ready(t, i)
                    wait(pe, tr_lo, Pos(u - 1))
                    for k in range(CT):
                        mm = pe.transpose(tb[u % 2][:, k * P:(k + 1) * P],
                                          x[:, t, (CT * i + k) * P:(CT * i + k + 1) * P], ident[:])
                    mm.then_inc(tr_done, 1)

            def by_tiles(lhs, groups, amid=None):
                for t in range(TT):
                    for j, (q, s, kts) in enumerate(groups):
                        if t == 1 and j == len(groups) - 1 and amid is not None:
                            n = len(kts) // 2 if len(kts) > 4 else 0
                            if n:
                                products(lhs, kts[:n], t, q, s, True, False)
                            amid()
                            products(lhs, kts[n:], t, q, s + n // SUBK, n == 0, True)
                        else:
                            products(lhs, kts, t, q, s, True, True)

            def wide_renewed(q, s, first, ready):
                turn_x(first, 0, ready, (2, 3))
                products(xT, range(0, 8), 0, q, s, True, False)
                pe.wait_ge(tr_lo, first + 3)
                products(xT, range(8, 12), 0, q, s + 4, False, False)
                turn_x(first, 1, ready, (0, 1))
                products(xT, range(12, 16), 0, q, s + 6, False, True)
                turn_x(first, 1, ready, (2, 3))
                products(xT, range(0, 8), 1, q, s, True, False)
                pe.wait_ge(tr_lo, first + 8)
                products(xT, range(8, 16), 1, q, s + 4, False, True)

            def warm_up(n):
                pe.wait_ge(gt_set, 1)
                for _ in range(n):
                    pe.matmul(sbk[0][:], gt[:, 0, 0, :], gt[:].rearrange("p t m n -> p (t m n)"), start=True, stop=True)

            def dt_group(ready):
                turn_x(0, 0, ready)
                turn_x(0, 1, ready)
                warm_up(1)
                pe.wait_ge(tr_lo, 8)
                pe.wait_ge(acc_free[Q_DT % 2][0], 1)
                dst = acc[Q_DT % 2][0][:, 0:T]
                for b in range(2):
                    pe.wait_ge(lo_ready, S_DT + b + 1)
                    for i in range(8):
                        kt, hi, lo = 8 * b + i, narrow(whi[:, S_DT + b])[:, i, :], narrow(wlo[:, S_DT + b])[:, i, :]
                        end = kt == KT - 1
                        pe.matmul(dst, hi, xT[1][:, kt, :], start=kt == 0, stop=False)
                        pe.matmul(dst, hi, xT[0][:, kt, :], start=False, stop=False)
                        mm = pe.matmul(dst, lo, xT[0][:, kt, :], start=False, stop=end)
                    mm.then_inc(w_used, 1)

            def turn_h(u, t):
                pe.wait_ge(squared, (u.times(2) + (t + 1)).n)
                for k in range(CT):
                    mm = pe.transpose(tb[t][:, k * P:(k + 1) * P], hr[:, t, k * P:(k + 1) * P], ident[:])
                mm.then_inc(h_tr[t], 1)

            def turn_pj(q):
                for t in range(TT):
                    pe.wait_ge(acc_free[q.slot(2)][t], (q.half() + 1).n)
                for t in range(TT):
                    for j in range(CT):
                        mm = pe.transpose(tb[t][:, j * P:(j + 1) * P], pj[:, t, j * P:(j + 1) * P], ident[:])
                mm.then_inc(cv_tr, 1)

            def score(g):
                pe.wait_ge(cur_done, (g + 1).n)
                wait(pe, gy_lo, g.times(4))
                for t in range(TT):
                    pe.matmul(sbk[0][:, rows(t)], cur[:, 0, rows(t)], cur[:, 1, rows(t)], start=True, stop=True)
                for t in range(TT):
                    mm = pe.transpose(sbk[1][:, rows(t)], cur[:, 0, rows(t)], ident[:])
                mm.then_inc(sc_done, 1)

            def turn_back(g):
                pe.wait_ge(cv_silu, (g + (4 + 1)).n)
                pe.wait_ge(cvin_full, (g.times(2) + 2 * (4 + 1)).n)
                for t in range(TT):
                    for j in range(CT):
                        mm = pe.transpose(tb[t][:, j * P:(j + 1) * P], cv[:, j, rows(t)], ident[:])
                mm.then_inc(back_tr, 1)

            def diag(g, u):
                t, hh = u // 2, u % 2
                pe.wait_ge(m_done, (g.times(4) + (u + 1)).n)
                pe.wait_ge(xs_out, (g.times(2) + (t + 1)).n)
                if u == 0:
                    pe.wait_ge(gt_done, (g.times(4) + 4).n)
                if u == 2:
                    pe.wait_ge(gy_yd, (g.times(2) + 1).n)
                for h in range(4):
                    cs = slice((4 * hh + h) * HD, (4 * hh + h + 1) * HD)
                    mm = pe.matmul(sbk[0][:, cs], mx[:, h, :], xs[:, t, cs], start=True, stop=True)
                mm.then_inc(yd_done, 1)

            def state(g, t):
                if t == 0:
                    pe.wait_ge(btok_done, (g + 1).n)
                else:
                    pe.wait_ge(gy_off, (g.times(16) + 8).n)
                pe.wait_ge(xw_done, (g.times(2) + (t + 1)).n)
                pe.matmul(sbk[1][:], btok[:, t, :], xw[:], start=True, stop=True).then_inc(st_done, 1)

            def carried(g, t):
                pe.wait_ge(st_out, (g.times(2) + (t + 1)).n)
                pe.matmul(sbk[1][:], cur[:, 1, rows(1 - t)], st[:, t, :], start=True, stop=True).then_inc(off_done, 1)

            def turn_gy(g):
                pe.wait_ge(gy_done, (g.times(2) + 2).n)
                pe.wait_ge(gy_off, (g.times(16) + 16).n)
                for b in range(2):
                    for k in range(2):
                        for t in range(TT):
                            ch = 2 * b + k
                            mm = pe.transpose(sbk[b][:, (2 * k + t) * P:(2 * k + t + 1) * P],
                                              gy[:, t, ch * P:(ch + 1) * P], ident[:])
                mm.then_inc(gy_tr, 1)

            def chain(g, k):
                if k == 1:
                    score(g)
                elif k == 3:
                    diag(g, 0)
                    state(g, 0)
                elif k == 4:
                    diag(g, 1)
                    carried(g, 0)
                elif k == 5:
                    diag(g, 2)
                    state(g, 1)
                elif k == 6:
                    diag(g, 3)
                    carried(g, 1)

            def wide_z(q, s, g, before=None):
                def amid():
                    if before is None:
                        pe.wait_ge(col_done, 2)
                    turn_pj(q + -1)
                    if before is not None:
                        turn_gy(before)
                wide(q, s, lambda k: chain(g, k), amid={0: (6, amid), 3: (TURN_BACK, lambda: turn_back(g))})

            warm_up(2)
            pe.wait_ge(ident_in, 16)
            dt_group(lambda t, i: pe.wait_ge(x_in[i // 2 if t == 0 else 2], 16))
            with pe.Fori(0, 2) as j:
                for i in range(2):
                    wide(Pos(Q_BC + i, 2, j), Pos(S_BC + 8 * i, 16, j))
                    turn_pj(Pos(Q_BC + i, 2, j))
            def turn_cols(k):
                if k == 3:
                    pe.wait_ge(dt_vec, 13)
                    for t in range(TT):
                        pe.transpose(tb[0][:, rows(t)], dtw[:, 3, rows(t)], ident[:])
                    for t in range(TT):
                        pe.transpose(tb[0][:, (2 + t) * P:(3 + t) * P], dtw[:, 2, rows(t)], ident[:])
                    pe.transpose(tb[1][:, 0:P], dtw[:, 4, 0:P], ident[:])
                    pe.transpose(tb[1][:, P:2 * P], dtw[:, 4, P:2 * P], ident[:]).then_inc(col_tr, 1)
            wide(Pos(Q_P0), Pos(S_P0), turn_cols)
            wide_z(Pos(Q_P0 + 1), Pos(S_P0 + 8), Pos(0))
            wide(Pos(Q_P1), Pos(S_P1), lambda k: chain(Pos(0), 4 + k))
            wide_z(Pos(Q_P1 + 1), Pos(S_P1 + 8), Pos(1), Pos(0))
            with pe.Fori(0, 3) as c:
                q, s = Pos(Q_SSD, 8, c), Pos(S_SSD, 48, c)
                ge, go = Pos(2, 2, c), Pos(3, 2, c)
                gl = Pos(1, 2, c)
                wide(q, s, lambda k: chain(gl, 4 + k))
                wide_z(q + 1, s + 8, ge, gl)
                pe.wait_ge(gy_lo, ge.times(4).n)
                for n in range(4):
                    down(q + (2 + n), s + (16 + 4 * n), lambda k: chain(ge, 4 + k), n=n)
                wide(q + 6, s + 32)
                wide_z(q + 7, s + 40, go, ge)
            def x_ready(i):
                return lambda t, j: pe.wait_ge(x_norm[t], NORMED[t][i] + j + 1)

            g7 = Pos(7)
            pe.wait_ge(gy_lo, 4 * 7)
            def last_ssd(k):
                if LAST_SSD.get(k, 7) < 7:
                    chain(g7, LAST_SSD[k])
                if k == 6:
                    turn_gy(g7)
            for n in range(4):
                down(Pos(Q_D3 + n), Pos(S_D3 + 2 * n), last_ssd, range(0, 4), n)
            pe.wait_ge(gy_lo, 4 * 8)
            by_tiles(hT, [(Pos(Q_D3 + 4 + n), Pos(S_D3 + 8 + 2 * n), range(4, 8)) for n in range(4)],
                     lambda: turn_x(8, 0, x_ready(0), (0, 1)))

            def mlp_chunk(q, s, u, first_group=None, amid=None, last=False):
                if first_group is None:
                    wide(q, s)
                else:
                    wide_renewed(q, s, *first_group)
                wide(q + 1, s + 8, lambda k: turn_h(u, k) if k < TT else None)
                for t in range(TT):
                    pe.wait_ge(h_lo[t], (u + 1).n)
                    products(hT, range(0, 4), t, q + 2, s + 16, True, False)
                    turn_h(u + 1, t)
                for t in range(TT):
                    pe.wait_ge(h_lo[t], (u + 2).n)
                    products(hT, range(4, 8), t, q + 2, s + 18, False, True)
                down(q + 3, s + 20)
                if last:
                    by_tiles(hT, [(q + (2 + n), s + (16 + 4 * n), range(CK)) for n in (2, 3)], amid)
                else:
                    for n in (2, 3):
                        down(q + (2 + n), s + (16 + 4 * n))

            def mlp(q0, s0, layer, i, first, amid=None):
                u0, last = 2 * CHUNKS * layer, CHUNKS - 1
                mlp_chunk(Pos(q0), Pos(s0), Pos(u0), (first, x_ready(i)))
                with pe.Fori(0, CHUNKS - 2) as c:
                    mlp_chunk(Pos(q0 + 6, 6, c), Pos(s0 + 32, 32, c), Pos(u0 + 2, 2, c))
                mlp_chunk(Pos(q0 + 6 * last), Pos(s0 + 32 * last), Pos(u0 + 2 * last), amid=amid, last=True)

            mlp(Q_M0, S_M0, 0, 0, 8)

            def pool_x(g):
                pe.wait_ge(x_norm[0], NORMED[0][1] + g + 1)
                if g < 3:
                    pe.wait_ge(x_norm[1], NORMED[1][1] + g + 1)
                else:
                    pe.wait_ge(x_norm_q3, 1)
                halo = WINDOWS[-1] // 2
                for u in (2 * g, 2 * g + 1):
                    pe.wait_ge(tr_lo, 16 + u - 1)
                    for k in range(2):
                        ch = 2 * u + k
                        lhs = [x[:, t, ch * P:(ch + 1) * P] for t in range(TT)]
                        col = k * T
                        pe.matmul(tb[u % 2][:, col:col + P + halo], lhs[0], bands[:, g, 0, 0:P + halo],
                                  start=True, stop=False)
                        pe.matmul(tb[u % 2][:, col + P - halo:col + P + halo], lhs[1],
                                  bands[:, g, 1, P - halo:P + halo], start=False, stop=False)
                        mm = pe.matmul(tb[u % 2][:, col + P + halo:col + T], lhs[1], bands[:, g, 1, P + halo:T],
                                       start=False, stop=True)
                    mm.then_inc(tr_done, 1)

            pe.wait_ge(bands_in, 16)
            for t in range(TT):
                pe.wait_ge(h_lo[t], 2 * CHUNKS)
            warm_up(4)
            pool_x(0)
            pool_groups = [(Pos(Q_POOL + g), Pos(S_POOL + 2 * g), range(4 * g, 4 * g + 4)) for g in range(4)]
            for g, (q, s, kts) in enumerate(pool_groups):
                if g < 3:
                    pool_x(g + 1)
                pe.wait_ge(tr_lo, 16 + 2 * g + 2)
                products(xT, kts, 0, q, s, True, True)
            for q, s, kts in pool_groups[:3]:
                products(xT, kts, 1, q, s, True, True)
            turn_x(24, 0, x_ready(2), (0, 1))
            q, s, kts = pool_groups[3]
            products(xT, kts, 1, q, s, True, True)
            mlp(Q_M1, S_M1, 1, 2, 24)

        @block.scalar
        def _(act):
            def split_hi(s):
                r = s.slot(RAW)
                act.wait_ge(raw_in[r], Pos(16 * (s.base // RAW + 1), 16 * s.step // RAW, s.loop).n)
                wait(act, w_used, s + (1 - RING))
                act.copy(whi[:, s.slot(RING)], raw[:, r]).then_inc(hi_ready, 1)

            def none(k):
                pass

            def blocks(s, n, subs, after=none, done=0):
                for b in range(n):
                    for i in range(subs):
                        if subs * b + i >= done:
                            split_hi(s + (subs * b + 4 + i))
                    for t in range(TT):
                        after(2 * b + t)

            def full(q, t, s_end):
                if t == 0:
                    act.wait_ge(acc_full[q.slot(2)], q.half().n)
                else:
                    act.wait_ge(w_used, s_end.n)

            def out_of_psum(q, t, s_end, dst, func, width=NB):
                full(q, t, s_end)
                act.activation(dst, acc[q.slot(2)][t][:, 0:width], func).then_inc(acc_free[q.slot(2)][t], 1)

            def hi_x(first, t, quarters=range(4)):
                for i in quarters:
                    u = first + 4 * t + i
                    act.wait_ge(tr_done, u + 1)
                    act.copy(xT[0][:, CT * i:CT * (i + 1), t * P:(t + 1) * P],
                             tb[u % 2][:].rearrange("p (k n) -> p k n", k=CT)).then_inc(tr_hi, 1)

            def pj_evac(q, s_end, t):
                out_of_psum(q, t, s_end, pj[:, t, :], ACT.Copy)

            def cvin_fill(k):
                act.wait_ge(cv_tr, (k + 1).n)
                for t in range(TT):
                    act.copy(cvin[:, :, PAD + t * P:PAD + (t + 1) * P],
                             tb[t][:].rearrange("p (j n) -> p j n", j=CT)).then_inc(cvin_full, 1)

            def silu_cv(k, dst):
                act.wait_ge(tap_done, (k + 1).times(TAPS * CT).n)
                act.activation(dst, cv[:], ACT.Silu).then_inc(cv_silu, 1)

            def decay(g, u):
                act.wait_ge(e_min, (g.times(4) + (u + 1)).n)
                act.activation(e1[:], e1[:], ACT.Exp).then_inc(e_exp, 1)

            def state_out(g, t):
                act.wait_ge(st_done, (g.times(2) + (t + 1)).n)
                act.copy(st[:, t, :], sbk[1][:]).then_inc(st_out, 1)

            def gy_high(g):
                act.wait_ge(gy_tr, (g + 1).n)
                for k in range(CT):
                    w = normw[:, bass.ds(g.times(CT).n + k, 1)]
                    act.activation(hT[0][:, CT * g.slot(2) + k, :], sbk[k // 2][:, (k % 2) * T:(k % 2 + 1) * T],
                                   ACT.Copy, scale=w).then_inc(gy_hi, 1)

            def chain(g, k, zq=None, z_end=None):
                if k == 0:
                    wait(act, e_sub, g.times(8))
                    cvin_fill(g + 4)
                elif k == 1:
                    silu_cv(g + 4, cv[:])
                    load_f(act, g, 1)
                    act.wait_ge(sc_done, (g + 1).n)
                    act.copy(btok[:].rearrange("p t n -> p (t n)"), sbk[1][:, 0:T]).then_inc(btok_done, 1)
                    decay(g, 0)
                    load_f(act, g, 2)
                elif k == 2:
                    act.wait_ge(back_tr, (g + 1).n)
                    wait(act, yd_done, g.times(4))
                    wait(act, xw_done, g.times(2))
                    wait(act, gy_skip, g.times(2))
                    for t in range(TT):
                        act.copy(xs[:, t, :], tb[t][:]).then_inc(xs_out, 1)
                elif k == 3:
                    wait(act, gated, g.times(2))
                    wait(act, sumsq, g.times(2))
                    out_of_psum(zq, 0, z_end, zs[:, 0, :], ACT.Copy)
                    decay(g, 1)
                    load_f(act, g, 3)
                    split_hi(z_end + 4)
                    split_hi(z_end + 5)
                    out_of_psum(zq, 1, z_end, zs[:, 1, :], ACT.Copy)
                    state_out(g, 0)
                elif k == 4:
                    decay(g, 2)
                elif k == 5:
                    state_out(g, 1)
                    decay(g, 3)
                    for t in range(TT):
                        act.wait_ge(acc_free[zq.slot(2)][t], (zq.half() + 1).n)
                    act.activation(zs[:], zs[:], ACT.Silu).then_inc(z_silu, 1)
                    act.activation(warm[:], eps[:], ACT.Sqrt)
                elif k == 7:
                    act.wait_ge(gated, (g.times(2) + 2).n)
                    for t in range(TT):
                        act.activation(zs[:, t, :], gy[:, t, :], ACT.Square,
                                       accum_out=ss[:, t, 0:1]).then_inc(sumsq, 1)
                    for t in range(TT):
                        act.wait_ge(sumsq, (g.times(2) + (t + 1)).n)
                        act.activation(ss[:, t, 1:2], ss[:, t, 0:1], ACT.Sqrt, bias=eps[:],
                                       scale=1.0 / NB).then_inc(rooted, 1)

            def xs_group(q, s, g, prior=None, prior_z=None, done=0):
                def after(k):
                    if k == 2:
                        wait(act, off_done, g.times(2) + -1)
                        pj_evac(q, s + 8, 0)
                    if k == 3:
                        split_hi(s + 12)
                        split_hi(s + 13)
                    if prior is not None:
                        chain(prior, 4 + k, prior_z)
                    if k == 3:
                        wait(act, off_done, g.times(2))
                        pj_evac(q, s + 8, 1)
                        split_hi(s + 14)
                        split_hi(s + 15)
                blocks(s, 2, 4, after, done)

            def z_group(q, s, g, before):
                chain(g, 0)
                if before is not None:
                    gy_high(before)
                for i in range(4):
                    split_hi(s + (8 + i))
                for k in range(1, 4):
                    chain(g, k, q, s + 8)

            def dt_steps(k):
                if k == 0:
                    act.wait_ge(dt_vec, 1)
                    act.activation(dtw[:, 0, :], dtw[:, 0, :], ACT.Exp, scale=-1.0).then_inc(dt_act, 1)
                    act.activation(dtp[:, 2:3], dtp[:, 1:2], ACT.Exp).then_inc(dt_act, 1)
                    act.wait_ge(dt_vec, 4)
                    act.activation(dtw[:, 3, :], dtw[:, 1, :], ACT.Ln).then_inc(dt_act, 1)
                    act.wait_ge(f_ready, 4)
                    f, h = dtw[:, 3, :], P // 2
                    act.activation(dtw[0:h, 4, 0:P], f[0:h, 0:P], ACT.Exp, scale=-1.0,
                                   bias=f[0:h, P - 1:P]).then_inc(dt_act, 1)
                    act.activation(dtw[h:P, 4, 0:P], f[h:P, P:T], ACT.Exp, scale=-1.0,
                                   bias=f[h:P, P:P + 1]).then_inc(dt_act, 1)
                    act.activation(dtw[0:h, 4, P:T], f[0:h, P:T], ACT.Exp).then_inc(dt_act, 1)
                    act.activation(dtw[h:P, 4, P:T], f[h:P, 0:P], ACT.Exp).then_inc(dt_act, 1)
                elif k == 3:
                    act.wait_ge(col_tr, 1)
                    act.copy(cols[:, 0:4, :], tb[0][:].rearrange("p (k n) -> p k n", k=4)).then_inc(col_done, 1)
                    act.copy(cols[:, 4:6, :], tb[1][:, 0:T].rearrange("p (k n) -> p k n", k=2)).then_inc(col_done, 1)

            hi_x(0, 0)
            hi_x(0, 1)
            split_hi(Pos(S_DT))
            split_hi(Pos(S_DT + 1))
            for i in range(8):
                split_hi(Pos(S_BC + i))
            act.wait_ge(const_in, 16 * 7)
            act.wait_ge(eps_set, 1)
            with act.Fori(0, 2) as j:
                for i in range(2):
                    k, s = Pos(i, 2, j), Pos(S_BC + 8 * i, 16, j)
                    def bc_out(n):
                        if n >= 2:
                            out_of_psum(Pos(Q_BC + i, 2, j), n - 2, s + 8, pj[:, n - 2, :], ACT.Copy)
                        if n == 3:
                            cvin_fill(k)
                            for m in range(4):
                                split_hi(s + (12 + m))
                            silu_cv(k, area_a[:, bass.ds(j * (NG * T) + i * (CT * T), CT * T)].rearrange(
                                "p (g t) -> p g t", g=CT))
                    blocks(s, 2, 4, bc_out, done=4)

            def first_xs(k):
                dt_steps(k)
                if k >= 2:
                    pj_evac(Pos(Q_P0), Pos(S_P0 + 8), k - 2)
            blocks(Pos(S_P0), 2, 4, first_xs, done=4)
            for i in range(4):
                split_hi(Pos(S_P0 + 12 + i))
            act.wait_ge(f_saved, 16)
            z_group(Pos(Q_P0 + 1), Pos(S_P0 + 8), Pos(0), None)
            xs_group(Pos(Q_P1), Pos(S_P1), Pos(1), Pos(0), Pos(Q_P0 + 1), done=2)
            z_group(Pos(Q_P1 + 1), Pos(S_P1 + 8), Pos(1), Pos(0))
            with act.Fori(0, 3) as c:
                q, s = Pos(Q_SSD, 8, c), Pos(S_SSD, 48, c)
                gl, ge, go = Pos(1, 2, c), Pos(2, 2, c), Pos(3, 2, c)
                xs_group(q, s, ge, gl, q + -1, done=2)
                z_group(q + 1, s + 8, ge, gl)
                blocks(s + 16, 4, 4, lambda k: chain(ge, 4 + k, q + 1), done=2)
                xs_group(q + 6, s + 32, go)
                z_group(q + 7, s + 40, go, ge)
            blocks(Pos(S_D3), 4, 2, lambda k: chain(Pos(7), LAST_SSD[k], Pos(Q_D3 - 1)) if k in LAST_SSD else None,
                   done=2)
            gy_high(Pos(7))
            blocks(Pos(S_D3 + 8), 2, 2)

            def norm(i, t):
                act.wait_ge(ln_vec[t], LN_BASE[t][i] + 5)
                act.activation(mv[:, t, 2:3], mv[:, t, 1:2], ACT.Sqrt, bias=eps[:]).then_inc(ln_root[t], 1)
                act.wait_ge(ln_vec[t], LN_BASE[t][i] + 7)
                for j in range(4):
                    cs = slice(j * NB, (j + 1) * NB)
                    act.activation(x[:, t, cs], x[:, t, cs], ACT.Identity, bias=mv[:, t, 4:5],
                                   scale=mv[:, t, 3:4]).then_inc(ln_act[t], 1)

            def quick_norm(i):
                act.wait_ge(ln_vec[1], LN_BASE[1][i] + 5)
                act.activation(mv[:, 1, 2:3], mv[:, 1, 1:2], ACT.Sqrt, bias=eps[:]).then_inc(ln_root[1], 1)
                act.wait_ge(ln_vec[1], LN_BASE[1][i] + 8)
                act.activation(x[:, 1, 3 * NB:], x[:, 1, 3 * NB:], ACT.Identity, bias=mv[:, 1, 4:5],
                               scale=mv[:, 1, 3:4]).then_inc(ln_act[1], 4)

            def renew_x(i, s, first):
                norm(i, 0)
                split_hi(s)
                split_hi(s + 1)
                hi_x(first, 0, (0, 1))
                split_hi(s + 2)
                split_hi(s + 3)
                hi_x(first, 0, (2, 3))
                split_hi(s + 4)
                split_hi(s + 5)
                norm(i, 1)
                split_hi(s + 6)
                split_hi(s + 7)
                hi_x(first, 1)

            def hidden(q, s_end, u, t):
                out_of_psum(q, t, s_end, hr[:, t, :], ACT.Relu)
                act.wait_ge(acc_free[q.slot(2)][t], (q.half() + 1).n)
                act.activation(hr[:, t, :], hr[:, t, :], ACT.Square).then_inc(squared, 1)

            def hi_h(u, t):
                act.wait_ge(h_tr[t], (u + 1).n)
                kt = CT * u.slot(2)
                act.copy(hT[0][:, kt:kt + CT, t * P:(t + 1) * P],
                         tb[t][:].rearrange("p (k n) -> p k n", k=CT)).then_inc(h_hi[t], 1)

            def mlp_chunk(q, s, u, first=False, last=False):
                if first:
                    hidden(q, s + 8, u, 0)
                    for i in range(4):
                        split_hi(s + (8 + i))
                    hidden(q, s + 8, u, 1)
                else:
                    blocks(s, 2, 4, lambda k: hidden(q, s + 8, u, k - 2) if k >= 2 else None)
                def second(k):
                    if k < 2:
                        hi_h(u, k)
                    else:
                        hidden(q + 1, s + 16, u + 1, k - 2)
                blocks(s + 8, 2, 4, second)
                for t in range(TT):
                    for i in range(2):
                        split_hi(s + (20 + 2 * t + i))
                    hi_h(u + 1, t)
                blocks(s + 20, 2 if last else 3, 4)

            def mlp(q0, s0, layer):
                u0, last = 2 * CHUNKS * layer, CHUNKS - 1
                mlp_chunk(Pos(q0), Pos(s0), Pos(u0), first=True)
                with act.Fori(0, CHUNKS - 2) as c:
                    mlp_chunk(Pos(q0 + 6, 6, c), Pos(s0 + 32, 32, c), Pos(u0 + 2, 2, c))
                mlp_chunk(Pos(q0 + 6 * last), Pos(s0 + 32 * last), Pos(u0 + 2 * last), last=True)

            act.wait_ge(yd_done, 4 * NG)
            renew_x(0, Pos(S_M0), 8)
            mlp(Q_M0, S_M0, 0)
            norm(1, 0)
            for i in range(4):
                split_hi(Pos(S_POOL + i))
            quick_norm(1)

            def hi_pool(g):
                for u in (2 * g, 2 * g + 1):
                    act.wait_ge(tr_done, 16 + u + 1)
                    act.copy(xT[0][:, 2 * u:2 * u + 2, :],
                             tb[u % 2][:].rearrange("p (k n) -> p k n", k=2)).then_inc(tr_hi, 1)
            hi_pool(0)
            split_hi(Pos(S_POOL + 4))
            split_hi(Pos(S_POOL + 5))
            hi_pool(1)
            hi_pool(2)
            split_hi(Pos(S_POOL + 6))
            split_hi(Pos(S_POOL + 7))
            hi_pool(3)
            renew_x(2, Pos(S_M1), 24)
            mlp(Q_M1, S_M1, 1)
            norm(3, 0)
            quick_norm(3)

        @block.vector
        def _(dve):
            def split_lo(s):
                r, slot = s.slot(RAW), s.slot(RING)
                dve.wait_ge(hi_ready, (s + 1).n)
                dve.tensor_tensor(wlo[:, slot], raw[:, r], whi[:, slot].bitcast(F32), ALU.subtract).then_inc(lo_ready, 1)

            def none(k):
                pass

            def blocks(s, n, subs, after=none, done=0):
                for b in range(n):
                    for i in range(subs):
                        if subs * b + i >= done:
                            split_lo(s + (subs * b + 4 + i))
                    for t in range(TT):
                        after(2 * b + t)

            def full(q, t, s_end):
                if t == 0:
                    dve.wait_ge(acc_full[q.slot(2)], q.half().n)
                else:
                    dve.wait_ge(w_used, s_end.n)

            def lo_of(dst, src, hi, done):
                dve.tensor_tensor(dst, src, hi.bitcast(F32), ALU.subtract).then_inc(done, 1)

            def lo_x(first, t, i):
                u = first + 4 * t + i
                dve.wait_ge(tr_hi, u + 1)
                part = (slice(None), slice(CT * i, CT * (i + 1)), slice(t * P, (t + 1) * P))
                lo_of(xT[1][part], tb[u % 2][:].rearrange("p (k n) -> p k n", k=CT), xT[0][part], tr_lo)

            def add_x(q, s_end, t, n, first=False, norm=False):
                full(q, t, s_end)
                cs, free = slice(n * NB, (n + 1) * NB), acc_free[q.slot(2)][t]
                if first:
                    dve.scalar_tensor_tensor(x[:, t, cs], x[:, t, cs], ALPHA, acc[q.slot(2)][t][:],
                                             ALU.mult, ALU.add).then_inc(free, 1)
                else:
                    dve.tensor_tensor(x[:, t, cs], x[:, t, cs], acc[q.slot(2)][t][:], ALU.add).then_inc(free, 1)
                if norm:
                    dve.wait_ge(free, (q.half() + 1).n)
                    stats(t, n)

            def stats(t, n):
                dve.bn_stats(bst[:, t, n, :], x[:, t, n * NB:(n + 1) * NB]).then_inc(ln_vec[t], 1)

            def down(q, s, n, after=none, subs=4, first=False, norm=False, done=0):
                def both(t):
                    add_x(q, s + subs, t, n, first, norm)
                    after(2 * n + t)
                blocks(s, 1, subs, both, done)

            def set_pads():
                dve.memset(cvin[:, :, 0:PAD], 0.0).then_inc(pad_set, 1)
                dve.memset(cvin[:, :, PAD + T:PAD + T + PAD], 0.0).then_inc(pad_set, 1)

            def convolve(k, ch):
                dve.wait_ge(cvin_full, (k.times(2) + 2).n)
                n = k.times(TAPS * CT)
                for tap in range(TAPS):
                    for j in range(CT):
                        w = convw[:, bass.ds(ch.n + j, 1), tap]
                        src = cvin[:, j, tap:tap + T]
                        if tap == 0:
                            dve.tensor_scalar(cv[:, j, :], src, w, convb[:, bass.ds(ch.n + j, 1)],
                                              ALU.mult, ALU.add).then_inc(tap_done, 1)
                        else:
                            dve.wait_ge(tap_done, (n + (CT * (tap - 1) + j + 1)).n)
                            dve.scalar_tensor_tensor(cv[:, j, :], src, w, cv[:, j, :],
                                                     ALU.mult, ALU.add).then_inc(tap_done, 1)

            def gy_low(g):
                for k in range(CT):
                    dve.wait_ge(gy_hi, (g.times(CT) + 2 * (k // 2 + 1)).n)
                    kt = CT * g.slot(2) + k
                    w = normw[:, bass.ds(g.times(CT).n + k, 1)]
                    dve.scalar_tensor_tensor(hT[1][:, kt, :], sbk[k // 2][:, (k % 2) * T:(k % 2 + 1) * T], w,
                                             hT[0][:, kt, :].bitcast(F32), ALU.mult, ALU.subtract).then_inc(gy_lo, 1)

            def heads(buf, g, first):
                return buf[:, bass.ds(g.times(HPG).n + first, 4)]

            def decays(g, u):
                t, hh = u // 2, u % 2
                dve.wait_ge(fbc_in[u], (g + 1).times(32).n)
                wait(dve, m_done, g.times(4) + u)
                for d, dst in ((0, e1), (1, e2)):
                    col = heads(cols[:, t, :], g, d * NH + 4 * hh)
                    dve.tensor_tensor(dst[:], fbc[u % 2][:, d], col.unsqueeze(2).to_broadcast([P, 4, P]),
                                      ALU.subtract).then_inc(e_sub, 1)
                dve.wait_ge(e_sub, (g.times(8) + 2 * (u + 1)).n)
                dve.tensor_tensor(e1[:], e1[:], e2[:], ALU.min).then_inc(e_min, 1)

            def decayed(g, u):
                dve.wait_ge(gd_done, (g.times(4) + (u + 1)).n)
                dve.wait_ge(e_exp, (g.times(4) + (u + 1)).n)
                wait(dve, yd_done, g.times(4) + u)
                dve.tensor_tensor(mx[:], e1[:], gd[:, 0], ALU.mult).then_inc(m_done, 1)

            def add_carried(g, t):
                o = 1 - t
                dve.wait_ge(off_done, (g.times(2) + (t + 1)).n)
                for h in range(HPG):
                    cs = slice(h * HD, (h + 1) * HD)
                    ef = cols[:, 5, bass.ds(g.times(HPG).n + t * NH + h, 1)]
                    dve.scalar_tensor_tensor(gy[:, o, cs], sbk[1][:, cs], ef, gy[:, o, cs],
                                             ALU.mult, ALU.add).then_inc(gy_off, 1)

            def chain(g, k):
                if k == 0:
                    wait(dve, gy_tr, g)
                    wait(dve, e_sub, g.times(8))
                    set_pads()
                    dve.wait_ge(pad_set, (g.times(2) + 4).n)
                    convolve(g + 4, g.times(CT))
                elif k == 1:
                    dve.wait_ge(sc_done, (g + 1).n)
                    for t in range(TT):
                        for d in range(2):
                            dve.tensor_tensor(gt[:, t, d, :], sbk[0][:, t * P:(t + 1) * P], masks[:, d, :],
                                              ALU.mult).then_inc(gt_done, 1)
                    decays(g, 0)
                elif k == 4:
                    decays(g, 2)
                    dve.wait_ge(yd_done, (g.times(4) + 2).n)
                    dve.wait_ge(gy_skip, (g.times(2) + 2).n)
                    dve.tensor_tensor(gy[:, 0, :], gy[:, 0, :], sbk[0][:], ALU.add).then_inc(gy_yd, 1)
                    add_carried(g, 0)
                    decayed(g, 2)
                elif k == 5:
                    decays(g, 3)
                    decayed(g, 3)
                elif k == 6:
                    dve.wait_ge(yd_done, (g.times(4) + 4).n)
                    dve.wait_ge(gy_off, (g.times(16) + 8).n)
                    dve.tensor_tensor(gy[:, 1, :], gy[:, 1, :], sbk[0][:], ALU.add).then_inc(gy_yd, 1)
                    dve.wait_ge(gy_yd, (g.times(2) + 1).n)
                    add_carried(g, 1)
                    dve.wait_ge(gy_off, (g.times(16) + 16).n)
                    dve.wait_ge(gy_yd, (g.times(2) + 2).n)
                    dve.wait_ge(z_silu, (g + 1).n)
                    for t in range(TT):
                        dve.tensor_tensor(gy[:, t, :], gy[:, t, :], zs[:, t, :], ALU.mult).then_inc(gated, 1)
                elif k == 7:
                    for t in range(TT):
                        dve.wait_ge(rooted, (g.times(2) + (t + 1)).n)
                        dve.reciprocal(ss[:, t, 2:3], ss[:, t, 1:2]).then_inc(inv_root, 1)
                    for t in range(TT):
                        dve.wait_ge(inv_root, (g.times(2) + (t + 1)).n)
                        dve.tensor_scalar(gy[:, t, :], gy[:, t, :], ss[:, t, 2:3], None, ALU.mult).then_inc(gy_done, 1)

            def xs_group(s, prior=None, done=0):
                def after(k):
                    if k == 3:
                        split_lo(s + 12)
                        split_lo(s + 13)
                    if prior is not None:
                        chain(prior, 4 + k)
                    if k == 3:
                        split_lo(s + 14)
                        split_lo(s + 15)
                blocks(s, 2, 4, after, done)

            def z_group(s, g, before):
                if before is not None:
                    gy_low(before)
                chain(g, 0)
                chain(g, 1)
                split_lo(s + 8)
                split_lo(s + 9)
                decayed(g, 0)
                decays(g, 1)
                split_lo(s + 10)
                split_lo(s + 11)
                decayed(g, 1)
                split_lo(s + 12)
                split_lo(s + 13)

            def dt_steps(k):
                if k != 0:
                    return
                h = P // 2
                dve.scalar_tensor_tensor(dtw[:, 0, :], dtv, -1.0, dtv, ALU.mult, ALU.max).then_inc(dt_vec, 1)
                dve.memset(dtw[:, 5, :], 1.0).then_inc(dt_vec, 1)
                dve.tensor_scalar(dtw[:, 2, :], dtv, 0.0, None, ALU.max).then_inc(dt_vec, 1)
                dve.wait_ge(dt_act, 1)
                dve.tensor_scalar(dtw[:, 1, :], dtw[:, 0, :], 1.0, None, ALU.add).then_inc(dt_vec, 1)
                dve.wait_ge(dt_vec, 4)
                dve.tensor_scalar(dtw[:, 4, :], dtw[:, 1, :], -1.0, TINY, ALU.add, ALU.add).then_inc(dt_vec, 1)
                dve.wait_ge(dt_vec, 5)
                dve.reciprocal(dtw[:, 4, :], dtw[:, 4, :]).then_inc(dt_vec, 1)
                dve.wait_ge(dt_vec, 6)
                dve.wait_ge(dt_act, 3)
                dve.scalar_tensor_tensor(dtw[:, 3, :], dtw[:, 3, :], TINY, dtw[:, 4, :], ALU.add, ALU.mult).then_inc(dt_vec, 1)
                dve.wait_ge(dt_vec, 7)
                dve.tensor_tensor(dtw[:, 3, :], dtw[:, 3, :], dtw[:, 0, :], ALU.mult).then_inc(dt_vec, 1)
                dve.wait_ge(dt_vec, 8)
                dve.tensor_tensor(dtw[:, 2, :], dtw[:, 2, :], dtw[:, 3, :], ALU.add).then_inc(dt_vec, 1)
                dve.tensor_scalar(dtp[:, 3:4], dtp[:, 2:3], -1.0, None, ALU.mult).then_inc(dt_vec, 1)
                dve.wait_ge(dt_vec, 10)
                dve.tensor_scalar(dtw[:, 0, :], dtw[:, 2, :], dtp[:, 3:4], None, ALU.mult).then_inc(dt_vec, 1)
                dve.wait_ge(dt_vec, 11)
                for t in range(TT):
                    for fwd in (True, False):
                        part = slice(0, h) if fwd else slice(h, P)
                        ts = slice(t * P, (t + 1) * P)
                        one, a_, f = dtw[part, 5, ts], dtw[part, 0, ts], dtw[part, 3, ts]
                        if not fwd:
                            a_, f = a_[:, ::-1], f[:, ::-1]
                        dve.tensor_tensor_scan(f, one, a_, 0.0, ALU.mult, ALU.add).then_inc(f_ready, 1)
                dve.wait_ge(dt_act, 7)
                dve.tensor_tensor(dtw[0:h, 4, 0:P], dtw[0:h, 4, 0:P], dtw[0:h, 2, 0:P], ALU.mult).then_inc(dt_vec, 1)
                dve.tensor_tensor(dtw[h:P, 4, 0:P], dtw[h:P, 4, 0:P], dtw[h:P, 2, P:T], ALU.mult).then_inc(dt_vec, 1)

            def mean_var(i, t):
                dve.wait_ge(ln_vec[t], LN_BASE[t][i] + 4)
                dve.bn_aggr(mv[:, t, 0:2], bst[:, t].rearrange("p j n -> p (j n)")).then_inc(ln_vec[t], 1)

            def factors(i, t):
                dve.wait_ge(ln_root[t], i + 1)
                dve.reciprocal(mv[:, t, 3:4], mv[:, t, 2:3]).then_inc(ln_vec[t], 1)
                dve.wait_ge(ln_vec[t], LN_BASE[t][i] + 6)
                dve.scalar_tensor_tensor(mv[:, t, 4:5], mv[:, t, 0:1], -1.0, mv[:, t, 3:4],
                                         ALU.mult, ALU.mult).then_inc(ln_vec[t], 1)

            def gains(i, t, quarters=range(3)):
                dve.wait_ge(gb_in, 32 * (i + 1))
                for j in quarters:
                    cs = slice(j * NB, (j + 1) * NB)
                    dve.wait_ge(ln_act[t], 4 * i + j + 1)
                    dve.tensor_tensor(x[:, t, cs], x[:, t, cs], gb[:, 0, cs], ALU.mult).then_inc(ln_vec[t], 1)

            def quick_norm(i):
                def centre(j):
                    cs = slice(j * NB, (j + 1) * NB)
                    dve.scalar_tensor_tensor(x[:, 1, cs], x[:, 1, cs], mv[:, 1, 0:1], gb[:, 0, cs],
                                             ALU.subtract, ALU.mult).then_inc(ln_vec[1], 1)
                mean_var(i, 1)
                dve.wait_ge(gb_in, 32 * (i + 1))
                dve.wait_ge(ln_vec[1], LN_BASE[1][i] + 5)
                centre(0)
                dve.wait_ge(ln_root[1], i + 1)
                dve.reciprocal(mv[:, 1, 3:4], mv[:, 1, 2:3]).then_inc(ln_vec[1], 1)
                dve.wait_ge(ln_vec[1], LN_BASE[1][i] + 7)
                dve.scalar_tensor_tensor(mv[:, 1, 4:5], mv[:, 1, 0:1], -1.0, mv[:, 1, 3:4],
                                         ALU.mult, ALU.mult).then_inc(ln_vec[1], 1)
                for j in range(3):
                    cs = slice(j * NB, (j + 1) * NB)
                    if j > 0:
                        centre(j)
                        dve.wait_ge(ln_vec[1], LN_BASE[1][i] + 8 + j)
                    dve.scalar_tensor_tensor(x[:, 1, cs], x[:, 1, cs], mv[:, 1, 3:4], gb[:, 1, cs],
                                             ALU.mult, ALU.add).then_inc(x_norm[1], 1)

            def renew_x(i, s, first, adds):
                mean_var(i, 0)
                factors(i, 0)
                early = len(adds) > 2
                if early:
                    adds[0](1)
                gains(i, 0, (0, 1))
                if early:
                    adds[1](1)
                gains(i, 0, (2,))
                for add in adds[2 if early else 0:-1]:
                    add(1)
                lo_x(first, 0, 0)
                split_lo(s)
                lo_x(first, 0, 1)
                split_lo(s + 1)
                split_lo(s + 2)
                adds[-1](1)
                mean_var(i, 1)
                lo_x(first, 0, 2)
                split_lo(s + 3)
                split_lo(s + 4)
                lo_x(first, 0, 3)
                factors(i, 1)
                split_lo(s + 5)
                gains(i, 1, (0, 1))
                split_lo(s + 6)
                split_lo(s + 7)
                gains(i, 1, (2, 3))
                for j in range(4):
                    lo_x(first, 1, j)

            def lo_h(u, t):
                dve.wait_ge(h_hi[t], (u + 1).n)
                kt = CT * u.slot(2)
                part = (slice(None), slice(kt, kt + CT), slice(t * P, (t + 1) * P))
                lo_of(hT[1][part], tb[t][:].rearrange("p (k n) -> p k n", k=CT), hT[0][part], h_lo[t])

            def mlp_chunk(q, s, u, first=False, last=False):
                if first:
                    for i in range(4):
                        split_lo(s + (8 + i))
                else:
                    blocks(s, 2, 4)
                blocks(s + 8, 2, 4, lambda k: lo_h(u, k) if k < 2 else None)
                for t in range(TT):
                    for i in range(2):
                        split_lo(s + (20 + 2 * t + i))
                    lo_h(u + 1, t)
                for t in range(TT):
                    add_x(q + 2, s + 20, t, 0, first, last)
                down(q + 3, s + 20, 1, first=first, norm=last)
                if last:
                    for i in range(4):
                        split_lo(s + (28 + i))
                    adds = [lambda t, n=n: add_x(q + (2 + n), s + (20 + 4 * n), t, n, first, True) for n in (2, 3)]
                    for add in adds:
                        add(0)
                    return adds
                for n in (2, 3):
                    down(q + (2 + n), s + (16 + 4 * n), n, first=first)

            def mlp(q0, s0, layer):
                u0, last = 2 * CHUNKS * layer, CHUNKS - 1
                mlp_chunk(Pos(q0), Pos(s0), Pos(u0), first=True)
                with dve.Fori(0, CHUNKS - 2) as c:
                    mlp_chunk(Pos(q0 + 6, 6, c), Pos(s0 + 32, 32, c), Pos(u0 + 2, 2, c))
                return mlp_chunk(Pos(q0 + 6 * last), Pos(s0 + 32 * last), Pos(u0 + 2 * last), last=True)

            dve.memset(gt[:], 0.0).then_inc(gt_set, 1)
            dve.memset(eps[:], EPS).then_inc(eps_set, 1)
            for pair in range(2):
                for t in range(TT):
                    dve.sem_inc(acc_free[pair][t], 1)
            dve.sem_inc(acc_free[Q_DT % 2][1], 1)
            dve.sem_inc(acc_full[Q_DT % 2], 1)
            for i in range(4):
                lo_x(0, 0, i)
            for i in range(4):
                lo_x(0, 1, i)
            split_lo(Pos(S_DT))
            split_lo(Pos(S_DT + 1))
            for i in range(4):
                split_lo(Pos(S_BC + i))
            dve.wait_ge(const_in, 16 * 7)
            dve.wait_ge(w_used, S_BC)
            dve.tensor_scalar(dtv, acc[Q_DT % 2][0][:, 0:T], dtp[:, 0:1], None, ALU.add).then_inc(
                acc_free[Q_DT % 2][0], 1)
            set_pads()
            dve.wait_ge(pad_set, 2)
            with dve.Fori(0, 2) as j:
                for i in range(2):
                    blocks(Pos(S_BC + 8 * i, 16, j), 2, 4,
                           lambda n: convolve(Pos(i, 2, j), Pos(CH_B + CT * i, 2 * CT, j)) if n == 3 else None)
            dve.wait_ge(acc_free[Q_DT % 2][0], 2)
            blocks(Pos(S_P0), 2, 4, dt_steps)
            for i in range(4):
                split_lo(Pos(S_P0 + 12 + i))
            dve.wait_ge(col_done, 2)
            z_group(Pos(S_P0 + 8), Pos(0), None)
            xs_group(Pos(S_P1), Pos(0), done=2)
            z_group(Pos(S_P1 + 8), Pos(1), Pos(0))
            dve.wait_ge(x_scaled, 1)
            with dve.Fori(0, 3) as c:
                q, s = Pos(Q_SSD, 8, c), Pos(S_SSD, 48, c)
                gl, ge, go = Pos(1, 2, c), Pos(2, 2, c), Pos(3, 2, c)
                xs_group(s, gl, done=2)
                z_group(s + 8, ge, gl)
                for n in range(4):
                    down(q + (2 + n), s + (16 + 4 * n), n, lambda k: chain(ge, 4 + k),
                         done=2 if n == 0 else 0)
                xs_group(s + 32)
                z_group(s + 40, go, ge)
            for n in (0, 1):
                down(Pos(Q_D3 + n), Pos(S_D3 + 2 * n), n,
                     lambda k: chain(Pos(7), LAST_SSD[k]) if k in LAST_SSD else None, 2, done=2 if n == 0 else 0)
            chain(Pos(7), 6)
            down(Pos(Q_D3 + 2), Pos(S_D3 + 4), 2, none, 2)
            chain(Pos(7), 7)
            down(Pos(Q_D3 + 3), Pos(S_D3 + 6), 3, none, 2)
            gy_low(Pos(7))
            adds = [lambda t, n=n: add_x(Pos(Q_D3 + 4 + n), Pos(S_D3 + 10 + 2 * n), t, n, norm=True) for n in range(4)]
            for n in range(4):
                if n < 2:
                    split_lo(Pos(S_D3 + 12 + 2 * n))
                    split_lo(Pos(S_D3 + 13 + 2 * n))
                adds[n](0)
            renew_x(0, Pos(S_M0), 8, adds)
            adds = mlp(Q_M0, S_M0, 0)

            def lo_pool(g):
                for u in (2 * g, 2 * g + 1):
                    dve.wait_ge(tr_hi, 16 + u + 1)
                    lo_of(xT[1][:, 2 * u:2 * u + 2, :], tb[u % 2][:].rearrange("p (k n) -> p k n", k=2),
                          xT[0][:, 2 * u:2 * u + 2, :], tr_lo)

            mean_var(1, 0)
            factors(1, 0)
            gains(1, 0)
            adds[0](1)
            for i in range(2):
                split_lo(Pos(S_POOL + i))
            adds[1](1)
            quick_norm(1)

            def pooled(g, t):
                q, cs = Pos(Q_POOL + g), slice(g * NB, (g + 1) * NB)
                full(q, t, Pos(S_POOL + 2 * g + 2))
                wait(dve, pool_added, Pos(4 * t + g))
                dve.tensor_tensor(ptmp, acc[q.slot(2)][t][:], psc[:, 0, cs], ALU.mult).then_inc(
                    acc_free[q.slot(2)][t], 1)
                dve.wait_ge(pool_bias, 2 * g + t + 1)
                dve.wait_ge(acc_free[q.slot(2)][t], (q.half() + 1).n)
                dve.tensor_tensor(x[:, t, cs], x[:, t, cs], ptmp, ALU.add).then_inc(pool_added, 1)
                dve.wait_ge(pool_added, 4 * t + g + 1)
                stats(t, g)

            dve.wait_ge(psc_in, 32)
            lo_pool(0)
            for g in range(1, 4):
                split_lo(Pos(S_POOL + 2 * g))
                split_lo(Pos(S_POOL + 2 * g + 1))
                lo_pool(g)
                if g == 2:
                    pooled(0, 0)
            for g in range(1, 4):
                pooled(g, 0)
            renew_x(2, Pos(S_M1), 24, [lambda t, g=g: pooled(g, t) for g in range(4)])
            adds = mlp(Q_M1, S_M1, 1)
            mean_var(3, 0)
            factors(3, 0)
            gains(3, 0)
            for add in adds:
                add(1)
            quick_norm(3)

        @block.gpsimd
        def _(pool):
            for dst, name in ((masks, "masks"), (convw, "conv_w"), (convb, "conv_b"),
                              (normw, "norm_w")):
                pool.dma_start(dst[:], a[name]).then_inc(const_in, 16)
            pool.dma_start(dtp[:, 0:1], a["dt_bias"]).then_inc(const_in, 16)
            pool.dma_start(dtp[:, 1:2], a["a_log"]).then_inc(const_in, 16)
            pool.dma_start(dskip[:], a["d_skip"].partition_broadcast(P)).then_inc(const_in, 16)

            def load_gb(i):
                for m, name in enumerate(("ln_g", "ln_b")):
                    pool.dma_start(gb[:, m, :], a[name][i].partition_broadcast(P)).then_inc(gb_in, 16)

            def weigh(g, t):
                pool.wait_ge(xs_out, (g.times(2) + (t + 1)).n)
                wait(pool, st_done, g.times(2) + t)
                w = cols[:, 4, bass.ds(g.times(HPG).n + t * NH, HPG)].unsqueeze(2).to_broadcast([P, HPG, HD])
                pool.tensor_tensor(xw[:].rearrange("p (h c) -> p h c", h=HPG),
                                   xs[:, t, :].rearrange("p (h c) -> p h c", h=HPG), w, ALU.mult).then_inc(xw_done, 1)

            def weigh_scores(g, u):
                t, hh = u // 2, u % 2
                pool.wait_ge(gt_done, (g.times(4) + 4).n)
                wait(pool, m_done, g.times(4) + u)
                for d in range(2):
                    w = cols[:, 2 + t, bass.ds(g.times(HPG).n + d * NH + 4 * hh, 4)]
                    pool.tensor_tensor(gd[:, d], gt[:, t, d, :].unsqueeze(1).to_broadcast([P, 4, P]),
                                       w.unsqueeze(2).to_broadcast([P, 4, P]), ALU.mult).then_inc(gd_part, 1)
                pool.wait_ge(gd_part, (g.times(8) + 2 * (u + 1)).n)
                pool.tensor_tensor(gd[:, 0], gd[:, 0], gd[:, 1], ALU.add).then_inc(gd_done, 1)

            def skip(g):
                pool.wait_ge(xs_out, (g.times(2) + 2).n)
                for t in range(TT):
                    w = dskip[:, bass.ds(g.times(HPG).n, HPG)].unsqueeze(2).to_broadcast([P, HPG, HD])
                    pool.tensor_tensor(gy[:, t, :].rearrange("p (h c) -> p h c", h=HPG),
                                       xs[:, t, :].rearrange("p (h c) -> p h c", h=HPG), w, ALU.mult).then_inc(gy_skip, 1)

            def head_group(g):
                wait(pool, off_done, g.times(2))
                for m in range(2):
                    src = area_a[:, bass.ds(g.times(T).n + m * (NG * T), T)]
                    if m == 1:
                        pool.tensor_copy(cur[:, m, :], src).then_inc(cur_done, 1)
                    else:
                        pool.tensor_copy(cur[:, m, :], src).then_inc(cur_half, 1)
                wait(pool, e_sub, g.times(8) + -2)
                load_f(pool, g, 0)
                weigh_scores(g, 0)
                weigh(g, 0)
                skip(g)
                weigh_scores(g, 1)
                weigh(g, 1)
                weigh_scores(g, 2)
                weigh_scores(g, 3)

            pool.wait_ge(tr_done, 8)
            pool.tensor_scalar(x[:], x[:], ALPHA, None, ALU.mult).then_inc(x_scaled, 1)
            pool.wait_ge(f_ready, 4)
            pool.dma_start(fscr, dtw[:, 3, :]).then_inc(f_saved, 16)
            pool.wait_ge(f_saved, 16)
            pool.wait_ge(cv_silu, 4)
            pool.wait_ge(col_done, 2)
            head_group(Pos(0))
            with pool.Fori(0, NG - 1) as c:
                head_group(Pos(1, 1, c))
            pool.wait_ge(cur_done, NG)
            load_gb(0)
            pool.wait_ge(e_sub, 8 * NG)
            pool.dma_start(bands[:], a["bands"]).then_inc(bands_in, 16)
            pool.wait_ge(gy_tr, NG)
            for m, name in enumerate(("pool_scale", "pool_b")):
                pool.dma_start(psc[:, m, :], a[name].partition_broadcast(P)).then_inc(psc_in, 16)
            def offsets(i):
                for t in range(TT if i in (0, 2) else 1):
                    for j in range(4):
                        cs = slice(j * NB, (j + 1) * NB)
                        if j == 3 and t == 0:
                            pool.wait_ge(ln_act[t], 4 * (i + 1))
                            pool.tensor_tensor(x[:, t, cs], x[:, t, cs], gb[:, 0, cs], ALU.mult).then_inc(ln_vec[t], 1)
                        pool.wait_ge(ln_vec[t], LN_BASE[t][i] + 8 + j)
                        pool.tensor_tensor(x[:, t, cs], x[:, t, cs], gb[:, 1, cs], ALU.add).then_inc(x_norm[t], 1)
                if i in (1, 3):
                    cs = slice(3 * NB, DM)
                    pool.wait_ge(ln_act[1], 4 * (i + 1))
                    pool.tensor_tensor(x[:, 1, cs], x[:, 1, cs], gb[:, 0, cs], ALU.mult).then_inc(q3_gain, 1)
                    pool.wait_ge(q3_gain, (i + 1) // 2)
                    pool.tensor_tensor(x[:, 1, cs], x[:, 1, cs], gb[:, 1, cs], ALU.add).then_inc(x_norm_q3, 1)
                if i < 3:
                    for t in range(TT):
                        pool.wait_ge(x_norm[t], NORMED[t][i + 1])
                    if i == 1:
                        pool.wait_ge(x_norm_q3, 1)
                    load_gb(i + 1)

            offsets(0)
            pool.wait_ge(psc_in, 32)
            pool.tensor_tensor(psc[:, 1, :], psc[:, 1, :], psc[:, 0, :], ALU.mult).then_inc(bias_scaled, 1)
            offsets(1)
            pool.wait_ge(bias_scaled, 1)
            for g in range(4):
                for t in range(TT):
                    cs = slice(g * NB, (g + 1) * NB)
                    pool.wait_ge(tr_done, 16 + 2 * g + 2)
                    pool.tensor_scalar(x[:, t, cs], x[:, t, cs], ALPHA, None, ALU.mult).then_inc(pool_alpha, 1)
                    pool.wait_ge(pool_alpha, 2 * g + t + 1)
                    pool.tensor_tensor(x[:, t, cs], x[:, t, cs], psc[:, 1, cs], ALU.add).then_inc(pool_bias, 1)
            offsets(2)
            offsets(3)


def kernel(**inputs):
    import numpy as np
    import concourse.bacc as bacc
    from concourse.bass_utils import run_bass_kernel_spmd

    s, l = np.arange(P)[:, None], np.arange(P)[None, :]
    masks = np.stack([s <= l, s >= l], axis=1).astype(np.float32)
    bands = np.zeros((T, len(WINDOWS), T), np.float32)
    for i, w in enumerate(WINDOWS):
        for t in range(T):
            lo, hi = max(t - w // 2, 0), min(t - w // 2 + w, T)
            bands[lo:hi, i, t] = np.float32(1.0) / np.float32(hi - lo)
            bands[t, i, t] -= 1.0
    bands = bands.reshape(TT, P, len(WINDOWS), T).transpose(1, 2, 0, 3)

    def by_channel(v):
        return np.asarray(v).reshape(-1, P).T

    d = {k: np.asarray(v) for k, v in inputs.items()}
    arrays = {
        "x": d["x"][0], "in_proj": d["ssd_in_proj"][0], "out_proj": d["ssd_out_proj"][0],
        "pool_w": d["pool_w"][0], "w1": d["mlp_w1"], "w2": d["mlp_w2"],
        "conv_w": d["ssd_conv_w"][0, :, 0, :].reshape(TAPS, -1, P).transpose(2, 1, 0),
        "conv_b": by_channel(d["ssd_conv_b"][0]), "norm_w": by_channel(d["ssd_norm_w"][0]),
        "dt_bias": d["ssd_dt_bias"][0].reshape(P, 1), "a_log": d["ssd_A_log"][0].reshape(P, 1),
        "d_skip": d["ssd_D"][0], "pool_scale": d["pool_scale"][0], "pool_b": d["pool_b"][0].reshape(DM),
        "ln_g": np.stack([d["ln_mix_g"][0], d["ln_ffn_g"][0], d["ln_mix_g"][1], d["ln_ffn_g"][1]]),
        "ln_b": np.stack([d["ln_mix_b"][0], d["ln_ffn_b"][0], d["ln_mix_b"][1], d["ln_ffn_b"][1]]),
        "ident": np.eye(P, dtype=np.float32), "masks": masks, "bands": bands,
    }
    arrays = {k: np.ascontiguousarray(v) for k, v in arrays.items()}
    nc = bacc.Bacc("TRN2", target_bir_lowering=False, num_devices=1)
    aps = {k: nc.dram_tensor(f"in_{k}", v.shape, mybir.dt.from_np(v.dtype), kind="ExternalInput").ap()
           for k, v in arrays.items()}
    out = nc.dram_tensor("out", (T, DM), F32, kind="ExternalOutput").ap()
    build(nc, aps, out)
    r = run_bass_kernel_spmd(nc, [{f"in_{k}": v for k, v in arrays.items()}], core_ids=[0])
    return r.results[0]["out"].reshape(1, T, DM)
```
